# Optimizing a Trainium2 kernel written in Bass

```python
import math
import jax, jax.numpy as jnp
from jax import lax
import numpy as np

D_MODEL = 1024
BATCH = 1
SEQ = 512
DEPTH = 2
DEC_BATCH = 8
DEC_SEQ = 8
PAST_LEN = 4096
PAGE_SIZE = 128

N_META = 16
D_MIX = D_MODEL
D_A = D_MIX // 2
D_R = D_MIX - D_A
H_A = 4
DK = D_A // H_A
DV = D_A // H_A
CHUNK = 64
CONV_W = 4
NB_R = 8
BW_R = D_R // NB_R
C_RG = 8.0
D_FF = ((8 * D_MODEL // 3 + 127) // 128) * 128
D_IN = 4 * D_A + 2 * H_A + 2 * D_R
EPS = 1e-6

kernel_name = "hymba_deltanet_rglru_macaron_step"

def rmsnorm(x, w):
    xf = x.astype(jnp.float32)
    y = xf * lax.rsqrt(jnp.mean(xf * xf, axis=-1, keepdims=True) + EPS)
    return (y * w.astype(jnp.float32)).astype(x.dtype)

def l2norm(x):
    xf = x.astype(jnp.float32)
    return (xf * lax.rsqrt(jnp.sum(xf * xf, axis=-1, keepdims=True) + EPS)).astype(x.dtype)

def swiglu(h, wg, wu, wd):
    return (jax.nn.silu(h @ wg) * (h @ wu)) @ wd

def causal_conv(x, buf, w):
    t = x.shape[1]
    xp = jnp.concatenate([buf.astype(x.dtype), x], axis=1)
    y = xp[:, 0:t] * w[0]
    for j in range(1, CONV_W):
        y = y + xp[:, j:j + t] * w[j]
    return y, xp[:, -(CONV_W - 1):]

def gated_delta_chunked(q, k, v, g, beta, s0, front):
    b, t = q.shape[:2]
    back = (-(front + t)) % CHUNK
    f32 = jnp.float32

    def prep(a):
        a = a.astype(f32)
        a = jnp.pad(a, [(0, 0), (front, back)] + [(0, 0)] * (a.ndim - 2))
        n = a.shape[1] // CHUNK
        a = a.reshape((b, n, CHUNK) + a.shape[2:])
        return a.transpose((1, 0, 3, 2) + tuple(range(4, a.ndim)))

    qc, kc, vc, gc, bc = prep(q), prep(k), prep(v), prep(g), prep(beta)
    gcum = jnp.cumsum(gc, axis=-1)
    idx = jnp.arange(CHUNK)
    causal = idx[:, None] >= idx[None, :]
    strict = idx[:, None] > idx[None, :]
    decay = jnp.exp(jnp.where(causal, gcum[..., :, None] - gcum[..., None, :], -jnp.inf))
    kb = kc * bc[..., None]
    lmat = jnp.where(strict, jnp.einsum('nbhik,nbhjk->nbhij', kb, kc) * decay, 0.0)
    rhs = jnp.concatenate([vc * bc[..., None], kb * jnp.exp(gcum)[..., None]], axis=-1)
    sol = lax.linalg.triangular_solve(lmat, rhs, left_side=True, lower=True, unit_diagonal=True)
    u, w = sol[..., :DV], sol[..., DV:]
    attn = jnp.einsum('nbhik,nbhjk->nbhij', qc, kc) * decay

    def step(s, xs):
        q_c, k_c, u_c, w_c, g_c, a_c = xs
        v_new = u_c - jnp.einsum('bhck,bhkv->bhcv', w_c, s)
        o_c = (jnp.einsum('bhck,bhkv->bhcv', q_c * jnp.exp(g_c)[..., None], s)
               + jnp.einsum('bhij,bhjv->bhiv', a_c, v_new))
        g_last = g_c[..., -1]
        k_dec = k_c * jnp.exp(g_last[..., None] - g_c)[..., None]
        s = s * jnp.exp(g_last)[..., None, None] + jnp.einsum('bhck,bhcv->bhkv', k_dec, v_new)
        return s, o_c

    s_final, o = lax.scan(step, s0.astype(f32), (qc, kc, u, w, gcum, attn))
    n = o.shape[0]
    o = o.transpose(1, 0, 3, 2, 4).reshape(b, n * CHUNK, H_A, DV)[:, front:front + t]
    return o, s_final

def lru_scan(a, u, h0):
    def step(h, au):
        a_t, u_t = au
        h = a_t * h + u_t
        return h, h
    h_t, hs = lax.scan(step, h0.astype(jnp.float32), (a.swapaxes(0, 1), u.swapaxes(0, 1)))
    return hs.swapaxes(0, 1), h_t

def trunk_layer(x, s_delta, s_dconv, s_lru, s_lconv, front, p):
    bsz, t, _ = x.shape
    dt = x.dtype
    f32 = jnp.float32
    x = x + 0.5 * swiglu(rmsnorm(x, p['n1']), p['f1g'], p['f1u'], p['f1d'])
    h = rmsnorm(x, p['nm'])
    proj = h @ p['w_in']
    c1 = 3 * D_A
    c2 = c1 + D_A
    c3 = c2 + H_A
    c4 = c3 + H_A
    c5 = c4 + D_R
    qkv_raw, z, b_logit = proj[..., :c1], proj[..., c1:c2], proj[..., c2:c3]
    a_logit, xr, gate = proj[..., c3:c4], proj[..., c4:c5], proj[..., c5:]
    qkv, new_dconv = causal_conv(qkv_raw, s_dconv, p['cqkv'])
    qkv = jax.nn.silu(qkv)
    q = l2norm(qkv[..., :D_A].reshape(bsz, t, H_A, DK)) * (DK ** -0.5)
    k = l2norm(qkv[..., D_A:2 * D_A].reshape(bsz, t, H_A, DK))
    v = qkv[..., 2 * D_A:].reshape(bsz, t, H_A, DV)
    beta = jax.nn.sigmoid(b_logit.astype(f32))
    g = -jnp.exp(p['a_log'].astype(f32)) * jax.nn.softplus(a_logit.astype(f32) + p['dt_bias'].astype(f32))
    o, new_delta = gated_delta_chunked(q, k, v, g, beta, s_delta, front)
    o = rmsnorm(o.astype(dt), p['onorm']) * jax.nn.silu(z.reshape(bsz, t, H_A, DV))
    o = o.reshape(bsz, t, D_A)
    xc, new_lconv = causal_conv(xr, s_lconv, p['clw'])
    xc = xc + p['clb']
    xb = xc.reshape(bsz, t, NB_R, BW_R)
    r = jax.nn.sigmoid((jnp.einsum('btnc,ncd->btnd', xb, p['wr']).reshape(bsz, t, D_R) + p['br']).astype(f32))
    i = jax.nn.sigmoid((jnp.einsum('btnc,ncd->btnd', xb, p['wi']).reshape(bsz, t, D_R) + p['bi']).astype(f32))
    log_a = -C_RG * r * jax.nn.softplus(-p['lam'].astype(f32))
    mult = jnp.sqrt(-jnp.expm1(2.0 * log_a))
    hs, new_lru = lru_scan(jnp.exp(log_a), mult * i * xc.astype(f32), s_lru)
    y = hs.astype(dt) * jax.nn.gelu(gate, approximate=True)
    x = x + jnp.concatenate([o, y], axis=-1) @ p['w_out']
    x = x + 0.5 * swiglu(rmsnorm(x, p['n2']), p['f2g'], p['f2u'], p['f2d'])
    return x, new_delta.astype(dt), new_dconv.astype(dt), new_lru.astype(dt), new_lconv.astype(dt)

def setup_inputs(seed: int = 0) -> dict:
    key = jax.random.key(seed)
    ks = iter(jax.random.split(key, 48))
    f32 = jnp.float32

    def nrm(shape, scale):
        return jax.random.normal(next(ks), shape, f32) * scale

    def gain(shape):
        return 1.0 + nrm(shape, 0.02)

    a_log = jnp.log(jax.random.uniform(next(ks), (DEPTH, H_A), f32, 1.0, 16.0))
    dtv = jnp.exp(jax.random.uniform(next(ks), (DEPTH, H_A), f32, math.log(1e-3), math.log(1e-1)))
    dt_bias = dtv + jnp.log(-jnp.expm1(-dtv))
    a_c = jax.random.uniform(next(ks), (DEPTH, D_R), f32, 0.9, 0.999)
    a_base = a_c ** (1.0 / C_RG)
    lru_lambda = jnp.log(a_base) - jnp.log1p(-a_base)
    return {
        'x_prompt': nrm((BATCH, SEQ, D_MODEL), 1.0),
        'x_sample': nrm((DEC_BATCH, DEC_SEQ, D_MODEL), 1.0),
        'state_delta': nrm((DEPTH, DEC_BATCH, H_A, DK, DV), 0.1),
        'state_delta_conv': nrm((DEPTH, DEC_BATCH, CONV_W - 1, 3 * D_A), 1.0),
        'state_lru': nrm((DEPTH, DEC_BATCH, D_R), 0.5),
        'state_lru_conv': nrm((DEPTH, DEC_BATCH, CONV_W - 1, D_R), 1.0),
        'meta_tokens': nrm((N_META, D_MODEL), 1.0),
        'norm_ffn1': gain((DEPTH, D_MODEL)),
        'w_ffn1_gate': nrm((DEPTH, D_MODEL, D_FF), D_MODEL ** -0.5),
        'w_ffn1_up': nrm((DEPTH, D_MODEL, D_FF), D_MODEL ** -0.5),
        'w_ffn1_down': nrm((DEPTH, D_FF, D_MODEL), D_FF ** -0.5),
        'norm_mix': gain((DEPTH, D_MODEL)),
        'w_in': nrm((DEPTH, D_MODEL, D_IN), D_MODEL ** -0.5),
        'conv_qkv': nrm((DEPTH, CONV_W, 3 * D_A), CONV_W ** -0.5),
        'a_log': a_log,
        'dt_bias': dt_bias,
        'norm_delta_out': gain((DEPTH, DV)),
        'conv_lru_w': nrm((DEPTH, CONV_W, D_R), CONV_W ** -0.5),
        'conv_lru_b': nrm((DEPTH, D_R), 0.01),
        'w_rgate': nrm((DEPTH, NB_R, BW_R, BW_R), BW_R ** -0.5),
        'b_rgate': nrm((DEPTH, D_R), 0.01),
        'w_igate': nrm((DEPTH, NB_R, BW_R, BW_R), BW_R ** -0.5),
        'b_igate': nrm((DEPTH, D_R), 0.01),
        'lru_lambda': lru_lambda,
        'w_out': nrm((DEPTH, D_MIX, D_MODEL), D_MIX ** -0.5),
        'norm_ffn2': gain((DEPTH, D_MODEL)),
        'w_ffn2_gate': nrm((DEPTH, D_MODEL, D_FF), D_MODEL ** -0.5),
        'w_ffn2_up': nrm((DEPTH, D_MODEL, D_FF), D_MODEL ** -0.5),
        'w_ffn2_down': nrm((DEPTH, D_FF, D_MODEL), D_FF ** -0.5),
        'norm_final': gain((D_MODEL,)),
    }

def reference(x_prompt, x_sample, state_delta, state_delta_conv, state_lru, state_lru_conv,
              meta_tokens, norm_ffn1, w_ffn1_gate, w_ffn1_up, w_ffn1_down, norm_mix, w_in,
              conv_qkv, a_log, dt_bias, norm_delta_out, conv_lru_w, conv_lru_b, w_rgate, b_rgate,
              w_igate, b_igate, lru_lambda, w_out, norm_ffn2, w_ffn2_gate, w_ffn2_up, w_ffn2_down,
              norm_final):
    layers = [dict(n1=norm_ffn1[l], f1g=w_ffn1_gate[l], f1u=w_ffn1_up[l], f1d=w_ffn1_down[l],
                   nm=norm_mix[l], w_in=w_in[l], cqkv=conv_qkv[l], a_log=a_log[l],
                   dt_bias=dt_bias[l], onorm=norm_delta_out[l], clw=conv_lru_w[l],
                   clb=conv_lru_b[l], wr=w_rgate[l], br=b_rgate[l], wi=w_igate[l], bi=b_igate[l],
                   lam=lru_lambda[l], w_out=w_out[l], n2=norm_ffn2[l], f2g=w_ffn2_gate[l],
                   f2u=w_ffn2_up[l], f2d=w_ffn2_down[l]) for l in range(DEPTH)]

    def run(x, sd, sdc, sl, slc, front):
        nd, ndc, nl, nlc = [], [], [], []
        for l in range(DEPTH):
            x, a, b, c, d = trunk_layer(x, sd[l], sdc[l], sl[l], slc[l], front, layers[l])
            nd.append(a)
            ndc.append(b)
            nl.append(c)
            nlc.append(d)
        return rmsnorm(x, norm_final), jnp.stack(nd), jnp.stack(ndc), jnp.stack(nl), jnp.stack(nlc)

    bp = x_prompt.shape[0]
    dtp = x_prompt.dtype
    meta = jnp.broadcast_to(meta_tokens.astype(dtp)[None], (bp, N_META, D_MODEL))
    xp = jnp.concatenate([meta, x_prompt], axis=1)
    zd = jnp.zeros((DEPTH, bp, H_A, DK, DV), dtp)
    zdc = jnp.zeros((DEPTH, bp, CONV_W - 1, 3 * D_A), dtp)
    zl = jnp.zeros((DEPTH, bp, D_R), dtp)
    zlc = jnp.zeros((DEPTH, bp, CONV_W - 1, D_R), dtp)
    yp, nd_p, ndc_p, nl_p, nlc_p = run(xp, zd, zdc, zl, zlc, (-N_META) % CHUNK)
    y_prompt = yp[:, N_META:]
    y_sample, nd_s, ndc_s, nl_s, nlc_s = run(x_sample, state_delta, state_delta_conv,
                                             state_lru, state_lru_conv, 0)
    return (y_prompt, y_sample, nd_p, ndc_p, nl_p, nlc_p, nd_s, ndc_s, nl_s, nlc_s)


_drawn_inputs = setup_inputs


def setup_inputs(seed=0):
    import zlib

    import numpy as np

    out = dict(_drawn_inputs(seed))
    spreads = {}
    factors = {'norm_ffn1': 3.668,
     'norm_delta_out': 20.856,
     'b_rgate': 24.457,
     'b_igate': 8.0,
     'norm_ffn2': 5.239,
     'norm_final': 8.561}
    for name, (base, spread) in spreads.items():
        noise = np.random.default_rng([zlib.crc32(name.encode()), seed]).standard_normal(out[name].shape)
        drawn = base * np.exp(spread * noise) if base else spread * noise
        out[name] = __import__('jax').numpy.asarray(drawn.astype(out[name].dtype))
    for name, factor in factors.items():
        out[name] = (out[name] * factor).astype(out[name].dtype)
    return out
```

```python
from contextlib import ExitStack

import numpy as np
import concourse.bass as bass
from concourse import mybir

F32 = mybir.dt.float32
F32R = mybir.dt.float32r
ACT = mybir.ActivationFunctionType
ALU = mybir.AluOpType

P = 128
DEPTH, D, SEQ, N_META = 2, 1024, 512, 16
SEQS, SLEN = 8, 8
TP = N_META + SEQ
TS = SEQS * SLEN
T = TP + TS
HALF = T // 2
KT = D // P
FT = 22
FA, FB = 12, 10
H, DK, DR = 4, 128, 512
TAPS = 4
PAD = TAPS - 1 + TP + SEQS * (TAPS - 1 + SLEN)
CONV = PAD - (TAPS - 1)
SAMP0 = TAPS - 1 + TP
STRIDE = TAPS - 1 + SLEN
NCH = 5
CH = [128, 128, 128, 128, 80]
SEGS = 9
LEVELS = [[2, 4, 8, 16, 32, 64]] * 4 + [[2, 4, 8]]
EPS = 1e-6

V_NM, V_N2, V_NN, V_CQ, V_CL, V_CB, V_BR, V_BI, V_LAM, V_ALOG, V_DT, V_ON = (
    0, 8, 16, 24, 72, 88, 92, 96, 100, 104, 108, 112)
NV = 113
M_TRI, M_TRIS, M_GT, M_GTS, M_L1T, M_L2, M_L4, M_L8, M_L16, M_L32, M_L64, M_ID, M_ONE = range(13)
N_MASKS, IND = 13, slice(96, 105)
LEVEL_MASK = {2: M_L2, 4: M_L4, 8: M_L8, 16: M_L16, 32: M_L32, 64: M_L64}

U_FFN = 2 * FT + 16
U_MIX = 24
U_OUT = 8
U_LAYER = 2 * U_FFN + U_MIX + U_OUT
B_FFN = (0, U_FFN + U_MIX + U_OUT)
B_MIX = U_FFN
B_OUT = U_FFN + U_MIX
AB_LAYER, AB_FFN, AB_MIX, AB_OUT = 54, (0, 35), 19, 31
CD_LAYER, CD_FFN = 22, (0, 11)
NORMS = 3
SMALL = 5
LRU_A, LRU_D = 5, 11
T_ABS, T_G, T_SS, TOK_D = 4, 21, 22, 26
ATANH = [1.0 / (2 * i + 1) for i in range(8, 0, -1)]


def chunk_masks():
    m = np.zeros((N_MASKS, P, P), np.float32)
    r = np.arange(P)
    row, col = r[:, None], r[None, :]
    seg = np.where(r < 16, 0, 1 + (r - 16) // SLEN)
    same = seg[:, None] == seg[None, :]
    m[M_TRI] = row <= col
    m[M_TRIS] = (row <= col) & same
    m[M_GT] = row > col
    m[M_GTS] = (row > col) & same
    for s, at in LEVEL_MASK.items():
        m[at] = (row // (2 * s) == col // (2 * s)) & (row % (2 * s) >= s) & (col % (2 * s) < s)
    m[M_L1T] = (row // 2 == col // 2) & (col % 2 == 1) & (row % 2 == 0)
    m[M_ID] = row == col
    m[M_ONE] = 1.0
    m[M_GTS, :, IND] = seg[:, None] == np.arange(SEGS)[None, :]
    return np.ascontiguousarray(m.transpose(1, 0, 2))


def build(nc, I, O):
    ctx = ExitStack()

    def sb(name, shape, dt=F32, stack=ctx):
        return stack.enter_context(nc.sbuf_tensor(name, shape, dt))

    def sem(name):
        return ctx.enter_context(nc.semaphore(name))

    with ctx:
        x = sb("x", [P, KT, T])
        h_hi, h_lo = sb("h_hi", [P, KT, T], F32R), sb("h_lo", [P, KT, T], F32R)
        w_raw = sb("w_raw", [P, 2, FA * P])
        w_hi, w_lo = sb("w_hi", [P, 2, FA * P], F32R), sb("w_lo", [P, 2, FA * P], F32R)
        rms, rstd = sb("rms", [P, T]), sb("rstd", [P, T])
        gain0 = sb("gain0", [P, KT])
        vec = sb("vec", [P, NV])
        w_ba = sb("w_ba", [P, KT * 8])
        w_ba_hi, w_ba_lo = sb("w_ba_hi", [P, KT * 8], F32R), sb("w_ba_lo", [P, KT * 8], F32R)
        w_ri = sb("w_ri", [P, 4, 2, P])
        conv_hist = sb("conv_hist", [P, 16, SEQS, TAPS - 1])
        lru_h0 = sb("lru_h0", [P, 4, SEQS])
        conv_new = sb("conv_new", [P, 16, 27])
        lru_new = sb("lru_new", [P, 4, 9])
        mask = sb("mask", [P, N_MASKS, P])
        ones_r = sb("ones_r", [P, P], F32R)
        tok = {n: sb("tok_" + n, [P, NCH, H]) for n in
               ("beta", "g", "nk", "nb", "bk2", "rq", "rq2", "nq", "rk")}
        logit = sb("logit", [P, NCH, 8])
        rstd_t = sb("rstd_t", [P, NCH])
        kq_ss = sb("kq_ss", [P, NCH, 8])
        sp = {n: sb("sp_" + n, [P, 24]) for n in ("y", "abs", "e", "z", "z2", "p", "out")}
        ea = sb("ea", [P, H])
        lam8 = sb("lam8", [P, 8])
        h_start = sb("h_start", [P, SEQS])
        e_g, e_g4 = sb("e_g", [P, 32]), sb("e_g4", [P, 8])
        g_seg = sb("g_seg", [P, SEGS, H])
        e_last = sb("e_last", [P, 16 + SEGS * H])
        o_ss, o_ms, o_rms, o_rec, o_fac = (sb(n, [P, H]) for n in ("o_ss", "o_ms", "o_rms", "o_rec", "o_fac"))

        eps = sb("eps", [P, 2])
        with ExitStack() as st:
            mid_hi, mid_lo = (sb(n, [P, FA, T], F32R, st) for n in ("mid_hi", "mid_lo"))
            gate_s, silu_s, prod = (sb(n, [P, 2, T], F32, st) for n in ("gate_s", "silu_s", "prod"))
            up_s = sb("up_s", [P, T], F32, st)
            sq = sb("sq", [P, 2, T], F32, st)
            sq_hi, sq_lo = sb("sq_hi", [P, 2, T], F32R, st), sb("sq_lo", [P, 2, T], F32R, st)
        with ExitStack() as st:
            cp = sb("cp", [P, 2, PAD], F32, st)
            acc = sb("acc", [P, PAD], F32, st)
            em, attn, nt, z_m, y_m = (sb(n, [P, H, P], F32, st) for n in ("em", "attn", "nt", "z_m", "y_m"))
            sb("gap0", [P, KT * T - 3 * PAD - 5 * H * P], F32, st)
            lt = sb("lt", [P, 4, T], F32, st)
            p_m, kdec, vn_s, qs = (sb(n, [P, H, P], F32, st) for n in ("p_m", "kdec", "vn_s", "qs"))
            z_s = sb("z_s", [P, 4, T], F32, st)
            sb("gap1", [P, 4 * T - 4 * H * P], F32, st)
            s0a = sb("s0a", [P, 2, SEQS, P], F32, st)
            s_p = sb("s_p", [P, H, P], F32, st)
            kqv = sb("kqv", [P, 12, T], F32, st)
            y_s = sb("y_s", [P, 4, T], F32, st)
        s0b = lt[:, :, :].rearrange("p a t -> p (a t)")[:, 0:2048].rearrange("p (h s d) -> p h s d", h=2, s=SEQS)
        vseg = cp[:, :, :].rearrange("p a t -> p (a t)")[:, 0:SEGS * P].rearrange("p (s d) -> p s d", s=SEGS)
        ks_t = acc[:, 0:320].rearrange("p (b k t) -> p b k t", b=2, k=2)

        pair = [ctx.enter_context(nc.psum_tensor(f"pair{n}", [P, 2, 512], F32)) for n in "ABCD"]
        PC0, PC1, PD0, PD1 = (pair[2][:, 0, :], pair[2][:, 1, :], pair[3][:, 0, :], pair[3][:, 1, :])

        w_loaded = [sem("w_loaded0"), sem("w_loaded1")]
        w_hi_done, w_lo_done, unit_done = (sem(n) for n in (
            "w_hi_done", "w_lo_done", "unit_done"))
        silu_done, prod_done, mid_hi_done, mid_done = (sem(n) for n in (
            "silu_done", "prod_done", "mid_hi_done", "mid_done"))
        h_hi_done, h_done, sq_hi_done, sq_done, ss_used = (sem(n) for n in (
            "h_hi_done", "h_done", "sq_hi_done", "sq_done", "ss_used"))
        rms_done, rstd_done, init_done = (sem(n) for n in (
            "rms_done", "rstd_done", "init_done"))
        x_loaded, gain_loaded, mask_loaded, small_loaded, s0a_loaded, s0b_loaded = (sem(n) for n in (
            "x_loaded", "gain_loaded", "mask_loaded", "small_loaded", "s0a_loaded", "s0b_loaded"))
        states_out, y_out, y_stored = (sem(n) for n in (
            "states_out", "y_out", "y_stored"))
        pad_done, conv_step, conv_done, kqv_done = (sem(n) for n in (
            "pad_done", "conv_step", "conv_done", "kqv_done"))
        wba_hi_done, wba_done, logit_done, kq_sq_done, kq_sum_done = (sem(n) for n in (
            "wba_hi_done", "wba_done", "logit_done", "kq_sq_done", "kq_sum_done"))
        tok_d, tok_a, gsum_done, gexp_done = (sem(n) for n in (
            "tok_d", "tok_a", "gsum_done", "gexp_done"))
        gelu_done, ri_done, lru_a, lru_d, silu_z_done = (sem(n) for n in (
            "gelu_done", "ri_done", "lru_a", "lru_d", "silu_z_done"))
        grhs_done, dt_done, em_done, emm_done, kq_done = (sem(n) for n in (
            "grhs_done", "dt_done", "em_done", "emm_done", "kq_done"))
        kt_done, vt_done, kdec_done, vscaled_done, nt_done, attn_done = (sem(n) for n in (
            "kt_done", "vt_done", "kdec_done", "vscaled_done", "nt_done", "attn_done"))
        y0_tmp, y0_done, z0_done, z_init, nz_done, p_done, zp_done, py_done, z_upd, y_upd = (sem(n) for n in (
            "y0_tmp", "y0_done", "z0_done", "z_init", "nz_done", "p_done", "zp_done", "py_done", "z_upd", "y_upd"))
        ks_done, qs_done, qs_scaled, r_done, zr_done, vnew_done, av_done, kv_done, s_done = (sem(n) for n in (
            "ks_done", "qs_done", "qs_scaled", "r_done", "zr_done", "vnew_done", "av_done", "kv_done", "s_done"))
        o_done, o_sq_done, o_step, o_rms_done, on_done, ot_done, og_done = (sem(n) for n in (
            "o_done", "o_sq_done", "o_step", "o_rms_done", "on_done", "ot_done", "og_done"))
        seg_done, kst_done, kstt_done, vseg_done, segkv_done, seg_s_done = (sem(n) for n in (
            "seg_done", "kst_done", "kstt_done", "vseg_done", "segkv_done", "seg_s_done"))
        oy_hi_done, oy_done = (sem(n) for n in (
            "oy_hi_done", "oy_done"))
        taken = [sem("taken" + n) for n in "ABCD"]
        block = ctx.enter_context(nc.Block())

        def lv(c, k):
            return sum(len(LEVELS[i]) for i in range(c)) + k
        LV = lv(NCH, 0)
        LZ = LV - NCH

        def bc(ap, n):
            return ap.unsqueeze(2).to_broadcast([ap.shape[0], ap.shape[1], n])

        def bh(ap, n):
            return ap.unsqueeze(1).to_broadcast([ap.shape[0], n, ap.shape[1]])

        def cols(pr):
            return pair[pr][:, :, 0:HALF]

        def tiles(ap):
            return ap.rearrange("p (a t) -> p a t", a=2)

        def seq(ap, n=SEQS):
            return ap.rearrange("p (b t) -> p b t", b=n)

        def samples(buf, first, n):
            return seq(buf[:, SAMP0:PAD])[:, :, first:first + n]

        def xc(c):
            return s0a[:, :, :, :].rearrange("p h s d -> p (h s d)")[:, (c % 2) * T:(c % 2 + 1) * T]

        def head(t, n, m):
            return t[0:n, :, 0:m]

        def bank(b, n, m):
            return b[0:n, 0:H * m].rearrange("p (h m) -> p h m", h=H)

        def segbank(h):
            return PD1 if h % 2 else PC1

        def tok_eg(c, h, n):
            return e_g[0:n, c * H + h:c * H + h + 1] if c < 4 else e_g4[0:n, h:h + 1]

        def tok_kd(c, n):
            return e_g[0:n, 16 + c * H:16 + c * H + H] if c < 4 else e_g4[0:n, H:2 * H]


        @block.sync
        def _(eng):
            for k in range(KT):
                eng.dma_start(x[:, k, :], I["xT"][k]).then_inc(x_loaded, 16)
            eng.sem_inc(w_lo_done, 2)

            def load(u, pairs, src, at, n):
                with eng.Fori(0, pairs) as it:
                    for s in range(2):
                        eng.wait_ge(w_lo_done, u + it * 2 + (s + 1))
                        eng.dma_start(w_raw[:, s, 0:n], src[at + it * 2 + s]).then_inc(w_loaded[s], 16)

            def ffn(l, f):
                u = l * U_LAYER + B_FFN[f]
                load(u, FA, I["wgu"], l * (4 * FT) + f * 2 * FT, KT * P)
                load(u + 2 * FA, KT // 2, I["wda"], l * (2 * KT) + f * KT, FA * P)
                load(u + (2 * FA + KT), FB, I["wgu"], l * (4 * FT) + (f * 2 * FT + 2 * FA), KT * P)
                load(u + (2 * FT + KT), KT // 2, I["wdb"], l * (2 * KT) + f * KT, FB * P)

            with eng.Fori(0, DEPTH) as l:
                ffn(l, 0)
                load(l * U_LAYER + B_MIX, U_MIX // 2, I["win"], l * U_MIX, KT * P)
                load(l * U_LAYER + B_OUT, U_OUT // 2, I["wout"], l * U_OUT, KT * P)
                ffn(l, 1)
            for k in range(KT):
                eng.wait_ge(y_out, k + 1)
                eng.dma_start(O["y"][k], x[:, k, :]).then_inc(y_stored, 16)
            eng.wait_ge(y_stored, 16 * KT)
            eng.wait_ge(states_out, DEPTH * 16 * 5)

        @block.gpsimd
        def _(eng):
            eng.dma_start(gain0[:, :], I["gain0"]).then_inc(gain_loaded, 16)
            eng.dma_start(mask[:, :, :], I["mask"]).then_inc(mask_loaded, 16)
            with eng.Fori(0, DEPTH) as l:
                eng.wait_ge(rstd_done, l * NORMS + 1)
                for dst, name in ((vec[:, :], "vec"), (w_ba[:, :], "wba"), (w_ri[:, :, :, :], "wri"),
                                  (conv_hist[:, :, :, :], "chist"), (lru_h0[:, :, :], "lru0")):
                    eng.dma_start(dst, I[name][l]).then_inc(small_loaded, 16)
                eng.wait_ge(lru_d, l * (4 * LRU_D) + 4 * LRU_D + 1)
                eng.dma_start(s0a[:, :, :, :], I["s0"][l * 2]).then_inc(s0a_loaded, 16)
                eng.dma_start(s0b, I["s0"][l * 2 + 1]).then_inc(s0b_loaded, 16)
                eng.dma_start(O["conv"][l], conv_new[:, :, :]).then_inc(states_out, 16)
                eng.dma_start(O["lru"][l], lru_new[:, :, :]).then_inc(states_out, 16)
                eng.wait_ge(seg_s_done, l * H + H)
                eng.dma_start(O["dp"][l], s_p[:, :, :]).then_inc(states_out, 16)
                eng.dma_start(O["ds"][l * 2], s0a[:, :, :, :]).then_inc(states_out, 16)
                eng.dma_start(O["ds"][l * 2 + 1], s0b).then_inc(states_out, 16)

        @block.scalar
        def _(eng):
            eng.sem_inc(unit_done, 2)
            eng.sem_inc(ss_used, 2)
            eng.sem_inc(kqv_done, 1)

            def split(u, s, n):
                eng.wait_ge(w_loaded[s], u * 8 + (16 - 8 * s))
                eng.wait_ge(unit_done, u + 1)
                eng.activation(w_hi[:, s, 0:n], w_raw[:, s, 0:n], ACT.Copy).then_inc(w_hi_done, 1)

            def new_x(m, s, gain, nsq):
                eng.wait_ge(ss_used, nsq + 1)
                eng.activation(sq[:, s, :], x[:, m, :], ACT.Square)
                eng.activation(sq_hi[:, s, :], x[:, m, :], ACT.Square).then_inc(sq_hi_done, 1)
                eng.activation(h_hi[:, m, :], x[:, m, :], ACT.Copy, scale=gain).then_inc(h_hi_done, 1)

            def root(norm):
                eng.wait_ge(ss_used, norm * KT + (KT + 2))
                eng.activation(tiles(rms[:, :]), cols(3), ACT.Sqrt, bias=eps[:, 0:1], scale=1.0 / D).then_inc(rms_done, 1)

            def gate_up(u, ab, tg, n, prev):
                def gate(use, s):
                    eng.wait_ge(taken[s], use + 2)
                    eng.activation(silu_s[:, s, :], gate_s[:, s, :], ACT.Silu).then_inc(silu_done, 1)

                def up(t, k, s):
                    eng.wait_ge(prod_done, t + 1)
                    eng.activation(mid_hi[:, k, :], prod[:, s, :], ACT.Copy).then_inc(mid_hi_done, 1)

                def turn(it, first):
                    v = u + it * 4
                    split(v, 0, KT * P)
                    prev(0) if first else gate(ab + it - 1, 1)
                    split(v + 1, 1, KT * P)
                    prev(1) if first else up(tg + it * 2 - 1, it * 2 - 1, 1)
                    split(v + 2, 0, KT * P)
                    gate(ab + it, 0)
                    split(v + 3, 1, KT * P)
                    up(tg + it * 2, it * 2, 0)
                turn(0, True)
                with eng.Fori(1, n // 2) as it:
                    turn(it, False)
                return lambda i: up(tg + (n - 1), n - 1, 1) if i else gate(ab + (n // 2 - 1), 1)

            def to_x(u, ab, n, norm, gain_col, prev):
                def evac(it, s):
                    if norm is not None:
                        m = it * 2 + s
                        eng.wait_ge(taken[s], ab + it + 2)
                        new_x(m, s, vec[:, bass.ds(gain_col + m, 1)], norm * KT + m)

                def turn(it, first):
                    for s in range(2):
                        split(u + it * 2 + s, s, n)
                        prev(s) if first else evac(it - 1, s)
                turn(0, True)
                with eng.Fori(1, KT // 2) as it:
                    turn(it, False)
                return lambda s: evac(KT // 2 - 1, s)

            def ffn(l, f, prev):
                u, ab, tg = l * U_LAYER + B_FFN[f], l * AB_LAYER + AB_FFN[f], l * (2 * FT) + f * FT
                t = gate_up(u, ab, tg, FA, prev)
                t = to_x(u + 2 * FA, ab + FA // 2, FA * P, None, 0, t)
                t = gate_up(u + (2 * FA + KT), ab + (FA // 2 + 4), tg + FA, FB, t)
                eng.wait_ge(small_loaded, l * (16 * SMALL) + 16 * SMALL)
                return to_x(u + (2 * FT + KT), ab + (FT // 2 + 4), FB * P, l * NORMS + (1 + 2 * f), (V_NM, V_NN)[f], t)

            def mix(l, prev):
                u, ab = l * U_LAYER + B_MIX, l * AB_LAYER + AB_MIX
                la, ld = l * (4 * LRU_A), l * (4 * LRU_D)

                def evac_kqv(j):
                    eng.wait_ge(conv_done, l * 16 + j + 1)
                    eng.activation(kqv[:, j, 0:TP], acc[:, 0:TP], ACT.Silu)
                    eng.activation(seq(kqv[:, j, TP:T]),
                                   samples(acc, 0, SLEN), ACT.Silu).then_inc(kqv_done, 1)

                def evac_gate(c):
                    eng.wait_ge(taken[1], ab + (6 + c + 1) + 1)
                    eng.activation(y_s[:, c, :], y_s[:, c, :], ACT.Gelu_apprx_tanh).then_inc(gelu_done, 1)

                def evac_z(c):
                    eng.wait_ge(taken[c % 2], ab + (10 + c // 2 + 1) + 1)
                    eng.activation(z_s[:, c, :], z_s[:, c, :], ACT.Silu).then_inc(silu_z_done, 1)

                def w_ba_high():
                    eng.activation(w_ba_hi[:, :], w_ba[:, :], ACT.Copy).then_inc(wba_hi_done, 1)

                def squares():
                    eng.wait_ge(kqv_done, l * 12 + 13)
                    for j in range(8):
                        eng.activation((z_s if j < 4 else y_s)[:, j % 4, :], kqv[:, 4 + j, :], ACT.Square).then_inc(kq_sq_done, 1)

                def tok1():
                    n = l * TOK_D
                    eng.wait_ge(tok_d, n + T_ABS)
                    eng.activation(sp["e"][:, :], sp["abs"][:, :], ACT.Exp, scale=-1.0)
                    eng.activation(ea[:, :], vec[:, V_ALOG:V_ALOG + H], ACT.Exp)
                    eng.activation(tok["beta"][:, :, :], logit[:, :, 0:4], ACT.Sigmoid).then_inc(tok_a, 1)

                def tok2():
                    eng.wait_ge(gsum_done, l + 1)
                    eng.activation(e_g[:, :], PD0[:, 0:32], ACT.Exp)
                    eng.activation(e_g4[0:CH[4], :], PD0[0:CH[4], 32:40], ACT.Exp)
                    eng.activation(e_last[:, :], PD0[:, 40:40 + 16 + SEGS * H], ACT.Exp).then_inc(gexp_done, 1)
                    eng.wait_ge(tok_d, l * TOK_D + T_SS)
                    eng.activation(tok["nk"][:, :, :], kq_ss[:, :, 0:4], ACT.Sqrt, bias=eps[:, 0:1])
                    eng.activation(tok["nq"][:, :, :], kq_ss[:, :, 4:8], ACT.Sqrt, bias=eps[:, 1:2], scale=float(DK)).then_inc(tok_a, 1)

                def lru_1(c):
                    eng.wait_ge(ri_done, l * 4 + (c + 1))
                    eng.wait_ge(lru_d, ld + c * LRU_D + 1)
                    eng.activation(tiles(lt[:, 1, :]), cols(2), ACT.Sigmoid, bias=vec[:, V_BR + c:V_BR + c + 1]).then_inc(lru_a, 1)
                    eng.activation(tiles(lt[:, 2, :]), cols(3), ACT.Sigmoid, bias=vec[:, V_BI + c:V_BI + c + 1]).then_inc(lru_a, 1)
                    eng.wait_ge(lru_a, la + (c * LRU_A + 1))
                    eng.activation(lt[:, 3, :], lt[:, 1, :], ACT.Tanh, scale=lam8[:, c:c + 1]).then_inc(lru_a, 1)
                    eng.activation(lt[:, 1, :], lt[:, 1, :], ACT.Exp, scale=lam8[:, 4 + c:5 + c]).then_inc(lru_a, 1)

                def lru_2(c):
                    eng.wait_ge(lru_d, ld + (c * LRU_D + 3) + 1)
                    eng.activation(lt[:, 0, :], lt[:, 3, :], ACT.Sqrt).then_inc(lru_a, 1)

                def turn(it, first):
                    for s in range(2):
                        split(u + it * 2 + s, s, KT * P)
                        prev(s) if first else evac_kqv(it * 2 - 2 + s)
                turn(0, True)
                root(l * NORMS + 1)
                w_ba_high()
                with eng.Fori(1, 6) as it:
                    turn(it, False)
                for n in range(12, U_MIX):
                    split(u + n, n % 2, KT * P)
                    if n < 14:
                        evac_kqv(n - 2)
                    elif n < 22:
                        if n % 2:
                            evac_gate((n - 14) // 2)
                    else:
                        evac_z(n - 22)
                    if n == 13:
                        tok1()
                        squares()
                    if n == 15:
                        tok2()
                    if n >= 16:
                        (lru_2 if n % 2 else lru_1)((n - 16) // 2)
                evac_z(2)
                evac_z(3)
                for c in range(NCH):
                    delta(l, c)
                eng.wait_ge(og_done, l * NCH + NCH)
                for j in range(KT):
                    eng.activation(mid_hi[:, j, :], kqv[:, 8 + j, :] if j < 4 else y_s[:, j - 4, :], ACT.Copy).then_inc(oy_hi_done, 1)

            def delta(l, c):
                n, lc = CH[c], l * NCH + c
                lz, ll = l * LV, lv(c, 0)
                bq, bk = (PD1, PC1) if c < 4 else (PD0, PC0)
                eng.wait_ge(dt_done, lc + 1)
                eng.activation(head(em, n, n), bank(PD0, n, n), ACT.Exp).then_inc(em_done, 1)
                eng.wait_ge(z0_done, lc + 1)
                eng.activation(head(z_m, n, n), bank(PC0, n, n), ACT.Copy).then_inc(z_init, 1)
                if c == 4:
                    for h in range(H):
                        eng.wait_ge(seg_done, l * H + (h + 1))
                        if h >= 2:
                            eng.wait_ge(kstt_done, l * H + (h - 1))
                        eng.activation(ks_t[:, h % 2, :, 0:n], segbank(h)[:, 0:2 * n].rearrange("p (k t) -> p k t", k=2), ACT.Copy).then_inc(kst_done, 1)
                eng.wait_ge(qs_done, l * 4 + (c + 1)) if c < 4 else eng.wait_ge(kstt_done, l * H + H)
                for h in range(H):
                    ins = eng.activation(qs[0:n, h, :], bq[0:n, h * P:(h + 1) * P], ACT.Copy, scale=tok_eg(c, h, n))
                ins.then_inc(qs_scaled, 1)
                eng.wait_ge(o_done, lc + 1)
                for h in range(H):
                    ins = eng.activation(qs[0:n, h, :], p_m[0:n, h, :], ACT.Square, accum_out=o_ss[0:n, h:h + 1])
                ins.then_inc(o_sq_done, 1)
                eng.wait_ge(o_step, l * (3 * NCH) + (3 * c + 1))
                eng.activation(o_rms[0:n, :], o_ms[0:n, :], ACT.Sqrt, bias=eps[0:n, 0:1]).then_inc(o_rms_done, 1)

            eng.wait_ge(gain_loaded, 16)
            eng.wait_ge(x_loaded, 16 * KT)
            eng.wait_ge(init_done, 1)
            for k in range(KT):
                new_x(k, k % 2, gain0[:, k:k + 1], k)
            root(0)
            with eng.Fori(0, DEPTH) as l:
                t = ffn(l, 0, lambda s: None)
                mix(l, t)
                t = to_x(l * U_LAYER + B_OUT, l * AB_LAYER + AB_OUT, KT * P, l * NORMS + 2, V_N2, lambda s: None)
                t(0)
                t(1)
                root(l * NORMS + 2)
                eng.wait_ge(states_out, l * (16 * 5) + 16 * 5)
                t = ffn(l, 1, lambda s: None)
                t(0)
                t(1)
                root(l * NORMS + 3)

        @block.vector
        def _(eng):
            def split(u, s, n):
                eng.wait_ge(w_hi_done, u + 1)
                eng.tensor_tensor(w_lo[:, s, 0:n], w_raw[:, s, 0:n], w_hi[:, s, 0:n].bitcast(F32), ALU.subtract).then_inc(w_lo_done, 1)

            def h_low(m, gain, nh):
                eng.wait_ge(h_hi_done, nh + 1)
                eng.scalar_tensor_tensor(h_lo[:, m, :], x[:, m, :], gain, h_hi[:, m, :].bitcast(F32), ALU.mult, ALU.subtract).then_inc(h_done, 1)

            def new_x(m, s, gain, nsq):
                eng.wait_ge(sq_hi_done, nsq + 1)
                eng.tensor_tensor(sq_lo[:, s, :], sq[:, s, :], sq_hi[:, s, :].bitcast(F32), ALU.subtract).then_inc(sq_done, 1)
                h_low(m, gain, nsq)

            def root(norm):
                eng.wait_ge(rms_done, norm + 1)
                eng.reciprocal(rstd[:, :], rms[:, :]).then_inc(rstd_done, 1)
                eng.wait_ge(rstd_done, norm + 1)

            def gate_up(u, ab, cd, tg, n, prev):
                def gate(v, s):
                    eng.wait_ge(unit_done, v + 3)
                    eng.tensor_tensor(tiles(gate_s[:, s, :]), cols(s), tiles(rstd[:, :]), ALU.mult).then_inc(taken[s], 1)

                def up(v, use, t, k, s):
                    eng.wait_ge(unit_done, v + 3)
                    eng.tensor_tensor(tiles(up_s[:, :]), cols(2 + s), tiles(rstd[:, :]), ALU.mult).then_inc(taken[2 + s], 1)
                    eng.wait_ge(taken[2 + s], use + 2)
                    eng.wait_ge(silu_done, t + 1)
                    eng.tensor_tensor(prod[:, s, :], silu_s[:, s, :], up_s[:, :], ALU.mult).then_inc(prod_done, 1)
                    eng.wait_ge(mid_hi_done, t + 1)
                    eng.tensor_tensor(mid_lo[:, k, :], prod[:, s, :], mid_hi[:, k, :].bitcast(F32), ALU.subtract).then_inc(mid_done, 1)

                def turn(it, first):
                    v = u + it * 4
                    split(v, 0, KT * P)
                    prev(0) if first else gate(v - 2, 1)
                    split(v + 1, 1, KT * P)
                    prev(1) if first else up(v - 1, cd + it - 1, tg + it * 2 - 1, it * 2 - 1, 1)
                    split(v + 2, 0, KT * P)
                    gate(v, 0)
                    split(v + 3, 1, KT * P)
                    up(v + 1, cd + it, tg + it * 2, it * 2, 0)
                turn(0, True)
                with eng.Fori(1, n // 2) as it:
                    turn(it, False)
                return lambda i: up(u + (2 * n - 1), cd + (n // 2 - 1), tg + (n - 1), n - 1, 1) if i else gate(u + (2 * n - 2), 1)

            def to_x(u, ab, n, weight, norm, gain_col, prev):
                def evac(it, s):
                    m = it * 2 + s
                    eng.wait_ge(unit_done, u + m + 3)
                    eng.scalar_tensor_tensor(tiles(x[:, m, :]), cols(s), weight, tiles(x[:, m, :]), ALU.mult, ALU.add).then_inc(taken[s], 1)
                    if norm is not None:
                        eng.wait_ge(taken[s], ab + it + 2)
                        new_x(m, s, vec[:, bass.ds(gain_col + m, 1)], norm * KT + m)

                def turn(it, first):
                    for s in range(2):
                        split(u + it * 2 + s, s, n)
                        prev(s) if first else evac(it - 1, s)
                turn(0, True)
                with eng.Fori(1, KT // 2) as it:
                    turn(it, False)
                return lambda s: evac(KT // 2 - 1, s)

            def ffn(l, f, prev):
                u, ab, cd, tg = l * U_LAYER + B_FFN[f], l * AB_LAYER + AB_FFN[f], l * CD_LAYER + CD_FFN[f], l * (2 * FT) + f * FT
                t = gate_up(u, ab, cd, tg, FA, prev)
                t = to_x(u + 2 * FA, ab + FA // 2, FA * P, 0.5, None, 0, t)
                t = gate_up(u + (2 * FA + KT), ab + (FA // 2 + 4), cd + FA // 2, tg + FA, FB, t)
                eng.wait_ge(taken[1], ab + (FA // 2 + 4) + 1)
                eng.wait_ge(small_loaded, l * (16 * SMALL) + 16 * SMALL)
                return to_x(u + (2 * FT + KT), ab + (FT // 2 + 4), FB * P, 0.5, l * NORMS + (1 + 2 * f), (V_NM, V_NN)[f], t)

            def mix(l, prev):
                u, ab = l * U_LAYER + B_MIX, l * AB_LAYER + AB_MIX
                la, ld = l * (4 * LRU_A), l * (4 * LRU_D)

                def evac_conv(s, m, use, j, out=None):
                    eng.wait_ge(unit_done, u + m + 3)
                    eng.tensor_tensor(cp[:, s, 3:3 + HALF], pair[s][:, 0, 0:HALF], rstd[:, 0:HALF], ALU.mult)
                    eng.tensor_tensor(cp[:, s, 3 + HALF:SAMP0], pair[s][:, 1, 0:TP - HALF], rstd[:, HALF:TP], ALU.mult)
                    eng.tensor_copy(samples(cp[:, s, :], 0, 3), conv_hist[:, j, :, :])
                    eng.tensor_tensor(samples(cp[:, s, :], 3, SLEN),
                                      pair[s][:, 1, TP - HALF:HALF].rearrange("p (b t) -> p b t", b=SEQS),
                                      seq(rstd[:, TP:T]), ALU.mult).then_inc(taken[s], 1)
                    eng.wait_ge(taken[s], use + 2)
                    eng.tensor_copy(conv_new[:, j, 0:3], cp[:, s, TP:TP + 3])
                    eng.tensor_copy(conv_new[:, j, 3:27].rearrange("p (b t) -> p b t", b=SEQS), samples(cp[:, s, :], SLEN, 3))
                    cs = l * (16 * 3) + j * 3
                    w = lambda i: vec[:, bass.ds(V_CQ + j * TAPS + i, 1)]
                    if out is None:
                        eng.wait_ge(pad_done, l + 1)
                        eng.wait_ge(kqv_done, l * 12 + j + 1)
                        eng.tensor_scalar(acc[:, 0:CONV], cp[:, s, 0:CONV], w(0), None, ALU.mult).then_inc(conv_step, 1)
                    else:
                        eng.wait_ge(kqv_done, l * 12 + 13)
                        eng.tensor_scalar(acc[:, 0:CONV], cp[:, s, 0:CONV], w(0), vec[:, V_CB + j - 12:V_CB + j - 11], ALU.mult, ALU.add).then_inc(conv_step, 1)
                    for i in (1, 2):
                        eng.wait_ge(conv_step, cs + i)
                        eng.scalar_tensor_tensor(acc[:, 0:CONV], cp[:, s, i:i + CONV], w(i), acc[:, 0:CONV], ALU.mult, ALU.add).then_inc(conv_step, 1)
                    eng.wait_ge(conv_step, cs + 3)
                    if out is None:
                        eng.scalar_tensor_tensor(acc[:, 0:CONV], cp[:, s, 3:3 + CONV], w(3), acc[:, 0:CONV], ALU.mult, ALU.add).then_inc(conv_done, 1)
                    else:
                        eng.scalar_tensor_tensor(out[:, 0:TP], cp[:, s, 3:3 + TP], w(3), acc[:, 0:TP], ALU.mult, ALU.add)
                        eng.scalar_tensor_tensor(seq(out[:, TP:T]), samples(cp[:, s, :], 3, SLEN), w(3),
                                                 samples(acc, 0, SLEN), ALU.mult, ALU.add).then_inc(conv_done, 1)

                def scaled(s, m, dst):
                    eng.wait_ge(unit_done, u + m + 3)
                    eng.tensor_tensor(tiles(dst), cols(s), tiles(rstd[:, :]), ALU.mult).then_inc(taken[s], 1)

                count = [0]

                def step(ins):
                    count[0] += 1
                    ins.then_inc(tok_d, 1)
                    eng.wait_ge(tok_d, l * TOK_D + count[0])

                def tok1():
                    n4 = CH[4]
                    lp = PC0[:, 0:40].rearrange("p (c j) -> p c j", c=NCH)
                    eng.wait_ge(logit_done, l + 1)
                    eng.tensor_copy(rstd_t[:, 0:4], PC0[:, 40:44])
                    step(eng.tensor_copy(rstd_t[0:n4, 4:5], PC0[0:n4, 44:45]))
                    eng.tensor_tensor(logit[:, 0:4, :], lp[:, 0:4, :], bc(rstd_t[:, 0:4], 8), ALU.mult)
                    step(eng.tensor_tensor(logit[0:n4, 4:5, :], lp[0:n4, 4:5, :], bc(rstd_t[0:n4, 4:5], 8), ALU.mult))
                    y, a, e, z, z2, p, out = (sp[n] for n in ("y", "abs", "e", "z", "z2", "p", "out"))
                    den = out
                    eng.tensor_tensor(y[:, 0:20].rearrange("p (c h) -> p c h", c=NCH), logit[:, :, 4:8], bh(vec[:, V_DT:V_DT + H], NCH), ALU.add)
                    step(eng.tensor_scalar(y[:, 20:24], vec[:, V_LAM:V_LAM + 4], -1.0, None, ALU.mult))
                    step(eng.scalar_tensor_tensor(a[:, :], y[:, :], -1.0, y[:, :], ALU.mult, ALU.max))
                    assert count[0] == T_ABS
                    eng.wait_ge(tok_a, l * 2 + 1)
                    step(eng.tensor_scalar(den[:, :], e[:, :], 2.0, None, ALU.add))
                    step(eng.reciprocal(den[:, :], den[:, :]))
                    step(eng.tensor_tensor(z[:, :], e[:, :], den[:, :], ALU.mult))
                    step(eng.tensor_tensor(z2[:, :], z[:, :], z[:, :], ALU.mult))
                    step(eng.tensor_scalar(p[:, :], z2[:, :], ATANH[0], None, ALU.mult))
                    for k in ATANH[1:]:
                        step(eng.scalar_tensor_tensor(p[:, :], p[:, :], k, z2[:, :], ALU.add, ALU.mult))
                    step(eng.scalar_tensor_tensor(p[:, :], p[:, :], 1.0, z[:, :], ALU.add, ALU.mult))
                    step(eng.tensor_scalar(p[:, :], p[:, :], 2.0, None, ALU.mult))
                    step(eng.scalar_tensor_tensor(out[:, :], y[:, :], 0.0, p[:, :], ALU.max, ALU.add))
                    g = tok["g"]
                    eng.tensor_scalar(lam8[:, 0:4], out[:, 20:24], 8.0, None, ALU.mult)
                    eng.tensor_scalar(lam8[:, 4:8], out[:, 20:24], -8.0, None, ALU.mult)
                    step(eng.scalar_tensor_tensor(g[:, :, :], out[:, 0:20].rearrange("p (c h) -> p c h", c=NCH), -1.0, bh(ea[:, :], NCH), ALU.mult, ALU.mult))
                    step(eng.tensor_tensor(g_seg[0:n4, :, :], bc(mask[0:n4, M_GTS, IND], H), bh(g[0:n4, 4, :], SEGS), ALU.mult))
                    assert count[0] == T_G

                def tok2():
                    n4 = CH[4]
                    kp = PC1[:, 0:40].rearrange("p (c j) -> p c j", c=NCH)
                    eng.wait_ge(kq_sum_done, l + 1)
                    eng.tensor_copy(kq_ss[:, 0:4, :], kp[:, 0:4, :])
                    step(eng.tensor_copy(kq_ss[0:n4, 4:5, :], kp[0:n4, 4:5, :]))
                    assert count[0] == T_SS
                    eng.wait_ge(tok_a, l * 2 + 2)
                    t = lambda n: tok[n][:, :, :]
                    eng.reciprocal(t("rq"), t("nq"))
                    step(eng.reciprocal(t("rk"), t("nk")))
                    eng.tensor_tensor(t("rq2"), t("rq"), t("rq"), ALU.mult)
                    step(eng.tensor_tensor(t("bk2"), t("rk"), t("rk"), ALU.mult))
                    step(eng.tensor_tensor(t("bk2"), t("bk2"), t("beta"), ALU.mult))
                    step(eng.tensor_scalar(t("nb"), t("bk2"), -1.0, None, ALU.mult))
                    assert count[0] == TOK_D

                def lru_1(c):
                    n = [ld + c * LRU_D]
                    eng.wait_ge(lru_a, la + (c * LRU_A + 4))
                    eng.tensor_tensor(lt[:, 2, :], lt[:, 2, :], xc(c), ALU.mult).then_inc(lru_d, 1)
                    eng.tensor_tensor(lt[:, 0, :], lt[:, 1, :], lt[:, 1, :], ALU.mult).then_inc(lru_d, 1)
                    eng.wait_ge(lru_d, n[0] + 3)
                    eng.scalar_tensor_tensor(lt[:, 3, :], lt[:, 0, :], 1.0, lt[:, 3, :], ALU.add, ALU.mult).then_inc(lru_d, 1)

                def lru_2(c):
                    base = ld + c * LRU_D
                    start = lambda i: seq(lt[:, i, TP:T])[:, :, 0]
                    eng.wait_ge(lru_a, la + (c * LRU_A + 5))
                    eng.tensor_tensor(lt[:, 2, :], lt[:, 2, :], lt[:, 0, :], ALU.mult).then_inc(lru_d, 1)
                    eng.tensor_tensor(h_start[:, :], start(1), lru_h0[:, c, :], ALU.mult).then_inc(lru_d, 1)
                    eng.wait_ge(lru_d, base + 6)
                    eng.tensor_tensor(start(2), start(2), h_start[:, :], ALU.add).then_inc(lru_d, 1)
                    eng.memset(start(1), 0.0).then_inc(lru_d, 1)
                    eng.wait_ge(lru_d, base + 8)
                    eng.tensor_tensor_scan(lt[:, 3, :], lt[:, 1, :], lt[:, 2, :], 0.0, ALU.mult, ALU.add).then_inc(lru_d, 1)
                    eng.wait_ge(lru_d, base + 9)
                    eng.tensor_copy(lru_new[:, c, 0:1], lt[:, 3, TP - 1:TP]).then_inc(lru_d, 1)
                    eng.tensor_copy(lru_new[:, c, 1:9], seq(lt[:, 3, TP:T])[:, :, SLEN - 1]).then_inc(lru_d, 1)
                    eng.wait_ge(gelu_done, l * 4 + (c + 1))
                    eng.tensor_tensor(y_s[:, c, :], y_s[:, c, :], lt[:, 3, :], ALU.mult).then_inc(lru_d, 1)

                def turn(it, first):
                    for s in range(2):
                        split(u + it * 2 + s, s, KT * P)
                        prev(s) if first else evac_conv(s, it * 2 - 2 + s, ab + it - 1, it * 2 - 2 + s)
                turn(0, True)
                root(l * NORMS + 1)
                eng.memset(cp[:, :, 0:3], 0.0).then_inc(pad_done, 1)
                eng.wait_ge(wba_hi_done, l + 1)
                eng.tensor_tensor(w_ba_lo[:, :], w_ba[:, :], w_ba_hi[:, :].bitcast(F32), ALU.subtract).then_inc(wba_done, 1)
                with eng.Fori(1, 6) as it:
                    turn(it, False)
                for n in range(12, U_MIX):
                    split(u + n, n % 2, KT * P)
                    m = n - 2
                    use = ab + m // 2
                    if m < 12:
                        evac_conv(m % 2, m, use, m)
                    elif m < 20:
                        if m % 2 == 0:
                            if m >= 16:
                                eng.wait_ge(ri_done, l * 4 + ((m - 12) // 2 - 1))
                            evac_conv(0, m, use, 12 + (m - 12) // 2, xc((m - 12) // 2))
                        else:
                            eng.wait_ge(kq_sum_done, l + 1)
                            scaled(1, m, y_s[:, (m - 12) // 2, :])
                    else:
                        scaled(m % 2, m, z_s[:, m - 20, :])
                    if n == 13:
                        tok1()
                    if n == 15:
                        tok2()
                    if n >= 16:
                        (lru_2 if n % 2 else lru_1)((n - 16) // 2)
                scaled(0, 22, z_s[:, 2, :])
                scaled(1, 23, z_s[:, 3, :])
                eng.memset(s_p[:, :, :], 0.0).then_inc(s_done, 1)
                eng.wait_ge(silu_z_done, l * 4 + 4)
                for c in range(NCH):
                    delta(l, c)
                for j in range(KT):
                    eng.wait_ge(oy_hi_done, l * KT + (j + 1))
                    eng.tensor_tensor(mid_lo[:, j, :], kqv[:, 8 + j, :] if j < 4 else y_s[:, j - 4, :],
                                      mid_hi[:, j, :].bitcast(F32), ALU.subtract).then_inc(oy_done, 1)

            def delta(l, c):
                n, lc = CH[c], l * NCH + c
                tri = mask[0:n, M_TRI if c < 4 else M_TRIS, 0:n]
                t0 = sum(CH[:c])
                bkk, bvt = PC0, PD0
                bks = PC1 if c < 4 else PC0
                tk = lambda name: tok[name][0:n, c, :]
                eng.tensor_tensor(head(z_m, n, n), bh(tri, H), bc(tk("g"), n), ALU.mult).then_inc(grhs_done, 1)
                eng.wait_ge(em_done, lc + 1)
                eng.tensor_tensor(head(em, n, n), head(em, n, n), bh(tri, H), ALU.mult).then_inc(emm_done, 1)
                eng.wait_ge(emm_done, lc + 1)
                eng.wait_ge(kq_done, lc + 1)
                for h in range(H):
                    ins = eng.scalar_tensor_tensor(nt[0:n, h, 0:n], PC0[0:n, h * n:(h + 1) * n], tok["bk2"][0:n, c, h:h + 1],
                                                   em[0:n, h, 0:n], ALU.mult, ALU.mult)
                ins.then_inc(nt_done, 1)
                eng.tensor_tensor(head(attn, n, n), bank(PC1, n, n), head(em, n, n), ALU.mult).then_inc(attn_done, 1)
                eng.wait_ge(nt_done, lc + 1)
                eng.tensor_tensor(head(y_m, n, n), head(nt, n, n), bh(mask[0:n, M_L1T, 0:n], H), ALU.mult).then_inc(y0_tmp, 1)
                eng.wait_ge(y0_tmp, lc + 1)
                eng.tensor_tensor(head(y_m, n, n), bh(mask[0:n, M_ID, 0:n], H), head(y_m, n, n), ALU.subtract).then_inc(y0_done, 1)
                eng.wait_ge(kt_done, lc + 1)
                eng.tensor_tensor(kdec[0:n, :, :], PD1[0:n, :].rearrange("p (h d) -> p h d", h=H), bc(tok_kd(c, n), P), ALU.mult).then_inc(kdec_done, 1)
                eng.wait_ge(vt_done, lc + 1)
                eng.tensor_tensor(vn_s[0:n, :, :], PD0[0:n, :].rearrange("p (h d) -> p h d", h=H), bc(tk("nk"), P), ALU.mult).then_inc(vscaled_done, 1)
                eng.wait_ge(z_init, lc + 1)
                eng.wait_ge(y0_done, lc + 1)
                for k, lev in enumerate(LEVELS[c]):
                    last = k == len(LEVELS[c]) - 1
                    i, iz = l * LV + (lv(c, k) + 1), l * LZ + (lv(c, k) - c + 1)
                    eng.wait_ge(nz_done, i)
                    eng.tensor_tensor(head(p_m, n, n), bank(PC0, n, n), bh(mask[0:n, LEVEL_MASK[lev], 0:n], H), ALU.mult).then_inc(p_done, 1)
                    if not last:
                        eng.wait_ge(zp_done, iz)
                        eng.tensor_tensor(head(z_m, n, n), head(z_m, n, n), bank(PC1, n, n), ALU.subtract).then_inc(z_upd, 1)
                    eng.wait_ge(py_done, i)
                    eng.tensor_tensor(head(y_m, n, n), head(y_m, n, n), bank(PD0, n, n), ALU.subtract).then_inc(y_upd, 1)
                    if not last:
                        eng.wait_ge(z_upd, iz)
                    eng.wait_ge(y_upd, i)
                eng.wait_ge(ks_done, l * 4 + (c + 1)) if c < 4 else eng.wait_ge(kstt_done, l * H + H)
                eng.wait_ge(vscaled_done, lc + 1)
                for h in range(H):
                    ins = eng.scalar_tensor_tensor(em[0:n, h, :], bks[0:n, h * P:(h + 1) * P], tok_eg(c, h, n),
                                                   vn_s[0:n, h, :], ALU.mult, ALU.subtract)
                ins.then_inc(r_done, 1)
                eng.wait_ge(zr_done, lc + 1)
                bz = PC0 if c < 4 else PC1
                eng.tensor_tensor(nt[0:n, :, :], bz[0:n, :].rearrange("p (h d) -> p h d", h=H), bc(tk("nb"), P), ALU.mult).then_inc(vnew_done, 1)
                if c < 4:
                    eng.wait_ge(kv_done, l * 4 + (c + 1))
                    for h in range(H):
                        ins = eng.scalar_tensor_tensor(s_p[:, h, :], s_p[:, h, :], e_last[:, c * H + h:c * H + h + 1],
                                                       PC1[:, h * P:(h + 1) * P], ALU.mult, ALU.add)
                    ins.then_inc(s_done, 1)
                    eng.wait_ge(s_done, l * 5 + (c + 2))
                eng.wait_ge(av_done, lc + 1)
                eng.wait_ge(qs_scaled, lc + 1)
                eng.tensor_tensor(p_m[0:n, :, :], qs[0:n, :, :], PD0[0:n, :].rearrange("p (h d) -> p h d", h=H), ALU.add).then_inc(o_done, 1)
                if c == 4:
                    segments(l)
                eng.wait_ge(o_sq_done, lc + 1)
                st = l * (3 * NCH) + 3 * c
                eng.scalar_tensor_tensor(o_ms[0:n, :], o_ss[0:n, :], 1.0 / DK, tk("rq2"), ALU.mult, ALU.mult).then_inc(o_step, 1)
                eng.wait_ge(o_rms_done, lc + 1)
                eng.reciprocal(o_rec[0:n, :], o_rms[0:n, :]).then_inc(o_step, 1)
                eng.wait_ge(o_step, st + 2)
                eng.tensor_tensor(o_fac[0:n, :], o_rec[0:n, :], tk("rq"), ALU.mult).then_inc(o_step, 1)
                eng.wait_ge(o_step, st + 3)
                eng.tensor_tensor(p_m[0:n, :, :], p_m[0:n, :, :], bc(o_fac[0:n, :], P), ALU.mult).then_inc(on_done, 1)
                eng.wait_ge(ot_done, lc + 1)
                eng.scalar_tensor_tensor(kqv[:, 8:12, t0:t0 + n], bank(PD1, P, n), vec[:, V_ON:V_ON + 1],
                                         z_s[:, :, t0:t0 + n], ALU.mult, ALU.mult).then_inc(og_done, 1)

            def segments(l):
                n = CH[4]
                eng.wait_ge(vnew_done, l * NCH + NCH)
                for h in range(H):
                    i = l * H + (h + 1)
                    if h:
                        eng.wait_ge(segkv_done, i - 1)
                    eng.tensor_tensor(vseg[0:n, :, :], bh(nt[0:n, h, :], SEGS), bc(mask[0:n, M_GTS, IND], P), ALU.mult).then_inc(vseg_done, 1)
                    eng.wait_ge(segkv_done, i)
                    for s in range(SEGS):
                        state = s_p[:, h, :] if s == 0 else (s0a if h < 2 else s0b)[:, h % 2, s - 1, :]
                        src = (PC1, PD1, PC0)[s // 4][:, (s % 4) * P:(s % 4 + 1) * P]
                        ins = eng.scalar_tensor_tensor(state, state, e_last[:, 16 + s * H + h:17 + s * H + h], src, ALU.mult, ALU.add)
                    ins.then_inc(seg_s_done, 1)

            for t in taken:
                eng.sem_inc(t, 1)
            eng.sem_inc(lru_d, 1)
            eng.memset(eps[:, 0:1], EPS)
            eng.memset(eps[:, 1:2], EPS * DK)
            for t in (logit[:, :, :], kq_ss[:, :, :], e_g4[:, :]):
                eng.memset(t, 0.0)
            eng.memset(rstd_t[:, :], 0.0).then_inc(init_done, 1)
            eng.wait_ge(mask_loaded, 16)
            eng.tensor_copy(ones_r[:, :], mask[:, M_ONE, :]).then_inc(init_done, 1)
            eng.wait_ge(x_loaded, 16 * KT)
            eng.wait_ge(gain_loaded, 16)
            for k in range(KT):
                new_x(k, k % 2, gain0[:, k:k + 1], k)
            root(0)
            with eng.Fori(0, DEPTH) as l:
                t = ffn(l, 0, lambda s: None)
                mix(l, t)
                t = to_x(l * U_LAYER + B_OUT, l * AB_LAYER + AB_OUT, KT * P, 1.0, l * NORMS + 2, V_N2, lambda s: None)
                t(0)
                t(1)
                root(l * NORMS + 2)
                eng.wait_ge(states_out, l * (16 * 5) + 16 * 5)
                t = ffn(l, 1, lambda s: None)
                t(0)
                t(1)
                root(l * NORMS + 3)
            for k in range(KT):
                eng.scalar_tensor_tensor(x[:, k, :], x[:, k, :], vec[:, V_NN + k:V_NN + k + 1], rstd[:, :], ALU.mult, ALU.mult).then_inc(y_out, 1)

        @block.tensor
        def _(eng):
            def product(pr, s, nk, hi, lo, u, each=None):
                eng.wait_ge(w_lo_done, u + 3)
                for k in range(nk):
                    if each:
                        each(k)
                    w = slice(k * P, (k + 1) * P)
                    for a, b in ((w_hi, hi), (w_hi, lo), (w_lo, hi)):
                        for half in range(2):
                            ins = eng.matmul(pair[pr][:, half, 0:HALF], a[:, s, w], b[:, k, half * HALF:(half + 1) * HALF],
                                             start=k == 0 and b is hi and a is w_hi, stop=k == nk - 1 and a is w_lo)
                ins.then_inc(unit_done, 1)

            def squares(s, nsq, first=False, last=False):
                eng.wait_ge(sq_done, nsq + 1)
                for part in (sq_hi, sq_lo):
                    for half in range(2):
                        ins = eng.matmul(pair[3][:, half, 0:HALF], ones_r[:, :], part[:, s, half * HALF:(half + 1) * HALF],
                                         start=first and part is sq_hi, stop=last and part is sq_lo)
                ins.then_inc(ss_used, 1)

            def gate_up(u, ab, cd, n, norm=None):
                def turn(it, first):
                    v = u + it * 4
                    for s in range(2):
                        eng.wait_ge(taken[s], ab + it + 1)
                        product(s, 0, KT, h_hi, h_lo, v + 2 * s, (lambda k: eng.wait_ge(h_done, norm * KT + (k + 1))) if first and s == 0 and norm is not None else None)
                        if first and s == 1 and norm is not None:
                            eng.wait_ge(rms_done, norm + 1)
                        eng.wait_ge(taken[2 + s], cd + it + 1)
                        product(2 + s, 1, KT, h_hi, h_lo, v + 2 * s + 1)
                turn(0, True)
                with eng.Fori(1, n // 2) as it:
                    turn(it, False)

            def to_x(u, ab, nk, norm, wait0):
                def turn(it, first):
                    for s in range(2):
                        eng.wait_ge(taken[s], ab + it + 1)
                        product(s, s, nk, mid_hi, mid_lo, u + it * 2 + s, wait0 if first and s == 0 else None)
                        if norm is not None and not (first and s == 0):
                            squares(1 - s, norm * KT + (it * 2 + s - 1), first=first)
                turn(0, True)
                with eng.Fori(1, KT // 2) as it:
                    turn(it, False)
                if norm is not None:
                    return lambda: squares(1, norm * KT + (KT - 1), last=True)

            def ffn(l, f, norm):
                u, ab, cd, tg = l * U_LAYER + B_FFN[f], l * AB_LAYER + AB_FFN[f], l * CD_LAYER + CD_FFN[f], l * (2 * FT) + f * FT
                gate_up(u, ab, cd, FA, norm)
                to_x(u + 2 * FA, ab + FA // 2, FA, None, lambda k: eng.wait_ge(mid_done, tg + (k + 1)))
                gate_up(u + (2 * FA + KT), ab + (FA // 2 + 4), cd + FA // 2, FB)
                return to_x(u + (2 * FT + KT), ab + (FT // 2 + 4), FB, norm + 1, lambda k: eng.wait_ge(mid_done, tg + (FA + k + 1)))

            def mix(l, last_squares):
                u, ab = l * U_LAYER + B_MIX, l * AB_LAYER + AB_MIX
                norm = l * NORMS + 1
                eng.wait_ge(taken[0], ab + 1)
                product(0, 0, KT, h_hi, h_lo, u, lambda k: eng.wait_ge(h_done, norm * KT + (k + 1)))
                last_squares()
                eng.wait_ge(taken[1], ab + 1)
                product(1, 1, KT, h_hi, h_lo, u + 1)
                with eng.Fori(1, 6) as it:
                    for s in range(2):
                        eng.wait_ge(taken[s], ab + it + 1)
                        product(s, s, KT, h_hi, h_lo, u + it * 2 + s)

                def logits():
                    eng.wait_ge(wba_done, l + 1)
                    eng.wait_ge(rstd_done, norm + 1)
                    for c in range(NCH):
                        n, t0 = CH[c], sum(CH[:c])
                        for k in range(KT):
                            for a, b in ((h_hi, w_ba_hi), (h_lo, w_ba_hi), (h_hi, w_ba_lo)):
                                eng.matmul(PC0[0:n, c * 8:c * 8 + 8], a[:, k, t0:t0 + n], b[:, k * 8:k * 8 + 8],
                                           start=k == 0 and a is h_hi and b is w_ba_hi, stop=k == KT - 1 and b is w_ba_lo)
                    for c in range(NCH):
                        n, t0 = CH[c], sum(CH[:c])
                        ins = eng.matmul(PC0[0:n, 40 + c:41 + c], rstd[0:1, t0:t0 + n], mask[0:1, M_ONE, 0:1], start=True, stop=True)
                    ins.then_inc(logit_done, 1)

                def kq_sums():
                    for j in range(8):
                        eng.wait_ge(kq_sq_done, l * 8 + (j + 1))
                        for c in range(NCH):
                            n, t0 = CH[c], sum(CH[:c])
                            ins = eng.matmul(PC1[0:n, c * 8 + j:c * 8 + j + 1], (z_s if j < 4 else y_s)[:, j % 4, t0:t0 + n],
                                             mask[:, M_ONE, 0:1], start=True, stop=True)
                    ins.then_inc(kq_sum_done, 1)

                def g_sums():
                    g, n4 = tok["g"], CH[4]
                    eng.wait_ge(tok_d, l * TOK_D + T_G)
                    g4 = g[:, 0:4, :].rearrange("p c h -> p (c h)")
                    mm = lambda out, a, b: eng.matmul(out, a, b, start=True, stop=True)
                    mm(PD0[:, 0:16], mask[:, M_TRI, :], g4)
                    mm(PD0[:, 16:32], mask[:, M_GT, :], g4)
                    mm(PD0[0:n4, 32:36], mask[0:n4, M_TRIS, 0:n4], g[0:n4, 4, :])
                    mm(PD0[0:n4, 36:40], mask[0:n4, M_GTS, 0:n4], g[0:n4, 4, :])
                    mm(PD0[:, 40:56], mask[:, M_ONE, :], g4)
                    mm(PD0[:, 56:56 + SEGS * H], mask[0:n4, M_ONE, :], g_seg[0:n4, :, :].rearrange("p s h -> p (s h)")).then_inc(gsum_done, 1)

                def ri(c):
                    eng.wait_ge(conv_done, l * 16 + (12 + c + 1))
                    if c:
                        eng.wait_ge(lru_a, l * (4 * LRU_A) + ((c - 1) * LRU_A + 2))
                    else:
                        eng.wait_ge(gexp_done, l + 1)
                        eng.wait_ge(tok_d, l * TOK_D + T_SS)
                    for g in range(2):
                        for half in range(2):
                            ins = eng.matmul(pair[2 + g][:, half, 0:HALF], w_ri[:, c, g, :], xc(c)[:, half * HALF:(half + 1) * HALF], start=True, stop=True)
                    ins.then_inc(ri_done, 1)

                for n in range(12, U_MIX):
                    eng.wait_ge(taken[n % 2], ab + n // 2 + 1)
                    product(n % 2, n % 2, KT, h_hi, h_lo, u + n)
                    if n == 12:
                        logits()
                    if n == 14:
                        kq_sums()
                        g_sums()
                    if n >= 15 and n % 2:
                        if n < 23:
                            ri((n - 15) // 2)
                for c in range(NCH):
                    delta(l, c)

            def delta(l, c):
                n, lc = CH[c], l * NCH + c
                t0 = sum(CH[:c])
                idn = mask[0:n, M_ID, 0:n]
                tt = slice(t0, t0 + n)
                mm = lambda out, a, b, start=True, stop=True: eng.matmul(out, a, b, start=start, stop=stop)
                if c == 0:
                    eng.wait_ge(lru_a, l * (4 * LRU_A) + (3 * LRU_A + 2))
                else:
                    eng.wait_ge(og_done, lc)
                for h in range(H):
                    mm(PC0[0:n, h * n:(h + 1) * n], kqv[:, 4 + h, tt], kqv[:, 4 + h, tt])
                for h in range(H):
                    ins = mm(PC1[0:n, h * n:(h + 1) * n], kqv[:, 4 + h, tt], kqv[:, 8 + h, tt])
                ins.then_inc(kq_done, 1)
                eng.wait_ge(grhs_done, lc + 1)
                mm(bank(PD0, n, n), mask[0:n, M_GT if c < 4 else M_GTS, 0:n], head(z_m, n, n)).then_inc(dt_done, 1)
                for h in range(H):
                    ins = eng.transpose(PD1[0:n, h * P:(h + 1) * P], kqv[:, 4 + h, tt], mask[:, M_ID, :])
                ins.then_inc(kt_done, 1)
                eng.wait_ge(em_done, lc + 1)
                for h in range(H):
                    ins = eng.transpose(PD0[0:n, h * P:(h + 1) * P], kqv[:, h, tt], mask[:, M_ID, :])
                ins.then_inc(vt_done, 1)
                eng.wait_ge(y0_done, lc + 1)
                for h in range(H):
                    ins = eng.transpose(PC0[0:n, h * n:(h + 1) * n], y_m[0:n, h, 0:n], idn)
                ins.then_inc(z0_done, 1)
                eng.wait_ge(z_init, lc + 1)
                eng.wait_ge(attn_done, lc + 1)
                eng.wait_ge(vscaled_done, lc + 1)
                for k, lev in enumerate(LEVELS[c]):
                    last = k == len(LEVELS[c]) - 1
                    i, iz = l * LV + (lv(c, k) + 1), l * LZ + (lv(c, k) - c + 1)
                    if k:
                        eng.wait_ge(z_upd, iz - 1)
                    for h in range(H):
                        ins = mm(PC0[0:n, h * n:(h + 1) * n], nt[0:n, h, 0:n], z_m[0:n, h, 0:n])
                    ins.then_inc(nz_done, 1)
                    eng.wait_ge(p_done, i)
                    if k:
                        eng.wait_ge(y_upd, i - 1)
                    if not last:
                        for h in range(H):
                            ins = mm(PC1[0:n, h * n:(h + 1) * n], y_m[0:n, h, 0:n], p_m[0:n, h, 0:n])
                        ins.then_inc(zp_done, 1)
                    for h in range(H):
                        ins = mm(PD0[0:n, h * n:(h + 1) * n], p_m[0:n, h, 0:n], y_m[0:n, h, 0:n])
                    ins.then_inc(py_done, 1)
                eng.wait_ge(kdec_done, lc + 1)
                eng.wait_ge(s_done, l * 5 + (min(c, 4) + 1))
                if c < 4:
                    for h in range(H):
                        ins = mm(PC1[0:n, h * P:(h + 1) * P], kqv[:, 4 + h, tt], s_p[:, h, :])
                    ins.then_inc(ks_done, 1)
                    for h in range(H):
                        ins = mm(PD1[0:n, h * P:(h + 1) * P], kqv[:, 8 + h, tt], s_p[:, h, :])
                    ins.then_inc(qs_done, 1)
                else:
                    eng.wait_ge(y_upd, l * LV + LV)
                    eng.wait_ge(s0a_loaded, l * 16 + 16)
                    eng.wait_ge(s0b_loaded, l * 16 + 16)

                    def turn_head(h):
                        eng.wait_ge(kst_done, l * H + (h + 1))
                        eng.transpose(PC0[0:n, h * P:(h + 1) * P], ks_t[:, h % 2, 0, 0:n], mask[:, M_ID, :])
                        eng.transpose(PD0[0:n, h * P:(h + 1) * P], ks_t[:, h % 2, 1, 0:n], mask[:, M_ID, :]).then_inc(kstt_done, 1)
                    for h in range(H):
                        if h >= 2:
                            eng.wait_ge(kst_done, l * H + (h - 1))
                        out = segbank(h)[:, 0:2 * n].rearrange("p (k t) -> p k t", k=2)
                        for s in range(SEGS):
                            state = s_p[:, h, :] if s == 0 else (s0a if h < 2 else s0b)[:, h % 2, s - 1, :]
                            a, b = (0, 16) if s == 0 else (16 + (s - 1) * SLEN, 16 + s * SLEN)
                            ins = mm(out[:, :, a:b], state, kqv[:, 4 + h:9 + h:4, t0 + a:t0 + b])
                        ins.then_inc(seg_done, 1)
                        if h:
                            turn_head(h - 1)
                    turn_head(3)
                eng.wait_ge(r_done, lc + 1)
                eng.wait_ge(y_upd, l * LV + lv(c + 1, 0))
                bz = PC0 if c < 4 else PC1
                for h in range(H):
                    ins = mm(bz[0:n, h * P:(h + 1) * P], y_m[0:n, h, 0:n], em[0:n, h, :])
                ins.then_inc(zr_done, 1)
                eng.wait_ge(vnew_done, lc + 1)
                eng.wait_ge(qs_scaled, lc + 1)
                if c < 4:
                    for h in range(H):
                        ins = mm(PC1[:, h * P:(h + 1) * P], kdec[0:n, h, :], nt[0:n, h, :])
                    ins.then_inc(kv_done, 1)
                for h in range(H):
                    ins = mm(PD0[0:n, h * P:(h + 1) * P], attn[0:n, h, 0:n], nt[0:n, h, :])
                ins.then_inc(av_done, 1)
                if c == 4:
                    for h in range(H):
                        i = l * H + (h + 1)
                        eng.wait_ge(vseg_done, i)
                        if h:
                            eng.wait_ge(seg_s_done, i - 1)
                        mm(PC1[:, :], kdec[0:n, h, :], vseg[0:n, 0:4, :])
                        mm(PD1[:, :], kdec[0:n, h, :], vseg[0:n, 4:8, :])
                        mm(PC0[:, 0:P], kdec[0:n, h, :], vseg[0:n, 8, :]).then_inc(segkv_done, 1)
                    eng.wait_ge(seg_s_done, l * H + H)
                eng.wait_ge(on_done, lc + 1)
                for h in range(H):
                    ins = eng.transpose(PD1[:, h * n:(h + 1) * n], p_m[0:n, h, :], idn)
                ins.then_inc(ot_done, 1)

            eng.wait_ge(init_done, 2)
            for k in range(KT):
                squares(k % 2, k, k == 0, k == KT - 1)
            with eng.Fori(0, DEPTH) as l:
                t = ffn(l, 0, l * NORMS)
                mix(l, t)
                t = to_x(l * U_LAYER + B_OUT, l * AB_LAYER + AB_OUT, KT, l * NORMS + 2,
                         lambda k: eng.wait_ge(oy_done, l * KT + (k + 1)))
                t()
                t = ffn(l, 1, l * NORMS + 2)
                t()


_OUTS = {"y": (KT, P, T), "conv": (DEPTH, P, 16, 27), "lru": (DEPTH, P, 4, 9), "dp": (DEPTH, P, H, P), "ds": (DEPTH * 2, P, 2, SEQS, P)}


def _units(w, m_tiles):
    rows = w.shape[0]
    return w.reshape(rows // P, P, m_tiles, P).transpose(2, 1, 0, 3).reshape(m_tiles, P, rows)


def _per_tile(v):
    return np.moveaxis(v.reshape(v.shape[:-1] + (-1, P)), -1, 0).reshape(P, -1)


def _rows(v):
    return np.broadcast_to(v, (P, v.shape[0]))


def _layout(a):
    d_a = H * DK
    x = np.concatenate([a["meta_tokens"], a["x_prompt"][0], a["x_sample"].reshape(TS, D)], axis=0)
    n1, nm, n2 = a["norm_ffn1"], a["norm_mix"], a["norm_ffn2"]
    vec, wba, wri, chist, lru0, s0, wgu, wda, wdb, win, wout = ([] for _ in range(11))
    for l in range(DEPTH):
        cw = a["conv_qkv"][l].T
        vkq = np.concatenate([cw[2 * d_a:], cw[d_a:2 * d_a], cw[:d_a], a["conv_lru_w"][l].T], axis=0)
        taps = vkq.reshape(16, P, TAPS).transpose(1, 0, 2).reshape(P, 16 * TAPS)
        after = n1[l + 1] if l + 1 < DEPTH else a["norm_final"]
        vec.append(np.concatenate([_per_tile(nm[l]), _per_tile(n2[l]), _per_tile(after), taps]
                                  + [_per_tile(a[n][l]) for n in ("conv_lru_b", "b_rgate", "b_igate", "lru_lambda")]
                                  + [_rows(a["a_log"][l]), _rows(a["dt_bias"][l]), _per_tile(a["norm_delta_out"][l])], axis=1))
        w = a["w_in"][l]
        q, k, v, z, ba, xr, gate = np.split(w, [d_a, 2 * d_a, 3 * d_a, 4 * d_a, 4 * d_a + 2 * H, 4 * d_a + 2 * H + DR], axis=1)
        wba.append(ba.reshape(KT, P, 8).transpose(1, 0, 2).reshape(P, KT * 8))
        u = lambda m: _units(m, 4)
        win.append(np.concatenate([u(v), u(k), u(q), np.stack([u(xr), u(gate)], axis=1).reshape(8, P, D), u(z)], axis=0))
        ri = np.zeros((P, 4, 2, P), np.float32)
        for g, name in enumerate(("w_rgate", "w_igate")):
            for b in range(8):
                r = slice((b % 2) * 64, (b % 2 + 1) * 64)
                ri[r, b // 2, g, r] = a[name][l, b]
        wri.append(ri)
        hq, hk, hv = np.split(a["state_delta_conv"][l], 3, axis=2)
        h = np.concatenate([hv, hk, hq, a["state_lru_conv"][l]], axis=2)
        chist.append(h.reshape(SEQS, TAPS - 1, 16, P).transpose(3, 2, 0, 1))
        lru0.append(a["state_lru"][l].reshape(SEQS, 4, P).transpose(2, 1, 0))
        s0.append(a["state_delta"][l].reshape(SEQS, 2, 2, DK, P).transpose(1, 3, 2, 0, 4))
        for f in ("1", "2"):
            gu = np.stack([_units(a[f"w_ffn{f}_gate"][l], FT), _units(a[f"w_ffn{f}_up"][l], FT)], axis=1)
            wgu.append(gu.reshape(2 * FT, P, D))
            down = _units(a[f"w_ffn{f}_down"][l], KT)
            wda.append(down[:, :, :FA * P])
            wdb.append(down[:, :, FA * P:])
        wout.append(_units(a["w_out"][l], KT))
    cat = lambda t: np.concatenate(t, axis=0)
    return {"xT": x.T.reshape(KT, P, T), "gain0": _per_tile(n1[0]), "mask": chunk_masks(), "vec": np.stack(vec),
            "wba": np.stack(wba), "wri": np.stack(wri), "chist": np.stack(chist), "lru0": np.stack(lru0), "s0": cat(s0),
            "wgu": cat(wgu), "wda": cat(wda), "wdb": cat(wdb), "win": cat(win), "wout": cat(wout)}


def _results(r):
    y = r["y"].reshape(D, T).T
    conv = r["conv"].transpose(0, 3, 2, 1).reshape(DEPTH, 27, 16 * P)
    v, k, q, xr = np.split(conv, 4, axis=2)
    qkv = np.concatenate([q, k, v], axis=2)
    lru = r["lru"].transpose(0, 3, 2, 1).reshape(DEPTH, 9, DR)
    dp = r["dp"].transpose(0, 2, 1, 3)[:, None]
    ds = r["ds"].reshape(DEPTH, 2, P, 2, SEQS, P).transpose(0, 4, 1, 3, 2, 5).reshape(DEPTH, SEQS, H, DK, P)
    rows = lambda t: (t[:, 0:3][:, None], t[:, 3:].reshape(DEPTH, SEQS, 3, t.shape[2]))
    (qkv_p, qkv_s), (xr_p, xr_s) = rows(qkv), rows(xr)
    out = (y[N_META:TP][None], y[TP:].reshape(SEQS, SLEN, D), dp, qkv_p, lru[:, 0:1], xr_p, ds, qkv_s, lru[:, 1:], xr_s)
    return tuple(np.ascontiguousarray(o) for o in out)


def kernel(**inputs):
    import concourse.bacc as _bacc
    from concourse.bass_utils import run_bass_kernel_spmd as _run

    arrays = {f"in_{n}": np.ascontiguousarray(v) for n, v in _layout({n: np.asarray(v) for n, v in inputs.items()}).items()}
    nc = _bacc.Bacc("TRN2", target_bir_lowering=False, num_devices=1)
    I = {n[3:]: nc.dram_tensor(n, v.shape, mybir.dt.from_np(v.dtype), kind="ExternalInput").ap() for n, v in arrays.items()}
    O = {n: nc.dram_tensor(f"out_{n}", s, F32, kind="ExternalOutput").ap() for n, s in _OUTS.items()}
    build(nc, I, O)
    r = _run(nc, [arrays], core_ids=[0])
    return _results({n: r.results[0][f"out_{n}"] for n in _OUTS})
```

```python
from contextlib import ExitStack

import numpy as np
import concourse.bass as bass
from concourse import mybir

F32 = mybir.dt.float32
F32R = mybir.dt.float32r
ACT = mybir.ActivationFunctionType
ALU = mybir.AluOpType

P = 128
DEPTH, D, SEQ, N_META = 2, 1024, 512, 16
SEQS, SLEN = 8, 8
TP = N_META + SEQ
TS = SEQS * SLEN
T = TP + TS
HALF = T // 2
KT = D // P
FT = 22
FA, FB = 12, 10
H, DK, DR = 4, 128, 512
TAPS = 4
PAD = TAPS - 1 + TP + SEQS * (TAPS - 1 + SLEN)
CONV = PAD - (TAPS - 1)
SAMP0 = TAPS - 1 + TP
STRIDE = TAPS - 1 + SLEN
SEGS = SEQS
CH = [TS, P, P, P, P, TP - 4 * P]
T0 = [TP, 0, P, 2 * P, 3 * P, 4 * P]
NCH = len(CH)
LEVELS = [[2, 4]] + [[2, 4, 8, 16, 32, 64]] * 4 + [[2, 4, 8]]
SUM_G = (NCH - 1) * H + SEGS * H
EPS = 1e-6

V_NM, V_N2, V_NN, V_CQ, V_CL, V_CB, V_BR, V_BI, V_LAM, V_ALOG, V_DT, V_ON = (
    0, 8, 16, 24, 72, 88, 92, 96, 100, 104, 108, 112)
NV = 113
M_TRI, M_TRIS, M_GT, M_GTS, M_L1T, M_L2, M_L4, M_L8, M_L16, M_L32, M_L64, M_ID, M_ONE = range(13)
N_MASKS, IND = 13, slice(96, 104)
LEVEL_MASK = {2: M_L2, 4: M_L4, 8: M_L8, 16: M_L16, 32: M_L32, 64: M_L64}

U_FFN = 2 * FT + 16
U_MIX = 24
U_OUT = 8
U_LAYER = 2 * U_FFN + U_MIX + U_OUT
B_FFN = (0, U_FFN + U_MIX + U_OUT)
B_MIX = U_FFN
B_OUT = U_FFN + U_MIX
AB_LAYER, AB_FFN, AB_MIX, AB_OUT = 54, (0, 35), 19, 31
CD_LAYER, CD_FFN = 22, (0, 11)
NORMS = 3
SMALL = 5
LRU_A, LRU_D = 5, 11
T_ABS, T_G, T_SS, TOK_D = 3, 21, 22, 26
SP_N = NCH * H + 4
ATANH = [1.0 / (2 * i + 1) for i in range(8, 0, -1)]


def chunk_masks():
    m = np.zeros((N_MASKS, P, P), np.float32)
    r = np.arange(P)
    row, col = r[:, None], r[None, :]
    seg = r // SLEN
    same = seg[:, None] == seg[None, :]
    m[M_TRI] = row <= col
    m[M_TRIS] = (row <= col) & same
    m[M_GT] = row > col
    m[M_GTS] = (row > col) & same
    for s, at in LEVEL_MASK.items():
        m[at] = (row // (2 * s) == col // (2 * s)) & (row % (2 * s) >= s) & (col % (2 * s) < s)
    m[M_L1T] = (row // 2 == col // 2) & (col % 2 == 1) & (row % 2 == 0)
    m[M_ID] = row == col
    m[M_ONE] = 1.0
    m[M_GTS, :, IND] = seg[:, None] == np.arange(SEGS)[None, :]
    return np.ascontiguousarray(m.transpose(1, 0, 2))


def build(nc, I, O):
    ctx = ExitStack()

    def sb(name, shape, dt=F32, stack=ctx):
        return stack.enter_context(nc.sbuf_tensor(name, shape, dt))

    def sem(name):
        return ctx.enter_context(nc.semaphore(name))

    with ctx:
        x = sb("x", [P, KT, T])
        with ExitStack() as st:
            h_hi, h_lo = sb("h_hi", [P, KT, T], F32R, st), sb("h_lo", [P, KT, T], F32R, st)
        with ExitStack() as st:
            y1, attn1, kdec1, vn1, r_s, v_new, o_s, qs = (
                sb(n, [P, H, P], F32, st) for n in ("y1", "attn1", "kdec1", "vn1", "r_s", "v_new", "o_s", "qs"))
            p_c, z_c = (sb(n, [P, H * P // 2], F32, st) for n in ("p_c", "z_c"))
        sb("h_room", [P, 2 * KT * T])
        w_raw = sb("w_raw", [P, 2, FA * P])
        w_hi, w_lo = sb("w_hi", [P, 2, FA * P], F32R), sb("w_lo", [P, 2, FA * P], F32R)
        rms, rstd = sb("rms", [P, T]), sb("rstd", [P, T])
        gain0 = sb("gain0", [P, KT])
        vec = sb("vec", [P, NV])
        w_ba = sb("w_ba", [P, KT * 8])
        w_ba_hi, w_ba_lo = sb("w_ba_hi", [P, KT * 8], F32R), sb("w_ba_lo", [P, KT * 8], F32R)
        w_ri = sb("w_ri", [P, 4, 2, P])
        conv_hist = sb("conv_hist", [P, 16, SEQS, TAPS - 1])
        lru_h0 = sb("lru_h0", [P, 4, SEQS])
        conv_new = sb("conv_new", [P, 16, 27])
        lru_new = sb("lru_new", [P, 4, 9])
        mask = sb("mask", [P, N_MASKS, P])
        ones_r = sb("ones_r", [P, P], F32R)
        tok = {n: sb("tok_" + n, [P, NCH, H]) for n in
               ("beta", "g", "nk", "nb", "bk2", "rq", "rq2", "nq", "rk")}
        logit = sb("logit", [P, NCH, 8])
        g_hi, g_lo = sb("g_hi", [P, NCH, H], F32R), sb("g_lo", [P, NCH, H])
        kq_ss = sb("kq_ss", [P, NCH, 8])
        ea = sb("ea", [P, H])
        lam8 = sb("lam8", [P, 8])
        h_start = sb("h_start", [P, SEQS])
        e_g, e_gs, e_gt = sb("e_g", [P, 32]), sb("e_gs", [P, 8]), sb("e_gt", [P, 8])
        g_seg = sb("g_seg", [P, SEGS, H])
        e_last = sb("e_last", [P, SUM_G])
        o_ss, o_ms, o_rms, o_rec, o_fac = (sb(n, [P, H]) for n in ("o_ss", "o_ms", "o_rms", "o_rec", "o_fac"))

        eps = sb("eps", [P, 2])
        with ExitStack() as st:
            mid_hi, mid_lo = (sb(n, [P, FA, T], F32R, st) for n in ("mid_hi", "mid_lo"))
            gate_s, silu_s, prod = (sb(n, [P, 2, T], F32, st) for n in ("gate_s", "silu_s", "prod"))
            up_s = sb("up_s", [P, T], F32, st)
            sq = sb("sq", [P, 2, T], F32, st)
            sq_hi, sq_lo = sb("sq_hi", [P, 2, T], F32R, st), sb("sq_lo", [P, 2, T], F32R, st)
        with ExitStack() as st:
            cp = sb("cp", [P, 2, PAD], F32, st)
            acc = sb("acc", [P, PAD], F32, st)
            with ExitStack() as inner:
                sq_k = sb("sq_k", [P, 4, T], F32, inner)
            em, attn0, nt, z_m, y0 = (sb(n, [P, H, P], F32, st) for n in ("em", "attn0", "nt", "z_m", "y0"))
            sp = {n: sb("sp_" + n, [P, SP_N], F32, st) for n in ("y", "abs", "e", "z", "z2", "p", "out")}
            sb("gap0", [P, KT * T - 3 * PAD - 5 * H * P - 7 * SP_N], F32, st)
            lt = sb("lt", [P, 4, T], F32, st)
            with ExitStack() as inner:
                sq_q = sb("sq_q", [P, 4, T], F32, inner)
            kdec0, vn0 = (sb(n, [P, H, P], F32, st) for n in ("kdec0", "vn0"))
            after_r = sb("after_r", [P, 2, P], F32R, st)
            gr_hi, gr_lo = (sb(n, [P, H, P], F32R, st) for n in ("gr_hi", "gr_lo"))
            sb("gap1", [P, 4 * T - 4 * H * P - 2 * P], F32, st)
            z_s = sb("z_s", [P, 4, T], F32, st)
            s0a = sb("s0a", [P, 2, SEQS, P], F32, st)
            s_p = sb("s_p", [P, H, P], F32, st)
            kqv = sb("kqv", [P, 12, T], F32, st)
            y_s = sb("y_s", [P, 4, T], F32, st)
        y_c, attn, kdec, vn_s = (y0, y1), (attn0, attn1), (kdec0, kdec1), (vn0, vn1)
        s0b = lt[:, :, :].rearrange("p a t -> p (a t)")[:, 0:2048].rearrange("p (h s d) -> p h s d", h=2, s=SEQS)
        vseg = cp[:, :, :].rearrange("p a t -> p (a t)")[:, 0:SEGS * P].rearrange("p (s d) -> p s d", s=SEGS)
        ks_t = acc[:, 0:4 * TS].rearrange("p (b k t) -> p b k t", b=2, k=2)

        pair = [ctx.enter_context(nc.psum_tensor(f"pair{n}", [P, 2, 512], F32)) for n in "ABCD"]
        PA0, PA1, PB0, PB1, PC0, PC1, PD0, PD1 = (pair[i // 2][:, i % 2, :] for i in range(8))

        w_loaded = [sem("w_loaded0"), sem("w_loaded1")]
        w_hi_done, w_lo_done, unit_done = (sem(n) for n in (
            "w_hi_done", "w_lo_done", "unit_done"))
        silu_done, prod_done, mid_hi_done, mid_done = (sem(n) for n in (
            "silu_done", "prod_done", "mid_hi_done", "mid_done"))
        h_hi_done, h_done, sq_hi_done, sq_done, ss_used = (sem(n) for n in (
            "h_hi_done", "h_done", "sq_hi_done", "sq_done", "ss_used"))
        rms_done, rstd_done, init_done = (sem(n) for n in (
            "rms_done", "rstd_done", "init_done"))
        x_loaded, gain_loaded, mask_loaded, small_loaded, s0a_loaded, s0b_loaded = (sem(n) for n in (
            "x_loaded", "gain_loaded", "mask_loaded", "small_loaded", "s0a_loaded", "s0b_loaded"))
        states_out, y_out, y_stored = (sem(n) for n in (
            "states_out", "y_out", "y_stored"))
        pad_done, conv_step, conv_done, kqv_done = (sem(n) for n in (
            "pad_done", "conv_step", "conv_done", "kqv_done"))
        wba_hi_done, wba_done, lg_done, lg_scaled, logit_done, kq_sq_done, kq_sum_done = (sem(n) for n in (
            "wba_hi_done", "wba_done", "lg_done", "lg_scaled", "logit_done", "kq_sq_done", "kq_sum_done"))
        tok_d, tok_a, gsum_done, gexp_done = (sem(n) for n in (
            "tok_d", "tok_a", "gsum_done", "gexp_done"))
        gelu_done, ri_done, lru_a, lru_d, silu_z_done = (sem(n) for n in (
            "gelu_done", "ri_done", "lru_a", "lru_d", "silu_z_done"))
        grhs_done, dt_done, em_done, emm_done, kq_done = (sem(n) for n in (
            "grhs_done", "dt_done", "em_done", "emm_done", "kq_done"))
        kt_done, vt_done, kdec_done, vscaled_done, nt_done, attn_done = (sem(n) for n in (
            "kt_done", "vt_done", "kdec_done", "vscaled_done", "nt_done", "attn_done"))
        y0_tmp, y0_done, z0_done, z_init, nz_done, p_done, zp_done, z_upd, zt_done, y_upd = (sem(n) for n in (
            "y0_tmp", "y0_done", "z0_done", "z_init", "nz_done", "p_done", "zp_done", "z_upd", "zt_done", "y_upd"))
        ks_done, qs_done, qs_scaled, r_done, zr_done, vnew_done, av_done, kv_done, s_done = (sem(n) for n in (
            "ks_done", "qs_done", "qs_scaled", "r_done", "zr_done", "vnew_done", "av_done", "kv_done", "s_done"))
        o_done, o_sq_done, o_step, o_rms_done, on_done, ot_done, og_done = (sem(n) for n in (
            "o_done", "o_sq_done", "o_step", "o_rms_done", "on_done", "ot_done", "og_done"))
        seg_done, kst_done, kstt_done, vseg_done, segkv_done, seg_s_done = (sem(n) for n in (
            "seg_done", "kst_done", "kstt_done", "vseg_done", "segkv_done", "seg_s_done"))
        oy_hi_done, oy_done = (sem(n) for n in (
            "oy_hi_done", "oy_done"))
        taken = [sem("taken" + n) for n in "ABCD"]
        block = ctx.enter_context(nc.Block())

        def lv(c, k):
            return sum(len(LEVELS[i]) for i in range(c)) + k
        LV = lv(NCH, 0)

        def at(l, c, k, g):
            return l * (2 * LV) + (2 * lv(c, k) + g + 1)

        def bc(ap, n):
            return ap.unsqueeze(2).to_broadcast([ap.shape[0], ap.shape[1], n])

        def bh(ap, n):
            return ap.unsqueeze(1).to_broadcast([ap.shape[0], n, ap.shape[1]])

        def cols(pr):
            return pair[pr][:, :, 0:HALF]

        def tiles(ap):
            return ap.rearrange("p (a t) -> p a t", a=2)

        def seq(ap, n=SEQS):
            return ap.rearrange("p (b t) -> p b t", b=n)

        def samples(buf, first, n):
            return seq(buf[:, SAMP0:PAD])[:, :, first:first + n]

        def xc(c):
            return s0a[:, :, :, :].rearrange("p h s d -> p (h s d)")[:, (c % 3) * T:(c % 3 + 1) * T]

        def head(t, n, m):
            return t[0:n, :, 0:m]

        def bank(b, n, m):
            return b[0:n, 0:H * m].rearrange("p (h m) -> p h m", h=H)

        def lower(ap, s):
            return ap.rearrange("p h (b t) -> p h b t", t=2 * s)[:, :, :, 0:s]

        def packed(b, n, s):
            return b[0:n, 0:H * n // 2].rearrange("p (h b t) -> p h b t", h=H, t=s)

        def tok_e(c, n, after):
            if c == 0:
                return e_gs[0:n, after * H:(after + 1) * H]
            if c == NCH - 1:
                return e_gt[0:n, after * H:(after + 1) * H]
            return e_g[0:n, after * 16 + (c - 1) * H:after * 16 + c * H]

        def seg_state(h, s):
            return (s0a if h < 2 else s0b)[:, h % 2, s, :]

        PARTS = ((P, slice(1, 5)), (CH[0], slice(0, 1)), (CH[5], slice(5, 6)))

        @block.sync
        def _(eng):
            for k in range(KT):
                eng.dma_start(x[:, k, :], I["xT"][k]).then_inc(x_loaded, 16)
            eng.sem_inc(w_lo_done, 2)

            def load(u, pairs, src, at, n):
                with eng.Fori(0, pairs) as it:
                    for s in range(2):
                        eng.wait_ge(w_lo_done, u + it * 2 + (s + 1))
                        eng.dma_start(w_raw[:, s, 0:n], src[at + it * 2 + s]).then_inc(w_loaded[s], 16)

            def ffn(l, f):
                u = l * U_LAYER + B_FFN[f]
                load(u, FA, I["wgu"], l * (4 * FT) + f * 2 * FT, KT * P)
                load(u + 2 * FA, KT // 2, I["wda"], l * (2 * KT) + f * KT, FA * P)
                load(u + (2 * FA + KT), FB, I["wgu"], l * (4 * FT) + (f * 2 * FT + 2 * FA), KT * P)
                load(u + (2 * FT + KT), KT // 2, I["wdb"], l * (2 * KT) + f * KT, FB * P)

            with eng.Fori(0, DEPTH) as l:
                ffn(l, 0)
                load(l * U_LAYER + B_MIX, U_MIX // 2, I["win"], l * U_MIX, KT * P)
                load(l * U_LAYER + B_OUT, U_OUT // 2, I["wout"], l * U_OUT, KT * P)
                ffn(l, 1)
            for k in range(KT):
                eng.wait_ge(y_out, k + 1)
                eng.dma_start(O["y"][k], x[:, k, :]).then_inc(y_stored, 16)
            eng.wait_ge(y_stored, 16 * KT)
            eng.wait_ge(states_out, DEPTH * 16 * 5)

        @block.gpsimd
        def _(eng):
            count = eng.alloc_register("awaited_count")

            def apart(sem, value):
                eng.reg_mov(count, value)
                eng.wait_ge(mask_loaded, 16)
                eng.wait_ge(sem, count)

            eng.dma_start(gain0[:, :], I["gain0"]).then_inc(gain_loaded, 16)
            eng.dma_start(mask[:, :, :], I["mask"]).then_inc(mask_loaded, 16)
            with eng.Fori(0, DEPTH) as l:
                eng.wait_ge(rstd_done, l * NORMS + 1)
                for dst, name in ((vec[:, :], "vec"), (w_ba[:, :], "wba"), (w_ri[:, :, :, :], "wri"),
                                  (conv_hist[:, :, :, :], "chist"), (lru_h0[:, :, :], "lru0")):
                    eng.dma_start(dst, I[name][l]).then_inc(small_loaded, 16)
                u = l * U_LAYER + B_MIX
                with eng.Fori(0, U_MIX // 2) as it:
                    for s in range(2):
                        eng.wait_ge(w_hi_done, u + it * 2 + (s + 1))
                        eng.tensor_tensor(w_lo[:, s, 0:KT * P], w_raw[:, s, 0:KT * P],
                                          w_hi[:, s, 0:KT * P].bitcast(F32), ALU.subtract).then_inc(w_lo_done, 1)
                apart(kq_sum_done, l + 1)
                eng.tensor_copy(after_r[:, 0, :], mask[:, M_GT, :])
                eng.tensor_copy(after_r[:, 1, :], mask[:, M_GTS, :])
                eng.wait_ge(tok_d, l * TOK_D + T_G)

                def spread(c):
                    n = CH[c]
                    if c:
                        eng.wait_ge(dt_done, l * NCH + c)
                    tri = bh(mask[0:n, M_TRIS if c == 0 else M_TRI, 0:n], H)
                    eng.tensor_tensor(head(gr_hi, n, n), tri, bc(g_hi[0:n, c, :].bitcast(F32), n), ALU.mult)
                    eng.tensor_tensor(head(gr_lo, n, n), tri, bc(g_lo[0:n, c, :], n), ALU.mult).then_inc(grhs_done, 1)

                spread(0)
                apart(lru_d, l * (4 * LRU_D) + 4 * LRU_D + 1)
                eng.dma_start(s0a[:, :, :, :], I["s0"][l * 2]).then_inc(s0a_loaded, 16)
                eng.dma_start(s0b, I["s0"][l * 2 + 1]).then_inc(s0b_loaded, 16)
                eng.dma_start(O["conv"][l], conv_new[:, :, :]).then_inc(states_out, 16)
                eng.dma_start(O["lru"][l], lru_new[:, :, :]).then_inc(states_out, 16)
                spread(1)
                spread(2)
                apart(seg_s_done, l * H + H)
                eng.dma_start(O["ds"][l * 2], s0a[:, :, :, :]).then_inc(states_out, 16)
                eng.dma_start(O["ds"][l * 2 + 1], s0b).then_inc(states_out, 16)
                for c in range(3, NCH):
                    spread(c)
                apart(s_done, l * NCH + NCH)
                eng.dma_start(O["dp"][l], s_p[:, :, :]).then_inc(states_out, 16)

        @block.scalar
        def _(eng):
            eng.sem_inc(unit_done, 2)
            eng.sem_inc(ss_used, 2)
            eng.sem_inc(kqv_done, 1)

            def split(u, s, n):
                eng.wait_ge(w_loaded[s], u * 8 + (16 - 8 * s))
                eng.wait_ge(unit_done, u + 1)
                eng.activation(w_hi[:, s, 0:n], w_raw[:, s, 0:n], ACT.Copy).then_inc(w_hi_done, 1)

            def new_x(m, s, gain, nsq):
                eng.wait_ge(ss_used, nsq + 1)
                eng.activation(sq[:, s, :], x[:, m, :], ACT.Square)
                eng.activation(sq_hi[:, s, :], x[:, m, :], ACT.Square).then_inc(sq_hi_done, 1)
                eng.activation(h_hi[:, m, :], x[:, m, :], ACT.Copy, scale=gain).then_inc(h_hi_done, 1)

            def root(norm):
                eng.wait_ge(ss_used, norm * KT + (KT + 2))
                eng.activation(tiles(rms[:, :]), cols(3), ACT.Sqrt, bias=eps[:, 0:1], scale=1.0 / D).then_inc(rms_done, 1)

            def gate_up(u, ab, tg, n, prev):
                def gate(use, s):
                    eng.wait_ge(taken[s], use + 2)
                    eng.activation(silu_s[:, s, :], gate_s[:, s, :], ACT.Silu).then_inc(silu_done, 1)

                def up(t, k, s):
                    eng.wait_ge(prod_done, t + 1)
                    eng.activation(mid_hi[:, k, :], prod[:, s, :], ACT.Copy).then_inc(mid_hi_done, 1)

                def turn(it, first):
                    v = u + it * 4
                    split(v, 0, KT * P)
                    prev(0) if first else gate(ab + it - 1, 1)
                    split(v + 1, 1, KT * P)
                    prev(1) if first else up(tg + it * 2 - 1, it * 2 - 1, 1)
                    split(v + 2, 0, KT * P)
                    gate(ab + it, 0)
                    split(v + 3, 1, KT * P)
                    up(tg + it * 2, it * 2, 0)
                turn(0, True)
                with eng.Fori(1, n // 2) as it:
                    turn(it, False)
                return lambda i: up(tg + (n - 1), n - 1, 1) if i else gate(ab + (n // 2 - 1), 1)

            def to_x(u, ab, n, norm, gain_col, prev):
                def evac(it, s):
                    if norm is not None:
                        m = it * 2 + s
                        eng.wait_ge(taken[s], ab + it + 2)
                        new_x(m, s, vec[:, bass.ds(gain_col + m, 1)], norm * KT + m)

                def turn(it, first):
                    for s in range(2):
                        split(u + it * 2 + s, s, n)
                        prev(s) if first else evac(it - 1, s)
                turn(0, True)
                with eng.Fori(1, KT // 2) as it:
                    turn(it, False)
                return lambda s: evac(KT // 2 - 1, s)

            def ffn(l, f, prev):
                u, ab, tg = l * U_LAYER + B_FFN[f], l * AB_LAYER + AB_FFN[f], l * (2 * FT) + f * FT
                t = gate_up(u, ab, tg, FA, prev)
                t = to_x(u + 2 * FA, ab + FA // 2, FA * P, None, 0, t)
                t = gate_up(u + (2 * FA + KT), ab + (FA // 2 + 4), tg + FA, FB, t)
                eng.wait_ge(small_loaded, l * (16 * SMALL) + 16 * SMALL)
                return to_x(u + (2 * FT + KT), ab + (FT // 2 + 4), FB * P, l * NORMS + (1 + 2 * f), (V_NM, V_NN)[f], t)

            def mix(l, prev):
                u, ab = l * U_LAYER + B_MIX, l * AB_LAYER + AB_MIX
                la, ld = l * (4 * LRU_A), l * (4 * LRU_D)

                def evac_kqv(j):
                    eng.wait_ge(conv_done, l * 16 + j + 1)
                    eng.activation(kqv[:, j, 0:TP], acc[:, 0:TP], ACT.Silu)
                    eng.activation(seq(kqv[:, j, TP:T]),
                                   samples(acc, 0, SLEN), ACT.Silu).then_inc(kqv_done, 1)

                def evac_gate(c):
                    eng.wait_ge(taken[1], ab + (6 + c + 1) + 1)
                    eng.activation(y_s[:, c, :], y_s[:, c, :], ACT.Gelu_apprx_tanh).then_inc(gelu_done, 1)

                def evac_z(c):
                    eng.wait_ge(taken[c % 2], ab + (10 + c // 2 + 1) + 1)
                    eng.activation(z_s[:, c, :], z_s[:, c, :], ACT.Silu).then_inc(silu_z_done, 1)

                def w_ba_high():
                    eng.activation(w_ba_hi[:, :], w_ba[:, :], ACT.Copy).then_inc(wba_hi_done, 1)

                def squares():
                    eng.wait_ge(kqv_done, l * 12 + 13)
                    for j in range(8):
                        eng.activation((sq_k if j < 4 else sq_q)[:, j % 4, :], kqv[:, 4 + j, :], ACT.Square).then_inc(kq_sq_done, 1)

                def tok1():
                    n = l * TOK_D
                    eng.wait_ge(tok_d, n + T_ABS)
                    eng.activation(sp["e"][:, :], sp["abs"][:, :], ACT.Exp, scale=-1.0)
                    eng.activation(ea[:, :], vec[:, V_ALOG:V_ALOG + H], ACT.Exp)
                    eng.activation(tok["beta"][:, :, :], logit[:, :, 0:4], ACT.Sigmoid).then_inc(tok_a, 1)

                def tok2():
                    eng.wait_ge(gsum_done, l + 1)
                    eng.activation(e_g[:, :], PD0[:, 0:32], ACT.Exp)
                    eng.activation(e_gs[0:CH[0], :], PD0[0:CH[0], 32:40], ACT.Exp)
                    eng.activation(e_gt[0:CH[5], :], PD0[0:CH[5], 40:48], ACT.Exp)
                    eng.activation(e_last[:, :], PD0[:, 48:48 + SUM_G], ACT.Exp).then_inc(gexp_done, 1)
                    eng.wait_ge(tok_d, l * TOK_D + T_SS)
                    eng.activation(tok["nk"][:, :, :], kq_ss[:, :, 0:4], ACT.Sqrt, bias=eps[:, 0:1])
                    eng.activation(tok["nq"][:, :, :], kq_ss[:, :, 4:8], ACT.Sqrt, bias=eps[:, 1:2], scale=float(DK)).then_inc(tok_a, 1)

                def lru_1(c):
                    eng.wait_ge(ri_done, l * 4 + (c + 1))
                    eng.wait_ge(lru_d, ld + c * LRU_D + 1)
                    eng.activation(tiles(lt[:, 1, :]), cols(2), ACT.Sigmoid, bias=vec[:, V_BR + c:V_BR + c + 1]).then_inc(lru_a, 1)
                    eng.activation(tiles(lt[:, 2, :]), cols(3), ACT.Sigmoid, bias=vec[:, V_BI + c:V_BI + c + 1]).then_inc(lru_a, 1)
                    eng.wait_ge(lru_a, la + (c * LRU_A + 1))
                    eng.activation(lt[:, 3, :], lt[:, 1, :], ACT.Tanh, scale=lam8[:, c:c + 1]).then_inc(lru_a, 1)
                    eng.activation(lt[:, 1, :], lt[:, 1, :], ACT.Exp, scale=lam8[:, 4 + c:5 + c]).then_inc(lru_a, 1)

                def lru_2(c):
                    eng.wait_ge(lru_d, ld + (c * LRU_D + 3) + 1)
                    eng.activation(lt[:, 0, :], lt[:, 3, :], ACT.Sqrt).then_inc(lru_a, 1)

                def turn(it, first):
                    for s in range(2):
                        split(u + it * 2 + s, s, KT * P)
                        prev(s) if first else evac_kqv(it * 2 - 3 + s)
                turn(0, True)
                root(l * NORMS + 1)
                w_ba_high()
                split(u + 2, 0, KT * P)
                split(u + 3, 1, KT * P)
                evac_kqv(0)
                with eng.Fori(2, 6) as it:
                    turn(it, False)
                for n in range(12, U_MIX + 2):
                    if n < U_MIX:
                        split(u + n, n % 2, KT * P)
                    if n < 15:
                        evac_kqv(n - 3)
                    elif n < 22:
                        if n % 2:
                            evac_gate((n - 14) // 2)
                    else:
                        evac_z(n - 22)
                    if n == 14:
                        squares()
                    if n == 15:
                        tok1()
                    if n == 17:
                        tok2()
                    if n >= 18:
                        (lru_2 if n % 2 else lru_1)((n - 18) // 2)
                for c in range(NCH + 1):
                    if c < NCH:
                        decays(l, c)
                    if c:
                        scale_qs(l, c - 1)
                    if c < NCH:
                        first_z(l, c)
                        new_y(l, c, 0)
                    if c:
                        o_squares(l, c - 1)
                    if c < NCH:
                        new_y(l, c, 1)
                    if c:
                        o_root(l, c - 1)
                    if c < NCH:
                        for k in range(2, len(LEVELS[c])):
                            new_y(l, c, k)
                eng.wait_ge(og_done, l * NCH + NCH)
                for j in range(KT):
                    eng.activation(mid_hi[:, j, :], kqv[:, 8 + j, :] if j < 4 else y_s[:, j - 4, :], ACT.Copy).then_inc(oy_hi_done, 1)

            def decays(l, c):
                n = CH[c]
                eng.wait_ge(dt_done, l * NCH + c + 1)
                eng.activation(head(em, n, n), bank(PD0, n, n), ACT.Exp).then_inc(em_done, 1)

            def first_z(l, c):
                n = CH[c]
                eng.wait_ge(z0_done, l * NCH + c + 1)
                eng.activation(packed(z_c, n, LEVELS[c][0]), lower(bank(PC0, n, n), LEVELS[c][0]), ACT.Copy)
                eng.activation(head(z_m, n, n), bank(PC0, n, n), ACT.Copy).then_inc(z_init, 1)

            def new_y(l, c, k):
                n = CH[c]
                for g in range(2):
                    hs = slice(2 * g, 2 * g + 2)
                    eng.wait_ge(zt_done, at(l, c, k, g))
                    eng.activation(y_c[c % 2][0:n, hs, 0:n], bank((PD0, PD1)[g], n, n)[:, hs], ACT.Copy).then_inc(y_upd, 1)

            def scale_qs(l, c):
                n = CH[c]
                if c == 0:
                    for h in range(H):
                        eng.wait_ge(seg_done, l * H + (h + 1))
                        if h >= 2:
                            eng.wait_ge(kstt_done, l * H + (h - 1))
                        eng.activation(ks_t[:, h % 2, :, :], (PB0, PB1)[h % 2][:, 0:2 * n].rearrange("p (k t) -> p k t", k=2), ACT.Copy).then_inc(kst_done, 1)
                    eng.wait_ge(kstt_done, l * H + H)
                else:
                    eng.wait_ge(qs_done, l * (NCH - 1) + c)
                for h in range(H):
                    ins = eng.activation(qs[0:n, h, :], PA1[0:n, h * P:(h + 1) * P], ACT.Copy, scale=tok_e(c, n, 0)[:, h:h + 1])
                ins.then_inc(qs_scaled, 1)

            def o_squares(l, c):
                n = CH[c]
                eng.wait_ge(o_done, l * NCH + c + 1)
                for h in range(H):
                    ins = eng.activation(qs[0:n, h, :], o_s[0:n, h, :], ACT.Square, accum_out=o_ss[0:n, h:h + 1])
                ins.then_inc(o_sq_done, 1)

            def o_root(l, c):
                n = CH[c]
                eng.wait_ge(o_step, l * (3 * NCH) + (3 * c + 1))
                eng.activation(o_rms[0:n, :], o_ms[0:n, :], ACT.Sqrt, bias=eps[0:n, 0:1]).then_inc(o_rms_done, 1)

            eng.wait_ge(gain_loaded, 16)
            eng.wait_ge(x_loaded, 16 * KT)
            eng.wait_ge(init_done, 1)
            for k in range(KT):
                new_x(k, k % 2, gain0[:, k:k + 1], k)
            root(0)
            with eng.Fori(0, DEPTH) as l:
                t = ffn(l, 0, lambda s: None)
                mix(l, t)
                t = to_x(l * U_LAYER + B_OUT, l * AB_LAYER + AB_OUT, KT * P, l * NORMS + 2, V_N2, lambda s: None)
                t(0)
                t(1)
                root(l * NORMS + 2)
                eng.wait_ge(states_out, l * (16 * 5) + 16 * 5)
                t = ffn(l, 1, lambda s: None)
                t(0)
                t(1)
                root(l * NORMS + 3)

        @block.vector
        def _(eng):
            def split(u, s, n):
                eng.wait_ge(w_hi_done, u + 1)
                eng.tensor_tensor(w_lo[:, s, 0:n], w_raw[:, s, 0:n], w_hi[:, s, 0:n].bitcast(F32), ALU.subtract).then_inc(w_lo_done, 1)

            def h_low(m, gain, nh):
                eng.wait_ge(h_hi_done, nh + 1)
                eng.scalar_tensor_tensor(h_lo[:, m, :], x[:, m, :], gain, h_hi[:, m, :].bitcast(F32), ALU.mult, ALU.subtract).then_inc(h_done, 1)

            def new_x(m, s, gain, nsq):
                eng.wait_ge(sq_hi_done, nsq + 1)
                eng.tensor_tensor(sq_lo[:, s, :], sq[:, s, :], sq_hi[:, s, :].bitcast(F32), ALU.subtract).then_inc(sq_done, 1)
                h_low(m, gain, nsq)

            def root(norm):
                eng.wait_ge(rms_done, norm + 1)
                eng.reciprocal(rstd[:, :], rms[:, :]).then_inc(rstd_done, 1)
                eng.wait_ge(rstd_done, norm + 1)

            def gate_up(u, ab, cd, tg, n, prev):
                def gate(v, s):
                    eng.wait_ge(unit_done, v + 3)
                    eng.tensor_tensor(tiles(gate_s[:, s, :]), cols(s), tiles(rstd[:, :]), ALU.mult).then_inc(taken[s], 1)

                def up(v, use, t, k, s):
                    eng.wait_ge(unit_done, v + 3)
                    eng.tensor_tensor(tiles(up_s[:, :]), cols(2 + s), tiles(rstd[:, :]), ALU.mult).then_inc(taken[2 + s], 1)
                    eng.wait_ge(taken[2 + s], use + 2)
                    eng.wait_ge(silu_done, t + 1)
                    eng.tensor_tensor(prod[:, s, :], silu_s[:, s, :], up_s[:, :], ALU.mult).then_inc(prod_done, 1)
                    eng.wait_ge(mid_hi_done, t + 1)
                    eng.tensor_tensor(mid_lo[:, k, :], prod[:, s, :], mid_hi[:, k, :].bitcast(F32), ALU.subtract).then_inc(mid_done, 1)

                def turn(it, first):
                    v = u + it * 4
                    split(v, 0, KT * P)
                    prev(0) if first else gate(v - 2, 1)
                    split(v + 1, 1, KT * P)
                    prev(1) if first else up(v - 1, cd + it - 1, tg + it * 2 - 1, it * 2 - 1, 1)
                    split(v + 2, 0, KT * P)
                    gate(v, 0)
                    split(v + 3, 1, KT * P)
                    up(v + 1, cd + it, tg + it * 2, it * 2, 0)
                turn(0, True)
                with eng.Fori(1, n // 2) as it:
                    turn(it, False)
                return lambda i: up(u + (2 * n - 1), cd + (n // 2 - 1), tg + (n - 1), n - 1, 1) if i else gate(u + (2 * n - 2), 1)

            def to_x(u, ab, n, weight, norm, gain_col, prev):
                def evac(it, s):
                    m = it * 2 + s
                    eng.wait_ge(unit_done, u + m + 3)
                    eng.scalar_tensor_tensor(tiles(x[:, m, :]), cols(s), weight, tiles(x[:, m, :]), ALU.mult, ALU.add).then_inc(taken[s], 1)
                    if norm is not None:
                        eng.wait_ge(taken[s], ab + it + 2)
                        new_x(m, s, vec[:, bass.ds(gain_col + m, 1)], norm * KT + m)

                def turn(it, first):
                    for s in range(2):
                        split(u + it * 2 + s, s, n)
                        prev(s) if first else evac(it - 1, s)
                turn(0, True)
                with eng.Fori(1, KT // 2) as it:
                    turn(it, False)
                return lambda s: evac(KT // 2 - 1, s)

            def ffn(l, f, prev):
                u, ab, cd, tg = l * U_LAYER + B_FFN[f], l * AB_LAYER + AB_FFN[f], l * CD_LAYER + CD_FFN[f], l * (2 * FT) + f * FT
                t = gate_up(u, ab, cd, tg, FA, prev)
                t = to_x(u + 2 * FA, ab + FA // 2, FA * P, 0.5, None, 0, t)
                t = gate_up(u + (2 * FA + KT), ab + (FA // 2 + 4), cd + FA // 2, tg + FA, FB, t)
                eng.wait_ge(taken[1], ab + (FA // 2 + 4) + 1)
                eng.wait_ge(small_loaded, l * (16 * SMALL) + 16 * SMALL)
                return to_x(u + (2 * FT + KT), ab + (FT // 2 + 4), FB * P, 0.5, l * NORMS + (1 + 2 * f), (V_NM, V_NN)[f], t)

            def mix(l, prev):
                u, ab = l * U_LAYER + B_MIX, l * AB_LAYER + AB_MIX
                la, ld = l * (4 * LRU_A), l * (4 * LRU_D)

                def evac_conv(s, m, use, j, out=None):
                    eng.wait_ge(unit_done, u + m + 3)
                    eng.tensor_tensor(cp[:, s, 3:3 + HALF], pair[s][:, 0, 0:HALF], rstd[:, 0:HALF], ALU.mult)
                    eng.tensor_tensor(cp[:, s, 3 + HALF:SAMP0], pair[s][:, 1, 0:TP - HALF], rstd[:, HALF:TP], ALU.mult)
                    eng.tensor_copy(samples(cp[:, s, :], 0, 3), conv_hist[:, j, :, :])
                    eng.tensor_tensor(samples(cp[:, s, :], 3, SLEN),
                                      pair[s][:, 1, TP - HALF:HALF].rearrange("p (b t) -> p b t", b=SEQS),
                                      seq(rstd[:, TP:T]), ALU.mult).then_inc(taken[s], 1)
                    eng.wait_ge(taken[s], use + 2)
                    eng.tensor_copy(conv_new[:, j, 0:3], cp[:, s, TP:TP + 3])
                    eng.tensor_copy(conv_new[:, j, 3:27].rearrange("p (b t) -> p b t", b=SEQS), samples(cp[:, s, :], SLEN, 3))
                    cs = l * (16 * 3) + j * 3
                    w = lambda i: vec[:, bass.ds(V_CQ + j * TAPS + i, 1)]
                    if out is None:
                        eng.wait_ge(pad_done, l + 1)
                        eng.wait_ge(kqv_done, l * 12 + j + 1)
                        eng.tensor_scalar(acc[:, 0:CONV], cp[:, s, 0:CONV], w(0), None, ALU.mult).then_inc(conv_step, 1)
                    else:
                        eng.wait_ge(kqv_done, l * 12 + 13)
                        eng.tensor_scalar(acc[:, 0:CONV], cp[:, s, 0:CONV], w(0), vec[:, V_CB + j - 12:V_CB + j - 11], ALU.mult, ALU.add).then_inc(conv_step, 1)
                    for i in (1, 2):
                        eng.wait_ge(conv_step, cs + i)
                        eng.scalar_tensor_tensor(acc[:, 0:CONV], cp[:, s, i:i + CONV], w(i), acc[:, 0:CONV], ALU.mult, ALU.add).then_inc(conv_step, 1)
                    eng.wait_ge(conv_step, cs + 3)
                    if out is None:
                        eng.scalar_tensor_tensor(acc[:, 0:CONV], cp[:, s, 3:3 + CONV], w(3), acc[:, 0:CONV], ALU.mult, ALU.add).then_inc(conv_done, 1)
                    else:
                        eng.scalar_tensor_tensor(out[:, 0:TP], cp[:, s, 3:3 + TP], w(3), acc[:, 0:TP], ALU.mult, ALU.add)
                        eng.scalar_tensor_tensor(seq(out[:, TP:T]), samples(cp[:, s, :], 3, SLEN), w(3),
                                                 samples(acc, 0, SLEN), ALU.mult, ALU.add).then_inc(conv_done, 1)

                def scaled(s, m, dst):
                    eng.wait_ge(unit_done, u + m + 3)
                    eng.tensor_tensor(tiles(dst), cols(s), tiles(rstd[:, :]), ALU.mult).then_inc(taken[s], 1)

                count = [0]

                def step(ins):
                    count[0] += 1
                    ins.then_inc(tok_d, 1)
                    eng.wait_ge(tok_d, l * TOK_D + count[0])

                def tok1a():
                    lp = PC0[:, 0:NCH * 8].rearrange("p (c j) -> p c j", c=NCH)
                    eng.wait_ge(logit_done, l + 1)
                    for n, cs in PARTS:
                        ins = eng.tensor_copy(logit[0:n, cs, :], lp[0:n, cs, :])
                    step(ins)
                    y, a = sp["y"], sp["abs"]
                    eng.tensor_tensor(y[:, 0:NCH * H].rearrange("p (c h) -> p c h", c=NCH), logit[:, :, 4:8], bh(vec[:, V_DT:V_DT + H], NCH), ALU.add)
                    step(eng.tensor_scalar(y[:, NCH * H:SP_N], vec[:, V_LAM:V_LAM + 4], -1.0, None, ALU.mult))
                    step(eng.scalar_tensor_tensor(a[:, :], y[:, :], -1.0, y[:, :], ALU.mult, ALU.max))
                    assert count[0] == T_ABS

                def tok1b():
                    y, e, z, z2, p, out = (sp[n] for n in ("y", "e", "z", "z2", "p", "out"))
                    den = out
                    eng.wait_ge(tok_a, l * 2 + 1)
                    step(eng.tensor_scalar(den[:, :], e[:, :], 2.0, None, ALU.add))
                    step(eng.reciprocal(den[:, :], den[:, :]))
                    step(eng.tensor_tensor(z[:, :], e[:, :], den[:, :], ALU.mult))
                    step(eng.tensor_tensor(z2[:, :], z[:, :], z[:, :], ALU.mult))
                    step(eng.tensor_scalar(p[:, :], z2[:, :], ATANH[0], None, ALU.mult))
                    for k in ATANH[1:]:
                        step(eng.scalar_tensor_tensor(p[:, :], p[:, :], k, z2[:, :], ALU.add, ALU.mult))
                    step(eng.scalar_tensor_tensor(p[:, :], p[:, :], 1.0, z[:, :], ALU.add, ALU.mult))
                    step(eng.tensor_scalar(p[:, :], p[:, :], 2.0, None, ALU.mult))
                    step(eng.scalar_tensor_tensor(out[:, :], y[:, :], 0.0, p[:, :], ALU.max, ALU.add))
                    g = tok["g"]
                    eng.tensor_scalar(lam8[:, 0:4], out[:, NCH * H:SP_N], 8.0, None, ALU.mult)
                    eng.tensor_scalar(lam8[:, 4:8], out[:, NCH * H:SP_N], -8.0, None, ALU.mult)
                    step(eng.scalar_tensor_tensor(g[:, :, :], out[:, 0:NCH * H].rearrange("p (c h) -> p c h", c=NCH), -1.0, bh(ea[:, :], NCH), ALU.mult, ALU.mult))
                    step(eng.tensor_copy(g_hi[:, :, :], g[:, :, :]))
                    eng.tensor_tensor(g_lo[:, :, :], g[:, :, :], g_hi[:, :, :].bitcast(F32), ALU.subtract)
                    step(eng.tensor_tensor(g_seg[0:TS, :, :], bc(mask[0:TS, M_GTS, IND], H), bh(g[0:TS, 0, :], SEGS), ALU.mult))
                    assert count[0] == T_G

                def tok2():
                    kp = PC1[:, 0:NCH * 8].rearrange("p (c j) -> p c j", c=NCH)
                    eng.wait_ge(kq_sum_done, l + 1)
                    for n, cs in PARTS:
                        ins = eng.tensor_copy(kq_ss[0:n, cs, :], kp[0:n, cs, :])
                    step(ins)
                    assert count[0] == T_SS
                    eng.wait_ge(tok_a, l * 2 + 2)
                    t = lambda n: tok[n][:, :, :]
                    eng.reciprocal(t("rq"), t("nq"))
                    step(eng.reciprocal(t("rk"), t("nk")))
                    eng.tensor_tensor(t("rq2"), t("rq"), t("rq"), ALU.mult)
                    step(eng.tensor_tensor(t("bk2"), t("rk"), t("rk"), ALU.mult))
                    step(eng.tensor_tensor(t("bk2"), t("bk2"), t("beta"), ALU.mult))
                    step(eng.tensor_scalar(t("nb"), t("bk2"), -1.0, None, ALU.mult))
                    assert count[0] == TOK_D

                def lru_1(c):
                    n = [ld + c * LRU_D]
                    eng.wait_ge(lru_a, la + (c * LRU_A + 4))
                    eng.tensor_tensor(lt[:, 2, :], lt[:, 2, :], xc(c), ALU.mult).then_inc(lru_d, 1)
                    eng.tensor_tensor(lt[:, 0, :], lt[:, 1, :], lt[:, 1, :], ALU.mult).then_inc(lru_d, 1)
                    eng.wait_ge(lru_d, n[0] + 3)
                    eng.scalar_tensor_tensor(lt[:, 3, :], lt[:, 0, :], 1.0, lt[:, 3, :], ALU.add, ALU.mult).then_inc(lru_d, 1)

                def lru_2(c):
                    base = ld + c * LRU_D
                    start = lambda i: seq(lt[:, i, TP:T])[:, :, 0]
                    eng.wait_ge(lru_a, la + (c * LRU_A + 5))
                    eng.tensor_tensor(lt[:, 2, :], lt[:, 2, :], lt[:, 0, :], ALU.mult).then_inc(lru_d, 1)
                    eng.tensor_tensor(h_start[:, :], start(1), lru_h0[:, c, :], ALU.mult).then_inc(lru_d, 1)
                    eng.wait_ge(lru_d, base + 6)
                    eng.tensor_tensor(start(2), start(2), h_start[:, :], ALU.add).then_inc(lru_d, 1)
                    eng.memset(start(1), 0.0).then_inc(lru_d, 1)
                    eng.wait_ge(lru_d, base + 8)
                    eng.tensor_tensor_scan(lt[:, 3, :], lt[:, 1, :], lt[:, 2, :], 0.0, ALU.mult, ALU.add).then_inc(lru_d, 1)
                    eng.wait_ge(lru_d, base + 9)
                    eng.tensor_copy(lru_new[:, c, 0:1], lt[:, 3, TP - 1:TP]).then_inc(lru_d, 1)
                    eng.tensor_copy(lru_new[:, c, 1:9], seq(lt[:, 3, TP:T])[:, :, SLEN - 1]).then_inc(lru_d, 1)
                    eng.wait_ge(gelu_done, l * 4 + (c + 1))
                    eng.tensor_tensor(y_s[:, c, :], y_s[:, c, :], lt[:, 3, :], ALU.mult).then_inc(lru_d, 1)

                prev(0)
                prev(1)
                root(l * NORMS + 1)
                eng.memset(cp[:, :, 0:3], 0.0).then_inc(pad_done, 1)
                eng.wait_ge(wba_hi_done, l + 1)
                eng.tensor_tensor(w_ba_lo[:, :], w_ba[:, :], w_ba_hi[:, :].bitcast(F32), ALU.subtract).then_inc(wba_done, 1)
                with eng.Fori(0, 6) as it:
                    for s in range(2):
                        evac_conv(s, it * 2 + s, ab + it, it * 2 + s)
                eng.wait_ge(lg_done, l + 1)
                eng.tensor_tensor(tiles(z_s[0:8, 0, :]), pair[2][0:8, :, 0:HALF], tiles(rstd[0:8, :]), ALU.mult).then_inc(lg_scaled, 1)
                for m in range(12, U_MIX):
                    use = ab + m // 2
                    if m < 20:
                        if m % 2 == 0:
                            c = (m - 12) // 2
                            if c == 3:
                                eng.wait_ge(ri_done, l * 4 + 1)
                            evac_conv(0, m, use, 12 + c, xc(c))
                        else:
                            scaled(1, m, y_s[:, (m - 12) // 2, :])
                    else:
                        if m == 20:
                            eng.wait_ge(kq_sum_done, l + 1)
                        scaled(m % 2, m, z_s[:, m - 20, :])
                    if m == 12:
                        tok1a()
                    if m == 13:
                        tok1b()
                    if m == 15:
                        tok2()
                    if m >= 16:
                        (lru_2 if m % 2 else lru_1)((m - 16) // 2)
                eng.memset(s_p[:, :, :], 0.0).then_inc(s_done, 1)
                eng.wait_ge(silu_z_done, l * 4 + 4)
                for c in range(NCH + 1):
                    new, old = c < NCH, c > 0
                    if new:
                        decays(l, c)
                        start(l, c)
                    if old:
                        residual(l, c - 1)
                    if new:
                        scale_v(l, c)
                    if old:
                        new_v(l, c - 1)
                    level(l, c, 0)
                    if old:
                        update(l, c - 1)
                    level(l, c, 1)
                    if old:
                        o_mean(l, c - 1)
                    level(l, c, 2)
                    if old:
                        o_norm(l, c - 1)
                    level(l, c, 3)
                    if old:
                        o_gate(l, c - 1)
                    level(l, c, 4)
                    level(l, c, 5)
                for j in range(KT):
                    eng.wait_ge(oy_hi_done, l * KT + (j + 1))
                    eng.tensor_tensor(mid_lo[:, j, :], kqv[:, 8 + j, :] if j < 4 else y_s[:, j - 4, :],
                                      mid_hi[:, j, :].bitcast(F32), ALU.subtract).then_inc(oy_done, 1)

            def tk(name, c):
                return tok[name][0:CH[c], c, :]

            def decays(l, c):
                n, lc = CH[c], l * NCH + c
                tri = bh(mask[0:n, M_TRIS if c == 0 else M_TRI, 0:n], H)
                eng.wait_ge(em_done, lc + 1)
                eng.tensor_tensor(head(em, n, n), head(em, n, n), tri, ALU.mult).then_inc(emm_done, 1)

            def start(l, c):
                n, lc, y = CH[c], l * NCH + c, y_c[c % 2]
                eng.wait_ge(emm_done, lc + 1)
                eng.wait_ge(kq_done, lc + 1)
                for h in range(H):
                    ins = eng.scalar_tensor_tensor(nt[0:n, h, 0:n], PC0[0:n, h * n:(h + 1) * n], tok["bk2"][0:n, c, h:h + 1],
                                                   em[0:n, h, 0:n], ALU.mult, ALU.mult)
                ins.then_inc(nt_done, 1)
                eng.wait_ge(nt_done, lc + 1)
                eng.tensor_tensor(head(y, n, n), head(nt, n, n), bh(mask[0:n, M_L1T, 0:n], H), ALU.mult).then_inc(y0_tmp, 1)
                eng.wait_ge(y0_tmp, lc + 1)
                eng.tensor_tensor(head(y, n, n), bh(mask[0:n, M_ID, 0:n], H), head(y, n, n), ALU.subtract).then_inc(y0_done, 1)
                eng.tensor_tensor(head(attn[c % 2], n, n), bank(PC1, n, n), head(em, n, n), ALU.mult).then_inc(attn_done, 1)
                eng.wait_ge(kt_done, lc + 1)
                eng.tensor_tensor(kdec[c % 2][0:n, :, :], bank(PD1, n, P), bc(tok_e(c, n, 1), P), ALU.mult).then_inc(kdec_done, 1)

            def scale_v(l, c):
                n, lc = CH[c], l * NCH + c
                eng.wait_ge(vt_done, lc + 1)
                eng.tensor_tensor(vn_s[c % 2][0:n, :, :], bank(PD0, n, P), bc(tk("nk", c), P), ALU.mult).then_inc(vscaled_done, 1)

            def level(l, c, k):
                if c == NCH or k >= len(LEVELS[c]):
                    return
                n, s = CH[c], LEVELS[c][k]
                m = mask[0:n, LEVEL_MASK[s], 0:n].rearrange("p (b t) -> p b t", t=2 * s)[:, :, 0:s]
                for g in range(2):
                    hs = slice(2 * g, 2 * g + 2)
                    eng.wait_ge(nz_done, at(l, c, k, g))
                    eng.tensor_tensor(packed(p_c, n, s)[:, hs], packed((PC0, PC1)[g], n, s)[:, hs],
                                      m.unsqueeze(1).to_broadcast([n, 2, n // (2 * s), s]), ALU.mult).then_inc(p_done, 1)
                for g in range(2):
                    hs = slice(2 * g, 2 * g + 2)
                    if k == 0:
                        eng.wait_ge(z_init, l * NCH + c + 1)
                    else:
                        eng.wait_ge(z_upd, at(l, c, k - 1, g))
                    eng.wait_ge(zp_done, at(l, c, k, g))
                    z = lower(head(z_m, n, n), s)[:, hs]
                    eng.tensor_tensor(z, z, packed((PC0, PC1)[g], n, s)[:, hs], ALU.subtract).then_inc(z_upd, 1)

            def residual(l, c):
                n, lc = CH[c], l * NCH + c
                if c == 0:
                    eng.wait_ge(kstt_done, l * H + H)
                else:
                    eng.wait_ge(ks_done, l * (NCH - 1) + c)
                eng.wait_ge(vscaled_done, lc + 1)
                for h in range(H):
                    ins = eng.scalar_tensor_tensor(r_s[0:n, h, :], PA0[0:n, h * P:(h + 1) * P], tok_e(c, n, 0)[:, h:h + 1],
                                                   vn_s[c % 2][0:n, h, :], ALU.mult, ALU.subtract)
                ins.then_inc(r_done, 1)

            def new_v(l, c):
                n, lc = CH[c], l * NCH + c
                eng.wait_ge(zr_done, lc + 1)
                eng.tensor_tensor(v_new[0:n, :, :], bank(PB0, n, P), bc(tk("nb", c), P), ALU.mult).then_inc(vnew_done, 1)

            def update(l, c):
                n, lc = CH[c], l * NCH + c
                if c:
                    eng.wait_ge(kv_done, l * (NCH - 1) + c)
                    for h in range(H):
                        at = (c - 1) * H + h
                        ins = eng.scalar_tensor_tensor(s_p[:, h, :], s_p[:, h, :], e_last[:, at:at + 1],
                                                       PB1[:, h * P:(h + 1) * P], ALU.mult, ALU.add)
                    ins.then_inc(s_done, 1)
                    eng.wait_ge(s_done, l * NCH + (c + 1))
                eng.wait_ge(av_done, lc + 1)
                eng.wait_ge(qs_scaled, lc + 1)
                eng.tensor_tensor(o_s[0:n, :, :], qs[0:n, :, :], bank(PA0, n, P), ALU.add).then_inc(o_done, 1)
                if c == 0:
                    eng.wait_ge(vnew_done, lc + 1)
                    segments(l, 0)

            def o_mean(l, c):
                n = CH[c]
                eng.wait_ge(o_sq_done, l * NCH + c + 1)
                eng.scalar_tensor_tensor(o_ms[0:n, :], o_ss[0:n, :], 1.0 / DK, tk("rq2", c), ALU.mult, ALU.mult).then_inc(o_step, 1)
                if c == 0:
                    segments(l, 1)

            def o_norm(l, c):
                n, lc, st = CH[c], l * NCH + c, l * (3 * NCH) + 3 * c
                eng.wait_ge(o_rms_done, lc + 1)
                eng.reciprocal(o_rec[0:n, :], o_rms[0:n, :]).then_inc(o_step, 1)
                eng.wait_ge(o_step, st + 2)
                eng.tensor_tensor(o_fac[0:n, :], o_rec[0:n, :], tk("rq", c), ALU.mult).then_inc(o_step, 1)
                eng.wait_ge(o_step, st + 3)
                eng.tensor_tensor(o_s[0:n, :, :], o_s[0:n, :, :], bc(o_fac[0:n, :], P), ALU.mult).then_inc(on_done, 1)
                if c == 0:
                    segments(l, 2)

            def o_gate(l, c):
                n, t0 = CH[c], T0[c]
                eng.wait_ge(ot_done, l * NCH + c + 1)
                eng.scalar_tensor_tensor(kqv[:, 8:12, t0:t0 + n], bank(PA1, P, n), vec[:, V_ON:V_ON + 1],
                                         z_s[:, :, t0:t0 + n], ALU.mult, ALU.mult).then_inc(og_done, 1)
                if c == 0:
                    segments(l, 3)

            def segments(l, h):
                n, i = CH[0], l * H + (h + 1)
                eng.tensor_tensor(vseg[0:n, :, :], bh(v_new[0:n, h, :], SEGS), bc(mask[0:n, M_GTS, IND], P), ALU.mult).then_inc(vseg_done, 1)
                eng.wait_ge(segkv_done, i)
                for s in range(SEGS):
                    at = (NCH - 1) * H + s * H + h
                    ins = eng.scalar_tensor_tensor(seg_state(h, s), seg_state(h, s), e_last[:, at:at + 1],
                                                   (PB0, PB1)[s // 4][:, (s % 4) * P:(s % 4 + 1) * P], ALU.mult, ALU.add)
                ins.then_inc(seg_s_done, 1)

            for t in taken:
                eng.sem_inc(t, 1)
            eng.sem_inc(lru_d, 1)
            eng.memset(eps[:, 0:1], EPS)
            eng.memset(eps[:, 1:2], EPS * DK)
            eng.memset(logit[:, :, :], 0.0)
            eng.memset(kq_ss[:, :, :], 0.0).then_inc(init_done, 1)
            eng.wait_ge(mask_loaded, 16)
            eng.tensor_copy(ones_r[:, :], mask[:, M_ONE, :]).then_inc(init_done, 1)
            eng.wait_ge(x_loaded, 16 * KT)
            eng.wait_ge(gain_loaded, 16)
            for k in range(KT):
                new_x(k, k % 2, gain0[:, k:k + 1], k)
            root(0)
            with eng.Fori(0, DEPTH) as l:
                t = ffn(l, 0, lambda s: None)
                mix(l, t)
                t = to_x(l * U_LAYER + B_OUT, l * AB_LAYER + AB_OUT, KT * P, 1.0, l * NORMS + 2, V_N2, lambda s: None)
                t(0)
                t(1)
                root(l * NORMS + 2)
                eng.wait_ge(states_out, l * (16 * 5) + 16 * 5)
                t = ffn(l, 1, lambda s: None)
                t(0)
                t(1)
                root(l * NORMS + 3)
            for k in range(KT):
                eng.scalar_tensor_tensor(x[:, k, :], x[:, k, :], vec[:, V_NN + k:V_NN + k + 1], rstd[:, :], ALU.mult, ALU.mult).then_inc(y_out, 1)

        @block.tensor
        def _(eng):
            def product(pr, s, nk, hi, lo, u, each=None):
                eng.wait_ge(w_lo_done, u + 3)
                for k in range(nk):
                    if each:
                        each(k)
                    w = slice(k * P, (k + 1) * P)
                    for a, b in ((w_hi, hi), (w_hi, lo), (w_lo, hi)):
                        for half in range(2):
                            ins = eng.matmul(pair[pr][:, half, 0:HALF], a[:, s, w], b[:, k, half * HALF:(half + 1) * HALF],
                                             start=k == 0 and b is hi and a is w_hi, stop=k == nk - 1 and a is w_lo)
                ins.then_inc(unit_done, 1)

            def squares(s, nsq, first=False, last=False):
                eng.wait_ge(sq_done, nsq + 1)
                for part in (sq_hi, sq_lo):
                    for half in range(2):
                        ins = eng.matmul(pair[3][:, half, 0:HALF], ones_r[:, :], part[:, s, half * HALF:(half + 1) * HALF],
                                         start=first and part is sq_hi, stop=last and part is sq_lo)
                ins.then_inc(ss_used, 1)

            def gate_up(u, ab, cd, n, norm=None):
                def turn(it, first):
                    v = u + it * 4
                    for s in range(2):
                        eng.wait_ge(taken[s], ab + it + 1)
                        product(s, 0, KT, h_hi, h_lo, v + 2 * s, (lambda k: eng.wait_ge(h_done, norm * KT + (k + 1))) if first and s == 0 and norm is not None else None)
                        if first and s == 1 and norm is not None:
                            eng.wait_ge(rms_done, norm + 1)
                        eng.wait_ge(taken[2 + s], cd + it + 1)
                        product(2 + s, 1, KT, h_hi, h_lo, v + 2 * s + 1)
                turn(0, True)
                with eng.Fori(1, n // 2) as it:
                    turn(it, False)

            def to_x(u, ab, nk, norm, wait0):
                def turn(it, first):
                    for s in range(2):
                        eng.wait_ge(taken[s], ab + it + 1)
                        product(s, s, nk, mid_hi, mid_lo, u + it * 2 + s, wait0 if first and s == 0 else None)
                        if norm is not None and not (first and s == 0):
                            squares(1 - s, norm * KT + (it * 2 + s - 1), first=first)
                turn(0, True)
                with eng.Fori(1, KT // 2) as it:
                    turn(it, False)
                if norm is not None:
                    return lambda: squares(1, norm * KT + (KT - 1), last=True)

            def ffn(l, f, norm):
                u, ab, cd, tg = l * U_LAYER + B_FFN[f], l * AB_LAYER + AB_FFN[f], l * CD_LAYER + CD_FFN[f], l * (2 * FT) + f * FT
                gate_up(u, ab, cd, FA, norm)
                to_x(u + 2 * FA, ab + FA // 2, FA, None, lambda k: eng.wait_ge(mid_done, tg + (k + 1)))
                gate_up(u + (2 * FA + KT), ab + (FA // 2 + 4), cd + FA // 2, FB)
                return to_x(u + (2 * FT + KT), ab + (FT // 2 + 4), FB, norm + 1, lambda k: eng.wait_ge(mid_done, tg + (FA + k + 1)))

            def mix(l, last_squares):
                u, ab = l * U_LAYER + B_MIX, l * AB_LAYER + AB_MIX
                norm = l * NORMS + 1
                eng.wait_ge(taken[0], ab + 1)
                product(0, 0, KT, h_hi, h_lo, u, lambda k: eng.wait_ge(h_done, norm * KT + (k + 1)))
                last_squares()
                eng.wait_ge(taken[1], ab + 1)
                product(1, 1, KT, h_hi, h_lo, u + 1)
                with eng.Fori(1, 6) as it:
                    for s in range(2):
                        eng.wait_ge(taken[s], ab + it + 1)
                        product(s, s, KT, h_hi, h_lo, u + it * 2 + s)

                def logits():
                    eng.wait_ge(wba_done, l + 1)
                    for k in range(KT):
                        for a, b in ((w_ba_hi, h_hi), (w_ba_hi, h_lo), (w_ba_lo, h_hi)):
                            for half in range(2):
                                ins = eng.matmul(pair[2][0:8, half, 0:HALF], a[:, k * 8:k * 8 + 8], b[:, k, half * HALF:(half + 1) * HALF],
                                                 start=k == 0 and a is w_ba_hi and b is h_hi, stop=k == KT - 1 and a is w_ba_lo)
                    ins.then_inc(lg_done, 1)

                def turn_logits():
                    eng.wait_ge(lg_scaled, l + 1)
                    for c in range(NCH):
                        n, t0 = CH[c], T0[c]
                        ins = eng.matmul(PC0[0:n, c * 8:c * 8 + 8], z_s[0:8, 0, t0:t0 + n], mask[0:8, M_ID, 0:8], start=True, stop=True)
                    ins.then_inc(logit_done, 1)

                def kq_sums():
                    for j in range(8):
                        eng.wait_ge(kq_sq_done, l * 8 + (j + 1))
                        for c in range(NCH):
                            n, t0 = CH[c], T0[c]
                            ins = eng.matmul(PC1[0:n, c * 8 + j:c * 8 + j + 1], (sq_k if j < 4 else sq_q)[:, j % 4, t0:t0 + n],
                                             mask[:, M_ONE, 0:1], start=True, stop=True)
                    ins.then_inc(kq_sum_done, 1)

                def g_sums():
                    g, ns, nr = tok["g"], CH[0], CH[5]
                    eng.wait_ge(tok_d, l * TOK_D + T_G)
                    g4 = g[:, 1:5, :].rearrange("p c h -> p (c h)")
                    mm = lambda out, a, b: eng.matmul(out, a, b, start=True, stop=True)
                    mm(PD0[:, 0:16], mask[:, M_TRI, :], g4)
                    mm(PD0[:, 16:32], mask[:, M_GT, :], g4)
                    mm(PD0[0:ns, 32:36], mask[0:ns, M_TRIS, 0:ns], g[0:ns, 0, :])
                    mm(PD0[0:ns, 36:40], mask[0:ns, M_GTS, 0:ns], g[0:ns, 0, :])
                    mm(PD0[0:nr, 40:44], mask[0:nr, M_TRI, 0:nr], g[0:nr, 5, :])
                    mm(PD0[0:nr, 44:48], mask[0:nr, M_GT, 0:nr], g[0:nr, 5, :])
                    mm(PD0[:, 48:64], mask[:, M_ONE, :], g4)
                    mm(PD0[:, 64:68], mask[0:nr, M_ONE, :], g[0:nr, 5, :])
                    mm(PD0[:, 68:68 + SEGS * H], mask[0:ns, M_ONE, :], g_seg[0:ns, :, :].rearrange("p s h -> p (s h)")).then_inc(gsum_done, 1)

                def ri(c):
                    eng.wait_ge(conv_done, l * 16 + (12 + c + 1))
                    if c:
                        eng.wait_ge(lru_a, l * (4 * LRU_A) + ((c - 1) * LRU_A + 2))
                    else:
                        eng.wait_ge(gexp_done, l + 1)
                        eng.wait_ge(tok_d, l * TOK_D + T_SS)
                    for g in range(2):
                        for half in range(2):
                            ins = eng.matmul(pair[2 + g][:, half, 0:HALF], w_ri[:, c, g, :], xc(c)[:, half * HALF:(half + 1) * HALF], start=True, stop=True)
                    ins.then_inc(ri_done, 1)

                logits()
                for n in range(12, U_MIX):
                    eng.wait_ge(taken[n % 2], ab + n // 2 + 1)
                    product(n % 2, n % 2, KT, h_hi, h_lo, u + n)
                    if n == 12:
                        turn_logits()
                    if n == 15:
                        kq_sums()
                        g_sums()
                    if n >= 16 and n % 2 == 0:
                        ri((n - 16) // 2)
                for c in range(NCH + 1):
                    new, old = c < NCH, c > 0
                    if new:
                        start(l, c)
                    if old:
                        old_state(l, c - 1)
                    if new:
                        first_z(l, c)
                    if old:
                        z_r(l, c - 1)
                    level(l, c, 0)
                    if old:
                        update(l, c - 1)
                    level(l, c, 1)
                    if c == 1:
                        segments(l, 1)
                    level(l, c, 2)
                    if c == 1:
                        segments(l, 2)
                    level(l, c, 3)
                    if old:
                        o_turned(l, c - 1)
                    level(l, c, 4)
                    level(l, c, 5)
                    if new:
                        turn_z(l, c, len(LEVELS[c]) - 1)

            count = eng.alloc_register("awaited_count")

            def wait(c, sem, value):
                if CH[c] < P:
                    eng.reg_mov(count, value)
                    eng.wait_ge(init_done, 2)
                    value = count
                eng.wait_ge(sem, value)

            def mm(out, a, b):
                return eng.matmul(out, a, b, start=True, stop=True)

            def start(l, c):
                n, lc, t0 = CH[c], l * NCH + c, T0[c]
                tt = slice(t0, t0 + n)
                if c == 0:
                    wait(c, lru_a, l * (4 * LRU_A) + (3 * LRU_A + 2))
                else:
                    wait(c, y_upd, l * (2 * LV) + 2 * lv(c, 0))
                for h in range(H):
                    mm(PC0[0:n, h * n:(h + 1) * n], kqv[:, 4 + h, tt], kqv[:, 4 + h, tt])
                for h in range(H):
                    ins = mm(PC1[0:n, h * n:(h + 1) * n], kqv[:, 4 + h, tt], kqv[:, 8 + h, tt])
                ins.then_inc(kq_done, 1)
                wait(c, grhs_done, lc + 1)
                for part in (gr_hi, gr_lo):
                    ins = eng.matmul(bank(PD0, n, n), after_r[0:n, c == 0, 0:n], head(part, n, n), start=part is gr_hi, stop=part is gr_lo)
                ins.then_inc(dt_done, 1)
                for h in range(H):
                    ins = eng.transpose(PD1[0:n, h * P:(h + 1) * P], kqv[:, 4 + h, tt], mask[:, M_ID, :])
                ins.then_inc(kt_done, 1)

            def first_z(l, c):
                n, lc, t0 = CH[c], l * NCH + c, T0[c]
                wait(c, em_done, lc + 1)
                for h in range(H):
                    ins = eng.transpose(PD0[0:n, h * P:(h + 1) * P], kqv[:, h, t0:t0 + n], mask[:, M_ID, :])
                ins.then_inc(vt_done, 1)
                wait(c, y0_done, lc + 1)
                for h in range(H):
                    ins = eng.transpose(PC0[0:n, h * n:(h + 1) * n], y_c[c % 2][0:n, h, 0:n], mask[0:n, M_ID, 0:n])
                ins.then_inc(z0_done, 1)

            def level(l, c, k):
                if c == NCH or k >= len(LEVELS[c]):
                    return
                n, s = CH[c], LEVELS[c][k]
                if k:
                    turn_z(l, c, k - 1)
                    z = lower(head(z_m, n, n), s)
                else:
                    wait(c, z_init, l * NCH + c + 1)
                    wait(c, attn_done, l * NCH + c + 1)
                    z = packed(z_c, n, s)
                for g in range(2):
                    for h in (2 * g, 2 * g + 1):
                        ins = mm(packed((PC0, PC1)[g], n, s)[:, h], nt[0:n, h, 0:n], z[:, h])
                    ins.then_inc(nz_done, 1)
                for g in range(2):
                    wait(c, p_done, at(l, c, k, g))
                    if k:
                        wait(c, y_upd, at(l, c, k - 1, g))
                    for h in (2 * g, 2 * g + 1):
                        ins = mm(packed((PC0, PC1)[g], n, s)[:, h], y_c[c % 2][0:n, h, 0:n], packed(p_c, n, s)[:, h])
                    ins.then_inc(zp_done, 1)

            def turn_z(l, c, k):
                n = CH[c]
                for g in range(2):
                    wait(c, z_upd, at(l, c, k, g))
                    if k:
                        wait(c, y_upd, at(l, c, k - 1, g))
                    else:
                        wait(c, (vscaled_done, kdec_done)[g], l * NCH + c + 1)
                    for h in (2 * g, 2 * g + 1):
                        ins = eng.transpose((PD0, PD1)[g][0:n, h * n:(h + 1) * n], z_m[0:n, h, 0:n], mask[0:n, M_ID, 0:n])
                    ins.then_inc(zt_done, 1)

            def old_state(l, c):
                n, t0 = CH[c], T0[c]
                if c:
                    wait(c, s_done, l * NCH + c)
                    wait(c, og_done, l * NCH + c)
                    for h in range(H):
                        ins = mm(PA0[0:n, h * P:(h + 1) * P], kqv[:, 4 + h, t0:t0 + n], s_p[:, h, :])
                    ins.then_inc(ks_done, 1)
                    for h in range(H):
                        ins = mm(PA1[0:n, h * P:(h + 1) * P], kqv[:, 8 + h, t0:t0 + n], s_p[:, h, :])
                    ins.then_inc(qs_done, 1)
                    return
                wait(c, s0a_loaded, l * 16 + 16)
                wait(c, s0b_loaded, l * 16 + 16)

                def turn_head(h):
                    wait(c, kst_done, l * H + (h + 1))
                    eng.transpose(PA0[0:n, h * P:(h + 1) * P], ks_t[:, h % 2, 0, :], mask[:, M_ID, :])
                    eng.transpose(PA1[0:n, h * P:(h + 1) * P], ks_t[:, h % 2, 1, :], mask[:, M_ID, :]).then_inc(kstt_done, 1)
                for h in range(H):
                    out = (PB0, PB1)[h % 2][:, 0:2 * n].rearrange("p (k t) -> p k t", k=2)
                    for s in range(SEGS):
                        a, b = s * SLEN, (s + 1) * SLEN
                        ins = mm(out[:, :, a:b], seg_state(h, s), kqv[:, 4 + h:9 + h:4, t0 + a:t0 + b])
                    ins.then_inc(seg_done, 1)
                    if h:
                        turn_head(h - 1)
                turn_head(3)

            def z_r(l, c):
                n = CH[c]
                wait(c, r_done, l * NCH + c + 1)
                wait(c, y_upd, l * (2 * LV) + 2 * lv(c + 1, 0))
                for h in range(H):
                    ins = mm(PB0[0:n, h * P:(h + 1) * P], y_c[c % 2][0:n, h, 0:n], r_s[0:n, h, :])
                ins.then_inc(zr_done, 1)

            def update(l, c):
                n = CH[c]
                wait(c, vnew_done, l * NCH + c + 1)
                if c:
                    for h in range(H):
                        ins = mm(PB1[:, h * P:(h + 1) * P], kdec[c % 2][0:n, h, :], v_new[0:n, h, :])
                    ins.then_inc(kv_done, 1)
                for h in range(H):
                    ins = mm(PA0[0:n, h * P:(h + 1) * P], attn[c % 2][0:n, h, 0:n], v_new[0:n, h, :])
                ins.then_inc(av_done, 1)
                if c == 0:
                    segments(l, 0)

            def segments(l, h):
                i, n = l * H + (h + 1), CH[0]
                wait(0, vseg_done, i)
                if h:
                    wait(0, seg_s_done, i - 1)
                mm(PB0[:, :], kdec[0][0:n, h, :], vseg[0:n, 0:4, :])
                mm(PB1[:, :], kdec[0][0:n, h, :], vseg[0:n, 4:8, :]).then_inc(segkv_done, 1)

            def o_turned(l, c):
                n = CH[c]
                wait(c, on_done, l * NCH + c + 1)
                for h in range(H):
                    ins = eng.transpose(PA1[:, h * n:(h + 1) * n], o_s[0:n, h, :], mask[0:n, M_ID, 0:n])
                ins.then_inc(ot_done, 1)
                if c == 0:
                    segments(l, 3)

            eng.wait_ge(init_done, 2)
            for k in range(KT):
                squares(k % 2, k, k == 0, k == KT - 1)
            with eng.Fori(0, DEPTH) as l:
                t = ffn(l, 0, l * NORMS)
                mix(l, t)
                t = to_x(l * U_LAYER + B_OUT, l * AB_LAYER + AB_OUT, KT, l * NORMS + 2,
                         lambda k: eng.wait_ge(oy_done, l * KT + (k + 1)))
                t()
                t = ffn(l, 1, l * NORMS + 2)
                t()


_OUTS = {"y": (KT, P, T), "conv": (DEPTH, P, 16, 27), "lru": (DEPTH, P, 4, 9), "dp": (DEPTH, P, H, P), "ds": (DEPTH * 2, P, 2, SEQS, P)}


def _units(w, m_tiles):
    rows = w.shape[0]
    return w.reshape(rows // P, P, m_tiles, P).transpose(2, 1, 0, 3).reshape(m_tiles, P, rows)


def _per_tile(v):
    return np.moveaxis(v.reshape(v.shape[:-1] + (-1, P)), -1, 0).reshape(P, -1)


def _rows(v):
    return np.broadcast_to(v, (P, v.shape[0]))


def _layout(a):
    d_a = H * DK
    x = np.concatenate([a["meta_tokens"], a["x_prompt"][0], a["x_sample"].reshape(TS, D)], axis=0)
    n1, nm, n2 = a["norm_ffn1"], a["norm_mix"], a["norm_ffn2"]
    vec, wba, wri, chist, lru0, s0, wgu, wda, wdb, win, wout = ([] for _ in range(11))
    for l in range(DEPTH):
        cw = a["conv_qkv"][l].T
        vkq = np.concatenate([cw[2 * d_a:], cw[d_a:2 * d_a], cw[:d_a], a["conv_lru_w"][l].T], axis=0)
        taps = vkq.reshape(16, P, TAPS).transpose(1, 0, 2).reshape(P, 16 * TAPS)
        after = n1[l + 1] if l + 1 < DEPTH else a["norm_final"]
        vec.append(np.concatenate([_per_tile(nm[l]), _per_tile(n2[l]), _per_tile(after), taps]
                                  + [_per_tile(a[n][l]) for n in ("conv_lru_b", "b_rgate", "b_igate", "lru_lambda")]
                                  + [_rows(a["a_log"][l]), _rows(a["dt_bias"][l]), _per_tile(a["norm_delta_out"][l])], axis=1))
        w = a["w_in"][l]
        q, k, v, z, ba, xr, gate = np.split(w, [d_a, 2 * d_a, 3 * d_a, 4 * d_a, 4 * d_a + 2 * H, 4 * d_a + 2 * H + DR], axis=1)
        wba.append(ba.reshape(KT, P, 8).transpose(1, 0, 2).reshape(P, KT * 8))
        u = lambda m: _units(m, 4)
        win.append(np.concatenate([u(v), u(k), u(q), np.stack([u(xr), u(gate)], axis=1).reshape(8, P, D), u(z)], axis=0))
        ri = np.zeros((P, 4, 2, P), np.float32)
        for g, name in enumerate(("w_rgate", "w_igate")):
            for b in range(8):
                r = slice((b % 2) * 64, (b % 2 + 1) * 64)
                ri[r, b // 2, g, r] = a[name][l, b]
        wri.append(ri)
        hq, hk, hv = np.split(a["state_delta_conv"][l], 3, axis=2)
        h = np.concatenate([hv, hk, hq, a["state_lru_conv"][l]], axis=2)
        chist.append(h.reshape(SEQS, TAPS - 1, 16, P).transpose(3, 2, 0, 1))
        lru0.append(a["state_lru"][l].reshape(SEQS, 4, P).transpose(2, 1, 0))
        s0.append(a["state_delta"][l].reshape(SEQS, 2, 2, DK, P).transpose(1, 3, 2, 0, 4))
        for f in ("1", "2"):
            gu = np.stack([_units(a[f"w_ffn{f}_gate"][l], FT), _units(a[f"w_ffn{f}_up"][l], FT)], axis=1)
            wgu.append(gu.reshape(2 * FT, P, D))
            down = _units(a[f"w_ffn{f}_down"][l], KT)
            wda.append(down[:, :, :FA * P])
            wdb.append(down[:, :, FA * P:])
        wout.append(_units(a["w_out"][l], KT))
    cat = lambda t: np.concatenate(t, axis=0)
    return {"xT": x.T.reshape(KT, P, T), "gain0": _per_tile(n1[0]), "mask": chunk_masks(), "vec": np.stack(vec),
            "wba": np.stack(wba), "wri": np.stack(wri), "chist": np.stack(chist), "lru0": np.stack(lru0), "s0": cat(s0),
            "wgu": cat(wgu), "wda": cat(wda), "wdb": cat(wdb), "win": cat(win), "wout": cat(wout)}


def _results(r):
    y = r["y"].reshape(D, T).T
    conv = r["conv"].transpose(0, 3, 2, 1).reshape(DEPTH, 27, 16 * P)
    v, k, q, xr = np.split(conv, 4, axis=2)
    qkv = np.concatenate([q, k, v], axis=2)
    lru = r["lru"].transpose(0, 3, 2, 1).reshape(DEPTH, 9, DR)
    dp = r["dp"].transpose(0, 2, 1, 3)[:, None]
    ds = r["ds"].reshape(DEPTH, 2, P, 2, SEQS, P).transpose(0, 4, 1, 3, 2, 5).reshape(DEPTH, SEQS, H, DK, P)
    rows = lambda t: (t[:, 0:3][:, None], t[:, 3:].reshape(DEPTH, SEQS, 3, t.shape[2]))
    (qkv_p, qkv_s), (xr_p, xr_s) = rows(qkv), rows(xr)
    out = (y[N_META:TP][None], y[TP:].reshape(SEQS, SLEN, D), dp, qkv_p, lru[:, 0:1], xr_p, ds, qkv_s, lru[:, 1:], xr_s)
    return tuple(np.ascontiguousarray(o) for o in out)


def kernel(**inputs):
    import concourse.bacc as _bacc
    from concourse.bass_utils import run_bass_kernel_spmd as _run

    arrays = {f"in_{n}": np.ascontiguousarray(v) for n, v in _layout({n: np.asarray(v) for n, v in inputs.items()}).items()}
    nc = _bacc.Bacc("TRN2", target_bir_lowering=False, num_devices=1)
    I = {n[3:]: nc.dram_tensor(n, v.shape, mybir.dt.from_np(v.dtype), kind="ExternalInput").ap() for n, v in arrays.items()}
    O = {n: nc.dram_tensor(f"out_{n}", s, F32, kind="ExternalOutput").ap() for n, s in _OUTS.items()}
    build(nc, I, O)
    r = _run(nc, [arrays], core_ids=[0])
    return _results({n: r.results[0][f"out_{n}"] for n in _OUTS})
```

```python
from contextlib import ExitStack

import numpy as np
import concourse.bass as bass
from concourse import mybir

F32 = mybir.dt.float32
F32R = mybir.dt.float32r
ACT = mybir.ActivationFunctionType
ALU = mybir.AluOpType

P = 128
DEPTH, D, SEQ, N_META = 2, 1024, 512, 16
SEQS, SLEN = 8, 8
TP = N_META + SEQ
TS = SEQS * SLEN
T = TP + TS
HALF = T // 2
KT = D // P
FT = 22
FA, FB = 12, 10
H, DK, DR = 4, 128, 512
TAPS = 4
PAD = TAPS - 1 + TP + SEQS * (TAPS - 1 + SLEN)
CONV = PAD - (TAPS - 1)
SAMP0 = TAPS - 1 + TP
STRIDE = TAPS - 1 + SLEN
SEGS = SEQS
CH = [TS, P, P, P, P, TP - 4 * P]
T0 = [TP, 0, P, 2 * P, 3 * P, 4 * P]
NCH = len(CH)
LEVELS = [[2, 4]] + [[2, 4, 8, 16, 32, 64]] * 4 + [[2, 4, 8]]
SUM_G = (NCH - 1) * H + SEGS * H
EPS = 1e-6

V_NM, V_N2, V_NN, V_CQ, V_CL, V_CB, V_BR, V_BI, V_LAM, V_ALOG, V_DT, V_ON = (
    0, 8, 16, 24, 72, 88, 92, 96, 100, 104, 108, 112)
NV = 113
M_TRI, M_TRIS, M_GT, M_GTS, M_L1T, M_L2, M_L4, M_L8, M_L16, M_L32, M_L64, M_ID, M_ONE = range(13)
N_MASKS, IND = 13, slice(96, 104)
LEVEL_MASK = {2: M_L2, 4: M_L4, 8: M_L8, 16: M_L16, 32: M_L32, 64: M_L64}

U_FFN = 2 * FT + 16
U_MIX = 24
U_OUT = 8
U_LAYER = 2 * U_FFN + U_MIX + U_OUT
B_FFN = (0, U_FFN + U_MIX + U_OUT)
B_MIX = U_FFN
B_OUT = U_FFN + U_MIX
AB_LAYER, AB_FFN, AB_MIX, AB_OUT = 54, (0, 35), 19, 31
CD_LAYER, CD_FFN = 22, (0, 11)
NORMS = 3
SS = KT + 1
SMALL = 5
LRU_A, LRU_D = 5, 11
T_ABS, T_G, T_SS, TOK_D = 3, 21, 22, 26
SP_N = NCH * H + 4
ATANH = [1.0 / (2 * i + 1) for i in range(8, 0, -1)]


def chunk_masks():
    m = np.zeros((N_MASKS, P, P), np.float32)
    r = np.arange(P)
    row, col = r[:, None], r[None, :]
    seg = r // SLEN
    same = seg[:, None] == seg[None, :]
    m[M_TRI] = row <= col
    m[M_TRIS] = (row <= col) & same
    m[M_GT] = row > col
    m[M_GTS] = (row > col) & same
    for s, at in LEVEL_MASK.items():
        m[at] = (row // (2 * s) == col // (2 * s)) & (row % (2 * s) >= s) & (col % (2 * s) < s)
    m[M_L1T] = (row // 2 == col // 2) & (col % 2 == 1) & (row % 2 == 0)
    m[M_ID] = row == col
    m[M_ONE] = 1.0
    m[M_GTS, :, IND] = seg[:, None] == np.arange(SEGS)[None, :]
    return np.ascontiguousarray(m.transpose(1, 0, 2))


def build(nc, I, O):
    ctx = ExitStack()

    def sb(name, shape, dt=F32, stack=ctx):
        return stack.enter_context(nc.sbuf_tensor(name, shape, dt))

    def sem(name):
        return ctx.enter_context(nc.semaphore(name))

    with ctx:
        x = sb("x", [P, KT, T])
        with ExitStack() as st:
            h_hi, h_lo = sb("h_hi", [P, KT, T], F32R, st), sb("h_lo", [P, KT, T], F32R, st)
        with ExitStack() as st:
            y1, attn1, kdec1, vn1, r_s, v_new, o_s, qs = (
                sb(n, [P, H, P], F32, st) for n in ("y1", "attn1", "kdec1", "vn1", "r_s", "v_new", "o_s", "qs"))
            p_c, z_c = (sb(n, [P, H * P // 2], F32, st) for n in ("p_c", "z_c"))
            s0a, s0b = (sb(n, [P, 2, SEQS, P], F32, st) for n in ("s0a", "s0b"))
            s_p = sb("s_p", [P, H, P], F32, st)
        sb("h_room", [P, 2 * KT * T])
        w_raw = sb("w_raw", [P, 2, FA * P])
        w_hi, w_lo = sb("w_hi", [P, 2, FA * P], F32R), sb("w_lo", [P, 2, FA * P], F32R)
        rms, rstd = sb("rms", [P, T]), sb("rstd", [P, T])
        gain0 = sb("gain0", [P, KT])
        vec = sb("vec", [P, NV])
        w_ba = sb("w_ba", [P, KT * 8])
        w_ba_hi, w_ba_lo = sb("w_ba_hi", [P, KT * 8], F32R), sb("w_ba_lo", [P, KT * 8], F32R)
        w_ri = sb("w_ri", [P, 4, 2, P])
        conv_hist = sb("conv_hist", [P, 16, SEQS, TAPS - 1])
        lru_h0 = sb("lru_h0", [P, 4, SEQS])
        conv_new = sb("conv_new", [P, 16, 27])
        lru_new = sb("lru_new", [P, 4, 9])
        mask = sb("mask", [P, N_MASKS, P])
        ones_r = sb("ones_r", [P, P], F32R)
        tok = {n: sb("tok_" + n, [P, NCH, H]) for n in
               ("beta", "g", "nk", "nb", "bk2", "rq", "rq2", "nq", "rk")}
        logit = sb("logit", [P, NCH, 8])
        g_hi, g_lo = sb("g_hi", [P, NCH, H], F32R), sb("g_lo", [P, NCH, H])
        kq_ss = sb("kq_ss", [P, NCH, 8])
        ea = sb("ea", [P, H])
        lam8 = sb("lam8", [P, 8])
        h_start = sb("h_start", [P, SEQS])
        e_g, e_gs, e_gt = sb("e_g", [P, 32]), sb("e_gs", [P, 8]), sb("e_gt", [P, 8])
        g_seg = sb("g_seg", [P, SEGS, H])
        e_last = sb("e_last", [P, SUM_G])
        o_ss, o_ms, o_rms, o_rec, o_fac = (sb(n, [P, H]) for n in ("o_ss", "o_ms", "o_rms", "o_rec", "o_fac"))

        eps = sb("eps", [P, 3])
        with ExitStack() as st:
            mid_hi, mid_lo = (sb(n, [P, FA, T], F32R, st) for n in ("mid_hi", "mid_lo"))
            gate_s, silu_s, prod = (sb(n, [P, 2, T], F32, st) for n in ("gate_s", "silu_s", "prod"))
            up_s = sb("up_s", [P, T], F32, st)
            sq = sb("sq", [P, 2, T], F32, st)
            ss = sb("ss", [P, T], F32, st)
            ss_hi, ss_lo = sb("ss_hi", [P, T], F32R, st), sb("ss_lo", [P, T], F32R, st)
        with ExitStack() as st:
            cp = sb("cp", [P, 2, PAD], F32, st)
            acc = sb("acc", [P, PAD], F32, st)
            with ExitStack() as inner:
                sq_k = sb("sq_k", [P, 4, T], F32, inner)
            em, attn0, nt, z_m, y0 = (sb(n, [P, H, P], F32, st) for n in ("em", "attn0", "nt", "z_m", "y0"))
            sp = {n: sb("sp_" + n, [P, SP_N], F32, st) for n in ("y", "abs", "e", "z", "z2", "p", "out")}
            sb("gap0", [P, KT * T - 3 * PAD - 5 * H * P - 7 * SP_N], F32, st)
            lt = sb("lt", [P, 4, T], F32, st)
            with ExitStack() as inner:
                sq_q = sb("sq_q", [P, 4, T], F32, inner)
            kdec0, vn0 = (sb(n, [P, H, P], F32, st) for n in ("kdec0", "vn0"))
            after_r = sb("after_r", [P, 2, P], F32R, st)
            gr_hi, gr_lo = (sb(n, [P, H, P], F32R, st) for n in ("gr_hi", "gr_lo"))
            sb("gap1", [P, 4 * T - 4 * H * P - 2 * P], F32, st)
            z_s = sb("z_s", [P, 4, T], F32, st)
            x_c = sb("x_c", [P, 3, T], F32, st)
            sb("gap2", [P, T], F32, st)
            kqv = sb("kqv", [P, 12, T], F32, st)
            y_s = sb("y_s", [P, 4, T], F32, st)
        y_c, attn, kdec, vn_s = (y0, y1), (attn0, attn1), (kdec0, kdec1), (vn0, vn1)
        vseg = cp[:, :, :].rearrange("p a t -> p (a t)")[:, 0:SEGS * P].rearrange("p (s d) -> p s d", s=SEGS)
        ks_t = acc[:, 0:4 * TS].rearrange("p (b k t) -> p b k t", b=2, k=2)

        pair = [ctx.enter_context(nc.psum_tensor(f"pair{n}", [P, 2, 512], F32)) for n in "ABCD"]
        PA0, PA1, PB0, PB1, PC0, PC1, PD0, PD1 = (pair[i // 2][:, i % 2, :] for i in range(8))

        w_loaded = [sem("w_loaded0"), sem("w_loaded1")]
        w_hi_done, w_lo_done, unit_done = (sem(n) for n in (
            "w_hi_done", "w_lo_done", "unit_done"))
        silu_done, prod_done, mid_hi_done, mid_done = (sem(n) for n in (
            "silu_done", "prod_done", "mid_hi_done", "mid_done"))
        h_hi_done, h_done, sq_done, ss_step, ss_hi_done, ss_lo_done, ss_done = (sem(n) for n in (
            "h_hi_done", "h_done", "sq_done", "ss_step", "ss_hi_done", "ss_lo_done", "ss_done"))
        rms_done, rstd_done, init_done = (sem(n) for n in (
            "rms_done", "rstd_done", "init_done"))
        x_loaded = [sem(f"x_loaded{k}") for k in range(KT)]
        gain_loaded, mask_loaded, small_loaded, s0a_loaded, s0b_loaded = (sem(n) for n in (
            "gain_loaded", "mask_loaded", "small_loaded", "s0a_loaded", "s0b_loaded"))
        states_out, seqs_out, y_out, y_stored = (sem(n) for n in (
            "states_out", "seqs_out", "y_out", "y_stored"))
        pad_done, conv_step, conv_done, kqv_done = (sem(n) for n in (
            "pad_done", "conv_step", "conv_done", "kqv_done"))
        wba_hi_done, wba_done, lg_done, lg_scaled, logit_done, kq_sq_done, kq_sum_done = (sem(n) for n in (
            "wba_hi_done", "wba_done", "lg_done", "lg_scaled", "logit_done", "kq_sq_done", "kq_sum_done"))
        tok_d, tok_a, gsum_done, gexp_done = (sem(n) for n in (
            "tok_d", "tok_a", "gsum_done", "gexp_done"))
        gelu_done, ri_done, lru_a, lru_d, silu_z_done = (sem(n) for n in (
            "gelu_done", "ri_done", "lru_a", "lru_d", "silu_z_done"))
        grhs_done, dt_done, em_done, emm_done, kq_done = (sem(n) for n in (
            "grhs_done", "dt_done", "em_done", "emm_done", "kq_done"))
        kt_done, vt_done, kdec_done, vscaled_done, nt_done, attn_done = (sem(n) for n in (
            "kt_done", "vt_done", "kdec_done", "vscaled_done", "nt_done", "attn_done"))
        y0_tmp, y0_done, z0_done, z_init, nz_done, p_done, zp_done, z_upd, zt_done, y_upd = (sem(n) for n in (
            "y0_tmp", "y0_done", "z0_done", "z_init", "nz_done", "p_done", "zp_done", "z_upd", "zt_done", "y_upd"))
        ks_done, qs_done, qs_scaled, r_done, zr_done, vnew_done, av_done, kv_done, s_done = (sem(n) for n in (
            "ks_done", "qs_done", "qs_scaled", "r_done", "zr_done", "vnew_done", "av_done", "kv_done", "s_done"))
        o_done, o_sq_done, o_step, o_rms_done, on_done, ot_done, og_done = (sem(n) for n in (
            "o_done", "o_sq_done", "o_step", "o_rms_done", "on_done", "ot_done", "og_done"))
        seg_done, kst_done, kstt_done, vseg_done, segkv_done, seg_s_done = (sem(n) for n in (
            "seg_done", "kst_done", "kstt_done", "vseg_done", "segkv_done", "seg_s_done"))
        oy_hi_done, oy_done = (sem(n) for n in (
            "oy_hi_done", "oy_done"))
        taken = [sem("taken" + n) for n in "ABCD"]
        block = ctx.enter_context(nc.Block())

        def lv(c, k):
            return sum(len(LEVELS[i]) for i in range(c)) + k
        LV = lv(NCH, 0)

        def at(l, c, k, g):
            return l * (2 * LV) + (2 * lv(c, k) + g + 1)

        def bc(ap, n):
            return ap.unsqueeze(2).to_broadcast([ap.shape[0], ap.shape[1], n])

        def bh(ap, n):
            return ap.unsqueeze(1).to_broadcast([ap.shape[0], n, ap.shape[1]])

        def cols(pr):
            return pair[pr][:, :, 0:HALF]

        def tiles(ap):
            return ap.rearrange("p (a t) -> p a t", a=2)

        def seq(ap, n=SEQS):
            return ap.rearrange("p (b t) -> p b t", b=n)

        def samples(buf, first, n):
            return seq(buf[:, SAMP0:PAD])[:, :, first:first + n]

        def xc(c):
            return x_c[:, c % 3, :]

        def head(t, n, m):
            return t[0:n, :, 0:m]

        def bank(b, n, m):
            return b[0:n, 0:H * m].rearrange("p (h m) -> p h m", h=H)

        def lower(ap, s):
            return ap.rearrange("p h (b t) -> p h b t", t=2 * s)[:, :, :, 0:s]

        def packed(b, n, s):
            return b[0:n, 0:H * n // 2].rearrange("p (h b t) -> p h b t", h=H, t=s)

        def tok_e(c, n, after):
            if c == 0:
                return e_gs[0:n, after * H:(after + 1) * H]
            if c == NCH - 1:
                return e_gt[0:n, after * H:(after + 1) * H]
            return e_g[0:n, after * 16 + (c - 1) * H:after * 16 + c * H]

        def seg_state(h, s):
            return (s0a if h < 2 else s0b)[:, h % 2, s, :]

        def turned(c):
            return PB0 if c == NCH - 1 else PA1

        PARTS = ((P, slice(1, 5)), (CH[0], slice(0, 1)), (CH[5], slice(5, 6)))

        @block.sync
        def _(eng):
            for k in range(KT):
                eng.dma_start(x[:, k, :], I["xT"][k]).then_inc(x_loaded[k], 16)
            eng.sem_inc(w_lo_done, 2)

            def load(u, pairs, src, at, n):
                with eng.Fori(0, pairs) as it:
                    for s in range(2):
                        eng.wait_ge(w_lo_done, u + it * 2 + (s + 1))
                        eng.dma_start(w_raw[:, s, 0:n], src[at + it * 2 + s]).then_inc(w_loaded[s], 16)

            def ffn(l, f):
                u = l * U_LAYER + B_FFN[f]
                load(u, FA, I["wgu"], l * (4 * FT) + f * 2 * FT, KT * P)
                load(u + 2 * FA, KT // 2, I["wda"], l * (2 * KT) + f * KT, FA * P)
                load(u + (2 * FA + KT), FB, I["wgu"], l * (4 * FT) + (f * 2 * FT + 2 * FA), KT * P)
                load(u + (2 * FT + KT), KT // 2, I["wdb"], l * (2 * KT) + f * KT, FB * P)

            with eng.Fori(0, DEPTH) as l:
                ffn(l, 0)
                load(l * U_LAYER + B_MIX, U_MIX // 2, I["win"], l * U_MIX, KT * P)
                load(l * U_LAYER + B_OUT, U_OUT // 2, I["wout"], l * U_OUT, KT * P)
                ffn(l, 1)
            for k in range(KT):
                eng.wait_ge(y_out, k + 1)
                eng.dma_start(O["y"][k], x[:, k, :]).then_inc(y_stored, 16)
            eng.wait_ge(y_stored, 16 * KT)
            eng.wait_ge(states_out, DEPTH * 16 * 2)
            eng.wait_ge(seqs_out, DEPTH * 16 * 3)

        @block.gpsimd
        def _(eng):
            count = eng.alloc_register("awaited_count")

            def apart(sem, value):
                eng.reg_mov(count, value)
                eng.wait_ge(mask_loaded, 16)
                eng.wait_ge(sem, count)

            eng.dma_start(gain0[:, :], I["gain0"]).then_inc(gain_loaded, 16)
            eng.wait_ge(x_loaded[KT - 1], 16)
            eng.dma_start(mask[:, :, :], I["mask"]).then_inc(mask_loaded, 16)
            with eng.Fori(0, DEPTH) as l:
                eng.wait_ge(rstd_done, l * NORMS + 1)
                for dst, name in ((vec[:, :], "vec"), (w_ba[:, :], "wba"), (w_ri[:, :, :, :], "wri"),
                                  (conv_hist[:, :, :, :], "chist"), (lru_h0[:, :, :], "lru0")):
                    eng.dma_start(dst, I[name][l]).then_inc(small_loaded, 16)
                u = l * U_LAYER + B_MIX
                with eng.Fori(0, U_MIX // 2) as it:
                    for s in range(2):
                        eng.wait_ge(w_hi_done, u + it * 2 + (s + 1))
                        eng.tensor_tensor(w_lo[:, s, 0:KT * P], w_raw[:, s, 0:KT * P],
                                          w_hi[:, s, 0:KT * P].bitcast(F32), ALU.subtract).then_inc(w_lo_done, 1)
                apart(kq_sum_done, l + 1)
                eng.tensor_copy(after_r[:, 0, :], mask[:, M_GT, :])
                eng.tensor_copy(after_r[:, 1, :], mask[:, M_GTS, :])
                eng.wait_ge(tok_d, l * TOK_D + T_G)

                def spread(c):
                    n = CH[c]
                    if c:
                        eng.wait_ge(dt_done, l * NCH + c)
                    tri = bh(mask[0:n, M_TRIS if c == 0 else M_TRI, 0:n], H)
                    eng.tensor_tensor(head(gr_hi, n, n), tri, bc(g_hi[0:n, c, :].bitcast(F32), n), ALU.mult)
                    eng.tensor_tensor(head(gr_lo, n, n), tri, bc(g_lo[0:n, c, :], n), ALU.mult).then_inc(grhs_done, 1)

                spread(0)
                apart(unit_done, u + (U_MIX + 2))
                eng.dma_start(s0a[:, :, :, :], I["s0"][l * 2]).then_inc(s0a_loaded, 16)
                eng.dma_start(s0b[:, :, :, :], I["s0"][l * 2 + 1]).then_inc(s0b_loaded, 16)
                spread(1)
                apart(lru_d, l * (4 * LRU_D) + 4 * LRU_D + 1)
                eng.dma_start(O["conv"][l], conv_new[:, :, :]).then_inc(states_out, 16)
                eng.dma_start(O["lru"][l], lru_new[:, :, :]).then_inc(states_out, 16)
                spread(2)
                apart(seg_s_done, l * H + H)
                eng.dma_start(O["ds"][l * 2], s0a[:, :, :, :]).then_inc(seqs_out, 16)
                eng.dma_start(O["ds"][l * 2 + 1], s0b[:, :, :, :]).then_inc(seqs_out, 16)
                for c in range(3, NCH):
                    spread(c)
                apart(s_done, l * NCH + NCH)
                eng.dma_start(O["dp"][l], s_p[:, :, :]).then_inc(seqs_out, 16)

        @block.scalar
        def _(eng):
            eng.sem_inc(unit_done, 2)
            eng.sem_inc(ss_step, 2)
            eng.sem_inc(kqv_done, 1)

            def split(u, s, n):
                eng.wait_ge(w_loaded[s], u * 8 + (16 - 8 * s))
                eng.wait_ge(unit_done, u + 1)
                eng.activation(w_hi[:, s, 0:n], w_raw[:, s, 0:n], ACT.Copy).then_inc(w_hi_done, 1)

            def new_x(m, s, gain, norm):
                eng.wait_ge(ss_step, norm * SS + m + 2)
                eng.activation(sq[:, s, :], x[:, m, :], ACT.Square).then_inc(sq_done, 1)
                eng.activation(h_hi[:, m, :], x[:, m, :], ACT.Copy, scale=gain).then_inc(h_hi_done, 1)

            def root(norm):
                eng.wait_ge(ss_step, norm * SS + (SS + 2))
                eng.activation(ss_hi[:, :], ss[:, :], ACT.Copy).then_inc(ss_hi_done, 1)
                eng.wait_ge(ss_done, norm + 1)
                eng.activation(tiles(rms[:, :]), cols(3), ACT.Sqrt, bias=eps[:, 0:1], scale=1.0 / D).then_inc(rms_done, 1)

            def gate_up(u, ab, tg, n, prev):
                def gate(use, s):
                    eng.wait_ge(taken[s], use + 2)
                    eng.activation(silu_s[:, s, :], gate_s[:, s, :], ACT.Silu).then_inc(silu_done, 1)

                def up(t, k, s):
                    eng.wait_ge(prod_done, t + 1)
                    eng.activation(mid_hi[:, k, :], prod[:, s, :], ACT.Copy).then_inc(mid_hi_done, 1)

                def turn(it, first):
                    v = u + it * 4
                    split(v, 0, KT * P)
                    prev(0) if first else gate(ab + it - 1, 1)
                    split(v + 1, 1, KT * P)
                    prev(1) if first else up(tg + it * 2 - 1, it * 2 - 1, 1)
                    split(v + 2, 0, KT * P)
                    gate(ab + it, 0)
                    split(v + 3, 1, KT * P)
                    up(tg + it * 2, it * 2, 0)
                turn(0, True)
                with eng.Fori(1, n // 2) as it:
                    turn(it, False)
                return lambda i: up(tg + (n - 1), n - 1, 1) if i else gate(ab + (n // 2 - 1), 1)

            def to_x(u, ab, n, norm, gain_col, prev, split_first=True):
                def evac(it, s):
                    if norm is not None:
                        m = it * 2 + s
                        eng.wait_ge(taken[s], ab + it + 2)
                        new_x(m, s, vec[:, bass.ds(gain_col + m, 1)], norm)

                def turn(it, first):
                    for s in range(2):
                        if split_first or s or not first:
                            split(u + it * 2 + s, s, n)
                        prev(s) if first else evac(it - 1, s)
                turn(0, True)
                with eng.Fori(1, KT // 2) as it:
                    turn(it, False)
                return lambda s: evac(KT // 2 - 1, s)

            def ffn(l, f, prev):
                u, ab, tg = l * U_LAYER + B_FFN[f], l * AB_LAYER + AB_FFN[f], l * (2 * FT) + f * FT
                t = gate_up(u, ab, tg, FA, prev)
                t = to_x(u + 2 * FA, ab + FA // 2, FA * P, None, 0, t)
                t = gate_up(u + (2 * FA + KT), ab + (FA // 2 + 4), tg + FA, FB, t)
                eng.wait_ge(small_loaded, l * (16 * SMALL) + 16 * SMALL)
                return to_x(u + (2 * FT + KT), ab + (FT // 2 + 4), FB * P, l * NORMS + (1 + 2 * f), (V_NM, V_NN)[f], t)

            def mix(l, prev):
                u, ab = l * U_LAYER + B_MIX, l * AB_LAYER + AB_MIX
                la, ld = l * (4 * LRU_A), l * (4 * LRU_D)

                def evac_kqv(j):
                    eng.wait_ge(conv_done, l * 16 + j + 1)
                    eng.activation(kqv[:, j, 0:TP], acc[:, 0:TP], ACT.Silu)
                    eng.activation(seq(kqv[:, j, TP:T]),
                                   samples(acc, 0, SLEN), ACT.Silu).then_inc(kqv_done, 1)

                def evac_gate(c):
                    eng.wait_ge(taken[1], ab + (6 + c + 1) + 1)
                    eng.activation(y_s[:, c, :], y_s[:, c, :], ACT.Gelu_apprx_tanh).then_inc(gelu_done, 1)

                def evac_z(c):
                    eng.wait_ge(taken[c % 2], ab + (10 + c // 2 + 1) + 1)
                    eng.activation(z_s[:, c, :], z_s[:, c, :], ACT.Silu).then_inc(silu_z_done, 1)

                def w_ba_high():
                    eng.activation(w_ba_hi[:, :], w_ba[:, :], ACT.Copy).then_inc(wba_hi_done, 1)

                def squares():
                    eng.wait_ge(kqv_done, l * 12 + 13)
                    for j in range(8):
                        eng.activation((sq_k if j < 4 else sq_q)[:, j % 4, :], kqv[:, 4 + j, :], ACT.Square).then_inc(kq_sq_done, 1)

                def tok1():
                    n = l * TOK_D
                    eng.wait_ge(tok_d, n + T_ABS)
                    eng.activation(sp["e"][:, :], sp["abs"][:, :], ACT.Exp, scale=-1.0)
                    eng.activation(ea[:, :], vec[:, V_ALOG:V_ALOG + H], ACT.Exp)
                    eng.activation(tok["beta"][:, :, :], logit[:, :, 0:4], ACT.Sigmoid).then_inc(tok_a, 1)

                def tok2():
                    eng.wait_ge(gsum_done, l + 1)
                    eng.activation(e_g[:, :], PD0[:, 0:32], ACT.Exp)
                    eng.activation(e_gs[0:CH[0], :], PD0[0:CH[0], 32:40], ACT.Exp)
                    eng.activation(e_gt[0:CH[5], :], PD0[0:CH[5], 40:48], ACT.Exp)
                    eng.activation(e_last[:, :], PD0[:, 48:48 + SUM_G], ACT.Exp).then_inc(gexp_done, 1)
                    eng.wait_ge(tok_d, l * TOK_D + T_SS)
                    eng.activation(tok["nk"][:, :, :], kq_ss[:, :, 0:4], ACT.Sqrt, bias=eps[:, 0:1])
                    eng.activation(tok["nq"][:, :, :], kq_ss[:, :, 4:8], ACT.Sqrt, bias=eps[:, 1:2], scale=float(DK)).then_inc(tok_a, 1)

                def lru_gates(c):
                    eng.wait_ge(ri_done, l * 4 + (c + 1))
                    eng.wait_ge(lru_d, ld + c * LRU_D + 1)
                    eng.activation(tiles(lt[:, 1, :]), cols(2), ACT.Sigmoid, bias=vec[:, V_BR + c:V_BR + c + 1]).then_inc(lru_a, 1)
                    eng.activation(tiles(lt[:, 2, :]), cols(3), ACT.Sigmoid, bias=vec[:, V_BI + c:V_BI + c + 1]).then_inc(lru_a, 1)

                def lru_decay(c):
                    eng.wait_ge(lru_a, la + (c * LRU_A + 1))
                    eng.activation(lt[:, 3, :], lt[:, 1, :], ACT.Tanh, scale=lam8[:, c:c + 1]).then_inc(lru_a, 1)
                    eng.activation(lt[:, 1, :], lt[:, 1, :], ACT.Exp, scale=lam8[:, 4 + c:5 + c]).then_inc(lru_a, 1)

                def lru_2(c):
                    eng.wait_ge(lru_d, ld + (c * LRU_D + 3) + 1)
                    eng.activation(lt[:, 0, :], lt[:, 3, :], ACT.Sqrt).then_inc(lru_a, 1)

                def turn(it, first):
                    for s in range(2):
                        split(u + it * 2 + s, s, KT * P)
                        prev(s) if first else evac_kqv(it * 2 - 3 + s)
                turn(0, True)
                root(l * NORMS + 1)
                w_ba_high()
                split(u + 2, 0, KT * P)
                split(u + 3, 1, KT * P)
                evac_kqv(0)
                with eng.Fori(2, 6) as it:
                    turn(it, False)
                for n in range(12, U_MIX + 2):
                    if n < U_MIX:
                        split(u + n, n % 2, KT * P)
                    if n == U_MIX:
                        lru_gates(3)
                    if n < 15:
                        evac_kqv(n - 3)
                    elif n < 22:
                        if n % 2:
                            evac_gate((n - 14) // 2)
                    else:
                        evac_z(n - 22)
                    if n == 14:
                        squares()
                    if n == 15:
                        tok1()
                    if n == 17:
                        tok2()
                    if 18 <= n < U_MIX:
                        if n % 2:
                            lru_2((n - 18) // 2)
                        else:
                            lru_gates((n - 18) // 2)
                            lru_decay((n - 18) // 2)
                decays(l, 0)
                for c in range(NCH + 1):
                    if c:
                        scale_qs(l, c - 1)
                    if c < NCH:
                        first_z(l, c)
                        if c == 0:
                            lru_decay(3)
                        new_y(l, c, 0)
                    if c:
                        o_squares(l, c - 1)
                    if c < NCH:
                        new_y(l, c, 1)
                    if c:
                        o_root(l, c - 1)
                    if c == 0:
                        lru_2(3)
                    if c < NCH:
                        for k in range(2, len(LEVELS[c])):
                            new_y(l, c, k)
                    if c == 1:
                        eng.wait_ge(lru_d, l * (4 * LRU_D) + 4 * LRU_D + 1)
                        for j in range(4):
                            eng.activation(mid_hi[:, 8 + j, :], y_s[:, j, :], ACT.Copy).then_inc(oy_hi_done, 1)
                    if c < NCH - 1:
                        decays(l, c + 1)
                    if c == NCH - 1:
                        split(l * U_LAYER + B_OUT, 0, KT * P)

            def split_o(l):
                eng.wait_ge(og_done, l * NCH + NCH)
                for j in range(4):
                    eng.activation(mid_hi[:, j, :], kqv[:, 8 + j, :], ACT.Copy).then_inc(oy_hi_done, 1)
                eng.wait_ge(seqs_out, l * 48 + 48)

            def decays(l, c):
                n = CH[c]
                eng.wait_ge(dt_done, l * NCH + c + 1)
                eng.activation(head(em, n, n), bank(PB1, n, n), ACT.Exp).then_inc(em_done, 1)

            def first_z(l, c):
                n = CH[c]
                eng.wait_ge(z0_done, l * NCH + c + 1)
                eng.activation(packed(z_c, n, LEVELS[c][0]), lower(bank(PC0, n, n), LEVELS[c][0]), ACT.Copy)
                eng.activation(head(z_m, n, n), bank(PC0, n, n), ACT.Copy).then_inc(z_init, 1)

            def new_y(l, c, k):
                n = CH[c]
                for g in range(2):
                    hs = slice(2 * g, 2 * g + 2)
                    eng.wait_ge(zt_done, at(l, c, k, g))
                    eng.activation(y_c[c % 2][0:n, hs, 0:n], bank((PD0, PD1)[g], n, n)[:, hs], ACT.Copy).then_inc(y_upd, 1)

            def scale_qs(l, c):
                n = CH[c]
                if c == 0:
                    for h in range(H):
                        eng.wait_ge(seg_done, l * H + (h + 1))
                        if h >= 2:
                            eng.wait_ge(kstt_done, l * H + (h - 1))
                        eng.activation(ks_t[:, h % 2, :, :], (PB0, PB1)[h % 2][:, 0:2 * n].rearrange("p (k t) -> p k t", k=2), ACT.Copy).then_inc(kst_done, 1)
                    eng.wait_ge(kstt_done, l * H + H)
                else:
                    eng.wait_ge(qs_done, l * (NCH - 1) + c)
                for h in range(H):
                    ins = eng.activation(qs[0:n, h, :], PA1[0:n, h * P:(h + 1) * P], ACT.Copy, scale=tok_e(c, n, 0)[:, h:h + 1])
                ins.then_inc(qs_scaled, 1)

            def o_squares(l, c):
                n = CH[c]
                eng.wait_ge(o_done, l * NCH + c + 1)
                for h in range(H):
                    ins = eng.activation(qs[0:n, h, :], o_s[0:n, h, :], ACT.Square, accum_out=o_ss[0:n, h:h + 1])
                ins.then_inc(o_sq_done, 1)

            def o_root(l, c):
                n = CH[c]
                eng.wait_ge(o_step, l * (3 * NCH) + (3 * c + 1))
                eng.activation(o_rms[0:n, :], o_ms[0:n, :], ACT.Sqrt, bias=eps[0:n, 0:1]).then_inc(o_rms_done, 1)

            eng.wait_ge(gain_loaded, 16)
            eng.wait_ge(init_done, 1)
            for k in range(KT):
                eng.wait_ge(x_loaded[k], 16)
                new_x(k, k % 2, gain0[:, k:k + 1], 0)
            with eng.Fori(0, DEPTH) as l:
                t = ffn(l, 0, lambda s: root(l * NORMS) if s else None)
                mix(l, t)
                t = to_x(l * U_LAYER + B_OUT, l * AB_LAYER + AB_OUT, KT * P, l * NORMS + 2, V_N2,
                         lambda s: None if s else split_o(l), split_first=False)

                def behind_out(s, last=t):
                    last(s)
                    if s:
                        root(l * NORMS + 2)
                        eng.wait_ge(states_out, l * (16 * 2) + 16 * 2)
                t = ffn(l, 1, behind_out)
                t(0)
                t(1)
            root(DEPTH * NORMS)

        @block.vector
        def _(eng):
            def split(u, s, n):
                eng.wait_ge(w_hi_done, u + 1)
                eng.tensor_tensor(w_lo[:, s, 0:n], w_raw[:, s, 0:n], w_hi[:, s, 0:n].bitcast(F32), ALU.subtract).then_inc(w_lo_done, 1)

            def h_low(m, gain, nh):
                eng.wait_ge(h_hi_done, nh + 1)
                eng.scalar_tensor_tensor(h_lo[:, m, :], x[:, m, :], gain, h_hi[:, m, :].bitcast(F32), ALU.mult, ALU.subtract).then_inc(h_done, 1)

            def new_x(m, s, gain, norm):
                eng.wait_ge(sq_done, norm * KT + m + 1)
                eng.wait_ge(ss_step, norm * SS + m + 3)
                eng.tensor_tensor(ss[:, :], ss[:, :], sq[:, s, :], ALU.add).then_inc(ss_step, 1)
                h_low(m, gain, norm * KT + m)

            def root(norm):
                eng.wait_ge(ss_hi_done, norm + 1)
                eng.tensor_tensor(ss_lo[:, :], ss[:, :], ss_hi[:, :].bitcast(F32), ALU.subtract).then_inc(ss_lo_done, 1)
                eng.wait_ge(rms_done, norm + 1)
                eng.reciprocal(rstd[:, :], rms[:, :]).then_inc(rstd_done, 1)
                eng.wait_ge(rstd_done, norm + 1)

            def gate_up(u, ab, cd, tg, n, prev):
                def gate(v, s):
                    eng.wait_ge(unit_done, v + 3)
                    eng.tensor_tensor(tiles(gate_s[:, s, :]), cols(s), tiles(rstd[:, :]), ALU.mult).then_inc(taken[s], 1)

                def up(v, use, t, k, s):
                    eng.wait_ge(unit_done, v + 3)
                    eng.tensor_tensor(tiles(up_s[:, :]), cols(2 + s), tiles(rstd[:, :]), ALU.mult).then_inc(taken[2 + s], 1)
                    eng.wait_ge(taken[2 + s], use + 2)
                    eng.wait_ge(silu_done, t + 1)
                    eng.tensor_tensor(prod[:, s, :], silu_s[:, s, :], up_s[:, :], ALU.mult).then_inc(prod_done, 1)
                    eng.wait_ge(mid_hi_done, t + 1)
                    eng.tensor_tensor(mid_lo[:, k, :], prod[:, s, :], mid_hi[:, k, :].bitcast(F32), ALU.subtract).then_inc(mid_done, 1)

                def turn(it, first):
                    v = u + it * 4
                    split(v, 0, KT * P)
                    prev(0) if first else gate(v - 2, 1)
                    split(v + 1, 1, KT * P)
                    prev(1) if first else up(v - 1, cd + it - 1, tg + it * 2 - 1, it * 2 - 1, 1)
                    split(v + 2, 0, KT * P)
                    gate(v, 0)
                    split(v + 3, 1, KT * P)
                    up(v + 1, cd + it, tg + it * 2, it * 2, 0)
                turn(0, True)
                with eng.Fori(1, n // 2) as it:
                    turn(it, False)
                return lambda i: up(u + (2 * n - 1), cd + (n // 2 - 1), tg + (n - 1), n - 1, 1) if i else gate(u + (2 * n - 2), 1)

            def to_x(u, ab, n, weight, norm, gain_col, prev, split_first=True):
                def evac(it, s):
                    m = it * 2 + s
                    eng.wait_ge(unit_done, u + m + 3)
                    eng.scalar_tensor_tensor(tiles(x[:, m, :]), cols(s), weight, tiles(x[:, m, :]), ALU.mult, ALU.add).then_inc(taken[s], 1)
                    if norm is not None:
                        eng.wait_ge(taken[s], ab + it + 2)
                        new_x(m, s, vec[:, bass.ds(gain_col + m, 1)], norm)

                def turn(it, first):
                    for s in range(2):
                        if split_first or s or not first:
                            split(u + it * 2 + s, s, n)
                        prev(s) if first else evac(it - 1, s)
                turn(0, True)
                if norm is not None:
                    eng.memset(ss[:, :], 0.0).then_inc(ss_step, 1)
                with eng.Fori(1, KT // 2) as it:
                    turn(it, False)
                return lambda s: evac(KT // 2 - 1, s)

            def ffn(l, f, prev):
                u, ab, cd, tg = l * U_LAYER + B_FFN[f], l * AB_LAYER + AB_FFN[f], l * CD_LAYER + CD_FFN[f], l * (2 * FT) + f * FT
                t = gate_up(u, ab, cd, tg, FA, prev)
                t = to_x(u + 2 * FA, ab + FA // 2, FA * P, 0.5, None, 0, t)
                t = gate_up(u + (2 * FA + KT), ab + (FA // 2 + 4), cd + FA // 2, tg + FA, FB, t)
                eng.wait_ge(taken[1], ab + (FA // 2 + 4) + 1)
                eng.wait_ge(small_loaded, l * (16 * SMALL) + 16 * SMALL)
                return to_x(u + (2 * FT + KT), ab + (FT // 2 + 4), FB * P, 0.5, l * NORMS + (1 + 2 * f), (V_NM, V_NN)[f], t)

            def mix(l, prev):
                u, ab = l * U_LAYER + B_MIX, l * AB_LAYER + AB_MIX
                la, ld = l * (4 * LRU_A), l * (4 * LRU_D)

                def evac_conv(s, m, use, j, out=None):
                    eng.wait_ge(unit_done, u + m + 3)
                    eng.tensor_tensor(cp[:, s, 3:3 + HALF], pair[s][:, 0, 0:HALF], rstd[:, 0:HALF], ALU.mult)
                    eng.tensor_tensor(cp[:, s, 3 + HALF:SAMP0], pair[s][:, 1, 0:TP - HALF], rstd[:, HALF:TP], ALU.mult)
                    eng.tensor_copy(samples(cp[:, s, :], 0, 3), conv_hist[:, j, :, :])
                    eng.tensor_tensor(samples(cp[:, s, :], 3, SLEN),
                                      pair[s][:, 1, TP - HALF:HALF].rearrange("p (b t) -> p b t", b=SEQS),
                                      seq(rstd[:, TP:T]), ALU.mult).then_inc(taken[s], 1)
                    eng.wait_ge(taken[s], use + 2)
                    eng.tensor_copy(conv_new[:, j, 0:3], cp[:, s, TP:TP + 3])
                    eng.tensor_copy(conv_new[:, j, 3:27].rearrange("p (b t) -> p b t", b=SEQS), samples(cp[:, s, :], SLEN, 3))
                    cs = l * (16 * 3) + j * 3
                    w = lambda i: vec[:, bass.ds(V_CQ + j * TAPS + i, 1)]
                    if out is None:
                        eng.wait_ge(pad_done, l + 1)
                        eng.wait_ge(kqv_done, l * 12 + j + 1)
                        eng.tensor_scalar(acc[:, 0:CONV], cp[:, s, 0:CONV], w(0), None, ALU.mult).then_inc(conv_step, 1)
                    else:
                        eng.wait_ge(kqv_done, l * 12 + 13)
                        eng.tensor_scalar(acc[:, 0:CONV], cp[:, s, 0:CONV], w(0), vec[:, V_CB + j - 12:V_CB + j - 11], ALU.mult, ALU.add).then_inc(conv_step, 1)
                    for i in (1, 2):
                        eng.wait_ge(conv_step, cs + i)
                        eng.scalar_tensor_tensor(acc[:, 0:CONV], cp[:, s, i:i + CONV], w(i), acc[:, 0:CONV], ALU.mult, ALU.add).then_inc(conv_step, 1)
                    eng.wait_ge(conv_step, cs + 3)
                    if out is None:
                        eng.scalar_tensor_tensor(acc[:, 0:CONV], cp[:, s, 3:3 + CONV], w(3), acc[:, 0:CONV], ALU.mult, ALU.add).then_inc(conv_done, 1)
                    else:
                        eng.scalar_tensor_tensor(out[:, 0:TP], cp[:, s, 3:3 + TP], w(3), acc[:, 0:TP], ALU.mult, ALU.add)
                        eng.scalar_tensor_tensor(seq(out[:, TP:T]), samples(cp[:, s, :], 3, SLEN), w(3),
                                                 samples(acc, 0, SLEN), ALU.mult, ALU.add).then_inc(conv_done, 1)

                def scaled(s, m, dst):
                    eng.wait_ge(unit_done, u + m + 3)
                    eng.tensor_tensor(tiles(dst), cols(s), tiles(rstd[:, :]), ALU.mult).then_inc(taken[s], 1)

                count = [0]

                def step(ins):
                    count[0] += 1
                    ins.then_inc(tok_d, 1)
                    eng.wait_ge(tok_d, l * TOK_D + count[0])

                def tok1a():
                    lp = PC0[:, 0:NCH * 8].rearrange("p (c j) -> p c j", c=NCH)
                    eng.wait_ge(logit_done, l + 1)
                    for n, cs in PARTS:
                        ins = eng.tensor_copy(logit[0:n, cs, :], lp[0:n, cs, :])
                    step(ins)
                    y, a = sp["y"], sp["abs"]
                    eng.tensor_tensor(y[:, 0:NCH * H].rearrange("p (c h) -> p c h", c=NCH), logit[:, :, 4:8], bh(vec[:, V_DT:V_DT + H], NCH), ALU.add)
                    step(eng.tensor_scalar(y[:, NCH * H:SP_N], vec[:, V_LAM:V_LAM + 4], -1.0, None, ALU.mult))
                    step(eng.scalar_tensor_tensor(a[:, :], y[:, :], -1.0, y[:, :], ALU.mult, ALU.max))
                    assert count[0] == T_ABS

                def tok1b():
                    y, e, z, z2, p, out = (sp[n] for n in ("y", "e", "z", "z2", "p", "out"))
                    den = out
                    eng.wait_ge(tok_a, l * 2 + 1)
                    step(eng.tensor_scalar(den[:, :], e[:, :], 2.0, None, ALU.add))
                    step(eng.reciprocal(den[:, :], den[:, :]))
                    step(eng.tensor_tensor(z[:, :], e[:, :], den[:, :], ALU.mult))
                    step(eng.tensor_tensor(z2[:, :], z[:, :], z[:, :], ALU.mult))
                    step(eng.tensor_scalar(p[:, :], z2[:, :], ATANH[0], None, ALU.mult))
                    for k in ATANH[1:]:
                        step(eng.scalar_tensor_tensor(p[:, :], p[:, :], k, z2[:, :], ALU.add, ALU.mult))
                    step(eng.scalar_tensor_tensor(p[:, :], p[:, :], 1.0, z[:, :], ALU.add, ALU.mult))
                    step(eng.tensor_scalar(p[:, :], p[:, :], 2.0, None, ALU.mult))
                    step(eng.scalar_tensor_tensor(out[:, :], y[:, :], 0.0, p[:, :], ALU.max, ALU.add))
                    g = tok["g"]
                    eng.tensor_scalar(lam8[:, 0:4], out[:, NCH * H:SP_N], 8.0, None, ALU.mult)
                    eng.tensor_scalar(lam8[:, 4:8], out[:, NCH * H:SP_N], -8.0, None, ALU.mult)
                    step(eng.scalar_tensor_tensor(g[:, :, :], out[:, 0:NCH * H].rearrange("p (c h) -> p c h", c=NCH), -1.0, bh(ea[:, :], NCH), ALU.mult, ALU.mult))
                    step(eng.tensor_copy(g_hi[:, :, :], g[:, :, :]))
                    eng.tensor_tensor(g_lo[:, :, :], g[:, :, :], g_hi[:, :, :].bitcast(F32), ALU.subtract)
                    step(eng.tensor_tensor(g_seg[0:TS, :, :], bc(mask[0:TS, M_GTS, IND], H), bh(g[0:TS, 0, :], SEGS), ALU.mult))
                    assert count[0] == T_G

                def tok2():
                    kp = PC1[:, 0:NCH * 8].rearrange("p (c j) -> p c j", c=NCH)
                    eng.wait_ge(kq_sum_done, l + 1)
                    for n, cs in PARTS:
                        ins = eng.tensor_copy(kq_ss[0:n, cs, :], kp[0:n, cs, :])
                    step(ins)
                    assert count[0] == T_SS
                    eng.wait_ge(tok_a, l * 2 + 2)
                    t = lambda n: tok[n][:, :, :]
                    eng.reciprocal(t("rq"), t("nq"))
                    step(eng.reciprocal(t("rk"), t("nk")))
                    eng.tensor_tensor(t("rq2"), t("rq"), t("rq"), ALU.mult)
                    step(eng.tensor_tensor(t("bk2"), t("rk"), t("rk"), ALU.mult))
                    step(eng.tensor_tensor(t("bk2"), t("bk2"), t("beta"), ALU.mult))
                    step(eng.tensor_scalar(t("nb"), t("bk2"), -1.0, None, ALU.mult))
                    assert count[0] == TOK_D

                def lru_1(c):
                    n = [ld + c * LRU_D]
                    eng.wait_ge(lru_a, la + (c * LRU_A + 4))
                    eng.tensor_tensor(lt[:, 2, :], lt[:, 2, :], xc(c), ALU.mult).then_inc(lru_d, 1)
                    eng.tensor_tensor(lt[:, 0, :], lt[:, 1, :], lt[:, 1, :], ALU.mult).then_inc(lru_d, 1)
                    eng.wait_ge(lru_d, n[0] + 3)
                    eng.scalar_tensor_tensor(lt[:, 3, :], lt[:, 0, :], 1.0, lt[:, 3, :], ALU.add, ALU.mult).then_inc(lru_d, 1)

                def lru_2(c):
                    base = ld + c * LRU_D
                    start = lambda i: seq(lt[:, i, TP:T])[:, :, 0]
                    eng.wait_ge(lru_a, la + (c * LRU_A + 5))
                    eng.tensor_tensor(lt[:, 2, :], lt[:, 2, :], lt[:, 0, :], ALU.mult).then_inc(lru_d, 1)
                    eng.tensor_tensor(h_start[:, :], start(1), lru_h0[:, c, :], ALU.mult).then_inc(lru_d, 1)
                    eng.wait_ge(lru_d, base + 6)
                    eng.tensor_tensor(start(2), start(2), h_start[:, :], ALU.add).then_inc(lru_d, 1)
                    eng.memset(start(1), 0.0).then_inc(lru_d, 1)
                    eng.wait_ge(lru_d, base + 8)
                    eng.tensor_tensor_scan(lt[:, 3, :], lt[:, 1, :], lt[:, 2, :], 0.0, ALU.mult, ALU.add).then_inc(lru_d, 1)
                    eng.wait_ge(lru_d, base + 9)
                    eng.tensor_copy(lru_new[:, c, 0:1], lt[:, 3, TP - 1:TP]).then_inc(lru_d, 1)
                    eng.tensor_copy(lru_new[:, c, 1:9], seq(lt[:, 3, TP:T])[:, :, SLEN - 1]).then_inc(lru_d, 1)
                    eng.wait_ge(gelu_done, l * 4 + (c + 1))
                    eng.tensor_tensor(y_s[:, c, :], y_s[:, c, :], lt[:, 3, :], ALU.mult).then_inc(lru_d, 1)

                prev(0)
                prev(1)
                root(l * NORMS + 1)
                eng.memset(cp[:, :, 0:3], 0.0).then_inc(pad_done, 1)
                eng.wait_ge(wba_hi_done, l + 1)
                eng.tensor_tensor(w_ba_lo[:, :], w_ba[:, :], w_ba_hi[:, :].bitcast(F32), ALU.subtract).then_inc(wba_done, 1)
                with eng.Fori(0, 6) as it:
                    for s in range(2):
                        evac_conv(s, it * 2 + s, ab + it, it * 2 + s)
                eng.wait_ge(lg_done, l + 1)
                eng.tensor_tensor(tiles(z_s[0:8, 0, :]), pair[2][0:8, :, 0:HALF], tiles(rstd[0:8, :]), ALU.mult).then_inc(lg_scaled, 1)
                for m in range(12, U_MIX):
                    use = ab + m // 2
                    if m < 20:
                        if m % 2 == 0:
                            c = (m - 12) // 2
                            if c == 3:
                                eng.wait_ge(ri_done, l * 4 + 1)
                            evac_conv(0, m, use, 12 + c, xc(c))
                        else:
                            scaled(1, m, y_s[:, (m - 12) // 2, :])
                    else:
                        if m == 20:
                            eng.wait_ge(kq_sum_done, l + 1)
                        scaled(m % 2, m, z_s[:, m - 20, :])
                    if m == 12:
                        tok1a()
                    if m == 13:
                        tok1b()
                    if m == 15:
                        tok2()
                    if 16 <= m < 22:
                        (lru_2 if m % 2 else lru_1)((m - 16) // 2)
                eng.memset(s_p[:, :, :], 0.0).then_inc(s_done, 1)
                decays(l, 0)
                for c in range(NCH + 1):
                    new, old = c < NCH, c > 0
                    if new:
                        start(l, c)
                    if old:
                        residual(l, c - 1)
                    if new:
                        masked(l, c)
                    if new:
                        scale_v(l, c)
                    if old:
                        new_v(l, c - 1)
                    level(l, c, 0)
                    if old:
                        update(l, c - 1)
                    level(l, c, 1)
                    if old:
                        o_mean(l, c - 1)
                    if c == 0:
                        lru_1(3)
                        lru_2(3)
                        eng.wait_ge(silu_z_done, l * 4 + 4)
                    level(l, c, 2)
                    if old:
                        o_norm(l, c - 1)
                    level(l, c, 3)
                    if old:
                        o_gate(l, c - 1)
                    level(l, c, 4)
                    level(l, c, 5)
                    if c == 1:
                        for j in range(4):
                            eng.wait_ge(oy_hi_done, l * KT + (j + 1))
                            eng.tensor_tensor(mid_lo[:, 8 + j, :], y_s[:, j, :], mid_hi[:, 8 + j, :].bitcast(F32), ALU.subtract).then_inc(oy_done, 1)
                    if c < NCH - 1:
                        decays(l, c + 1)
                    if c == NCH - 1:
                        split(l * U_LAYER + B_OUT, 0, KT * P)

            def split_o(l):
                for j in range(4):
                    eng.wait_ge(oy_hi_done, l * KT + (j + 5))
                    eng.tensor_tensor(mid_lo[:, j, :], kqv[:, 8 + j, :], mid_hi[:, j, :].bitcast(F32), ALU.subtract).then_inc(oy_done, 1)
                eng.wait_ge(oy_done, l * KT + KT)
                eng.wait_ge(seqs_out, l * 48 + 48)

            def tk(name, c):
                return tok[name][0:CH[c], c, :]

            def decays(l, c):
                n, lc = CH[c], l * NCH + c
                tri = bh(mask[0:n, M_TRIS if c == 0 else M_TRI, 0:n], H)
                eng.wait_ge(em_done, lc + 1)
                eng.tensor_tensor(head(em, n, n), head(em, n, n), tri, ALU.mult).then_inc(emm_done, 1)

            def start(l, c):
                n, lc, y = CH[c], l * NCH + c, y_c[c % 2]
                eng.wait_ge(emm_done, lc + 1)
                eng.wait_ge(kq_done, lc + 1)
                for h in range(H):
                    ins = eng.scalar_tensor_tensor(nt[0:n, h, 0:n], PC0[0:n, h * n:(h + 1) * n], tok["bk2"][0:n, c, h:h + 1],
                                                   em[0:n, h, 0:n], ALU.mult, ALU.mult)
                ins.then_inc(nt_done, 1)
                eng.wait_ge(nt_done, lc + 1)
                eng.tensor_tensor(head(y, n, n), head(nt, n, n), bh(mask[0:n, M_L1T, 0:n], H), ALU.mult).then_inc(y0_tmp, 1)
                eng.wait_ge(y0_tmp, lc + 1)
                eng.tensor_tensor(head(y, n, n), bh(mask[0:n, M_ID, 0:n], H), head(y, n, n), ALU.subtract).then_inc(y0_done, 1)

            def masked(l, c):
                n, lc = CH[c], l * NCH + c
                eng.tensor_tensor(head(attn[c % 2], n, n), bank(PC1, n, n), head(em, n, n), ALU.mult).then_inc(attn_done, 1)
                eng.wait_ge(kt_done, lc + 1)
                eng.tensor_tensor(kdec[c % 2][0:n, :, :], bank(PD1, n, P), bc(tok_e(c, n, 1), P), ALU.mult).then_inc(kdec_done, 1)

            def scale_v(l, c):
                n, lc = CH[c], l * NCH + c
                eng.wait_ge(vt_done, lc + 1)
                eng.tensor_tensor(vn_s[c % 2][0:n, :, :], bank(PD0, n, P), bc(tk("nk", c), P), ALU.mult).then_inc(vscaled_done, 1)

            def level(l, c, k):
                if c == NCH or k >= len(LEVELS[c]):
                    return
                n, s = CH[c], LEVELS[c][k]
                m = mask[0:n, LEVEL_MASK[s], 0:n].rearrange("p (b t) -> p b t", t=2 * s)[:, :, 0:s]
                for g in range(2):
                    hs = slice(2 * g, 2 * g + 2)
                    eng.wait_ge(nz_done, at(l, c, k, g))
                    eng.tensor_tensor(packed(p_c, n, s)[:, hs], packed((PC0, PC1)[g], n, s)[:, hs],
                                      m.unsqueeze(1).to_broadcast([n, 2, n // (2 * s), s]), ALU.mult).then_inc(p_done, 1)
                for g in range(2):
                    hs = slice(2 * g, 2 * g + 2)
                    if k == 0:
                        eng.wait_ge(z_init, l * NCH + c + 1)
                    else:
                        eng.wait_ge(z_upd, at(l, c, k - 1, g))
                    eng.wait_ge(zp_done, at(l, c, k, g))
                    z = lower(head(z_m, n, n), s)[:, hs]
                    eng.tensor_tensor(z, z, packed((PC0, PC1)[g], n, s)[:, hs], ALU.subtract).then_inc(z_upd, 1)

            def residual(l, c):
                n, lc = CH[c], l * NCH + c
                if c == 0:
                    eng.wait_ge(kstt_done, l * H + H)
                else:
                    eng.wait_ge(ks_done, l * (NCH - 1) + c)
                eng.wait_ge(vscaled_done, lc + 1)
                for h in range(H):
                    ins = eng.scalar_tensor_tensor(r_s[0:n, h, :], PA0[0:n, h * P:(h + 1) * P], tok_e(c, n, 0)[:, h:h + 1],
                                                   vn_s[c % 2][0:n, h, :], ALU.mult, ALU.subtract)
                ins.then_inc(r_done, 1)

            def new_v(l, c):
                n, lc = CH[c], l * NCH + c
                eng.wait_ge(zr_done, lc + 1)
                eng.tensor_tensor(v_new[0:n, :, :], bank(PB0, n, P), bc(tk("nb", c), P), ALU.mult).then_inc(vnew_done, 1)

            def update(l, c):
                n, lc = CH[c], l * NCH + c
                if c:
                    eng.wait_ge(kv_done, l * (NCH - 1) + c)
                    for h in range(H):
                        at = (c - 1) * H + h
                        ins = eng.scalar_tensor_tensor(s_p[:, h, :], s_p[:, h, :], e_last[:, at:at + 1],
                                                       PB1[:, h * P:(h + 1) * P], ALU.mult, ALU.add)
                    ins.then_inc(s_done, 1)
                    eng.wait_ge(s_done, l * NCH + (c + 1))
                eng.wait_ge(av_done, lc + 1)
                eng.wait_ge(qs_scaled, lc + 1)
                eng.tensor_tensor(o_s[0:n, :, :], qs[0:n, :, :], bank(PA0, n, P), ALU.add).then_inc(o_done, 1)
                if c == 0:
                    eng.wait_ge(vnew_done, lc + 1)
                    segments(l, 0)

            def o_mean(l, c):
                n = CH[c]
                eng.wait_ge(o_sq_done, l * NCH + c + 1)
                eng.scalar_tensor_tensor(o_ms[0:n, :], o_ss[0:n, :], 1.0 / DK, tk("rq2", c), ALU.mult, ALU.mult).then_inc(o_step, 1)
                if c == 0:
                    segments(l, 1)

            def o_norm(l, c):
                n, lc, st = CH[c], l * NCH + c, l * (3 * NCH) + 3 * c
                eng.wait_ge(o_rms_done, lc + 1)
                eng.reciprocal(o_rec[0:n, :], o_rms[0:n, :]).then_inc(o_step, 1)
                eng.wait_ge(o_step, st + 2)
                eng.tensor_tensor(o_fac[0:n, :], o_rec[0:n, :], tk("rq", c), ALU.mult).then_inc(o_step, 1)
                eng.wait_ge(o_step, st + 3)
                eng.tensor_tensor(o_s[0:n, :, :], o_s[0:n, :, :], bc(o_fac[0:n, :], P), ALU.mult).then_inc(on_done, 1)
                if c == 0:
                    segments(l, 2)

            def o_gate(l, c):
                n, t0 = CH[c], T0[c]
                eng.wait_ge(ot_done, l * NCH + c + 1)
                eng.scalar_tensor_tensor(kqv[:, 8:12, t0:t0 + n], bank(turned(c), P, n), vec[:, V_ON:V_ON + 1],
                                         z_s[:, :, t0:t0 + n], ALU.mult, ALU.mult).then_inc(og_done, 1)
                if c == 0:
                    segments(l, 3)

            def segments(l, h):
                n = CH[0]

                def spread_v(h):
                    eng.tensor_tensor(vseg[0:n, :, :], bh(v_new[0:n, h, :], SEGS), bc(mask[0:n, M_GTS, IND], P), ALU.mult).then_inc(vseg_done, 1)
                if h == 0:
                    spread_v(0)
                eng.wait_ge(segkv_done, l * H + (h + 1))
                if h < H - 1:
                    spread_v(h + 1)
                for s in range(SEGS):
                    at = (NCH - 1) * H + s * H + h
                    ins = eng.scalar_tensor_tensor(seg_state(h, s), seg_state(h, s), e_last[:, at:at + 1],
                                                   (PB0, PB1)[s // 4][:, (s % 4) * P:(s % 4 + 1) * P], ALU.mult, ALU.add)
                ins.then_inc(seg_s_done, 1)

            for t in taken:
                eng.sem_inc(t, 1)
            eng.sem_inc(lru_d, 1)
            eng.memset(eps[:, 0:1], EPS)
            eng.memset(eps[:, 1:2], EPS * DK)
            eng.memset(eps[:, 2:3], 1.0)
            eng.memset(logit[:, :, :], 0.0)
            eng.memset(kq_ss[:, :, :], 0.0).then_inc(init_done, 1)
            eng.wait_ge(init_done, 1)
            eng.tensor_copy(ones_r[:, :], eps[:, 2:3].to_broadcast([P, P])).then_inc(init_done, 1)
            eng.memset(ss[:, :], 0.0).then_inc(ss_step, 1)
            eng.wait_ge(gain_loaded, 16)
            for k in range(KT):
                eng.wait_ge(x_loaded[k], 16)
                new_x(k, k % 2, gain0[:, k:k + 1], 0)
            eng.wait_ge(mask_loaded, 16)
            eng.wait_ge(init_done, 2)
            with eng.Fori(0, DEPTH) as l:
                t = ffn(l, 0, lambda s: root(l * NORMS) if s else None)
                mix(l, t)
                t = to_x(l * U_LAYER + B_OUT, l * AB_LAYER + AB_OUT, KT * P, 1.0, l * NORMS + 2, V_N2,
                         lambda s: None if s else split_o(l), split_first=False)

                def behind_out(s, last=t):
                    last(s)
                    if s:
                        root(l * NORMS + 2)
                        eng.wait_ge(states_out, l * (16 * 2) + 16 * 2)
                t = ffn(l, 1, behind_out)
                t(0)
                t(1)
            root(DEPTH * NORMS)
            for k in range(KT):
                eng.scalar_tensor_tensor(x[:, k, :], x[:, k, :], vec[:, V_NN + k:V_NN + k + 1], rstd[:, :], ALU.mult, ALU.mult).then_inc(y_out, 1)

        @block.tensor
        def _(eng):
            def product(pr, s, nk, hi, lo, u, each=None, tiles_at=None):
                eng.wait_ge(w_lo_done, u + 3)
                for k in range(nk):
                    if each:
                        each(k)
                    at = tiles_at[k] if tiles_at else k
                    w = slice(k * P, (k + 1) * P)
                    for a, b in ((w_hi, hi), (w_hi, lo), (w_lo, hi)):
                        for half in range(2):
                            ins = eng.matmul(pair[pr][:, half, 0:HALF], a[:, s, w], b[:, at, half * HALF:(half + 1) * HALF],
                                             start=k == 0 and b is hi and a is w_hi, stop=k == nk - 1 and a is w_lo)
                ins.then_inc(unit_done, 1)

            def sum_squares(norm):
                eng.wait_ge(ss_lo_done, norm + 1)
                for part in (ss_hi, ss_lo):
                    for half in range(2):
                        ins = eng.matmul(pair[3][:, half, 0:HALF], ones_r[:, :], part[:, half * HALF:(half + 1) * HALF],
                                         start=part is ss_hi, stop=part is ss_lo)
                ins.then_inc(ss_done, 1)

            def gate_up(u, ab, cd, n, norm=None, behind=None):
                def turn(it, first):
                    v = u + it * 4
                    for s in range(2):
                        eng.wait_ge(taken[s], ab + it + 1)
                        product(s, 0, KT, h_hi, h_lo, v + 2 * s, (lambda k: eng.wait_ge(h_done, norm * KT + (k + 1))) if first and s == 0 and norm is not None else None)
                        if first and s == 0 and behind:
                            behind()
                        if first and s == 1 and norm is not None:
                            eng.wait_ge(rms_done, norm + 1)
                        eng.wait_ge(taken[2 + s], cd + it + 1)
                        product(2 + s, 1, KT, h_hi, h_lo, v + 2 * s + 1)
                turn(0, True)
                with eng.Fori(1, n // 2) as it:
                    turn(it, False)

            def to_x(u, ab, nk, wait0, tiles_at=None):
                def turn(it, first):
                    for s in range(2):
                        eng.wait_ge(taken[s], ab + it + 1)
                        product(s, s, nk, mid_hi, mid_lo, u + it * 2 + s, wait0 if first and s == 0 else None, tiles_at)
                turn(0, True)
                with eng.Fori(1, KT // 2) as it:
                    turn(it, False)

            def ffn(l, f, norm, behind=None):
                u, ab, cd, tg = l * U_LAYER + B_FFN[f], l * AB_LAYER + AB_FFN[f], l * CD_LAYER + CD_FFN[f], l * (2 * FT) + f * FT
                gate_up(u, ab, cd, FA, norm, behind)
                to_x(u + 2 * FA, ab + FA // 2, FA, lambda k: eng.wait_ge(mid_done, tg + (k + 1)))
                gate_up(u + (2 * FA + KT), ab + (FA // 2 + 4), cd + FA // 2, FB)
                to_x(u + (2 * FT + KT), ab + (FT // 2 + 4), FB, lambda k: eng.wait_ge(mid_done, tg + (FA + k + 1)))

            def mix(l):
                u, ab = l * U_LAYER + B_MIX, l * AB_LAYER + AB_MIX
                norm = l * NORMS + 1
                eng.wait_ge(taken[0], ab + 1)
                product(0, 0, KT, h_hi, h_lo, u, lambda k: eng.wait_ge(h_done, norm * KT + (k + 1)))
                sum_squares(norm)
                eng.wait_ge(taken[1], ab + 1)
                product(1, 1, KT, h_hi, h_lo, u + 1)
                with eng.Fori(1, 6) as it:
                    for s in range(2):
                        eng.wait_ge(taken[s], ab + it + 1)
                        product(s, s, KT, h_hi, h_lo, u + it * 2 + s)

                def logits():
                    eng.wait_ge(wba_done, l + 1)
                    for k in range(KT):
                        for a, b in ((w_ba_hi, h_hi), (w_ba_hi, h_lo), (w_ba_lo, h_hi)):
                            for half in range(2):
                                ins = eng.matmul(pair[2][0:8, half, 0:HALF], a[:, k * 8:k * 8 + 8], b[:, k, half * HALF:(half + 1) * HALF],
                                                 start=k == 0 and a is w_ba_hi and b is h_hi, stop=k == KT - 1 and a is w_ba_lo)
                    ins.then_inc(lg_done, 1)

                def turn_logits():
                    eng.wait_ge(lg_scaled, l + 1)
                    for c in range(NCH):
                        n, t0 = CH[c], T0[c]
                        ins = eng.matmul(PC0[0:n, c * 8:c * 8 + 8], z_s[0:8, 0, t0:t0 + n], mask[0:8, M_ID, 0:8], start=True, stop=True)
                    ins.then_inc(logit_done, 1)

                def kq_sums():
                    for j in range(8):
                        eng.wait_ge(kq_sq_done, l * 8 + (j + 1))
                        for c in range(NCH):
                            n, t0 = CH[c], T0[c]
                            ins = eng.matmul(PC1[0:n, c * 8 + j:c * 8 + j + 1], (sq_k if j < 4 else sq_q)[:, j % 4, t0:t0 + n],
                                             mask[:, M_ONE, 0:1], start=True, stop=True)
                    ins.then_inc(kq_sum_done, 1)

                def g_sums():
                    g, ns, nr = tok["g"], CH[0], CH[5]
                    eng.wait_ge(tok_d, l * TOK_D + T_G)
                    g4 = g[:, 1:5, :].rearrange("p c h -> p (c h)")
                    mm = lambda out, a, b: eng.matmul(out, a, b, start=True, stop=True)
                    mm(PD0[:, 0:16], mask[:, M_TRI, :], g4)
                    mm(PD0[:, 16:32], mask[:, M_GT, :], g4)
                    mm(PD0[0:ns, 32:36], mask[0:ns, M_TRIS, 0:ns], g[0:ns, 0, :])
                    mm(PD0[0:ns, 36:40], mask[0:ns, M_GTS, 0:ns], g[0:ns, 0, :])
                    mm(PD0[0:nr, 40:44], mask[0:nr, M_TRI, 0:nr], g[0:nr, 5, :])
                    mm(PD0[0:nr, 44:48], mask[0:nr, M_GT, 0:nr], g[0:nr, 5, :])
                    mm(PD0[:, 48:64], mask[:, M_ONE, :], g4)
                    mm(PD0[:, 64:68], mask[0:nr, M_ONE, :], g[0:nr, 5, :])
                    mm(PD0[:, 68:68 + SEGS * H], mask[0:ns, M_ONE, :], g_seg[0:ns, :, :].rearrange("p s h -> p (s h)")).then_inc(gsum_done, 1)

                def ri(c):
                    eng.wait_ge(conv_done, l * 16 + (12 + c + 1))
                    if c:
                        eng.wait_ge(lru_a, l * (4 * LRU_A) + ((c - 1) * LRU_A + 2))
                    else:
                        eng.wait_ge(gexp_done, l + 1)
                        eng.wait_ge(tok_d, l * TOK_D + T_SS)
                    for g in range(2):
                        for half in range(2):
                            ins = eng.matmul(pair[2 + g][:, half, 0:HALF], w_ri[:, c, g, :], xc(c)[:, half * HALF:(half + 1) * HALF], start=True, stop=True)
                    ins.then_inc(ri_done, 1)

                logits()
                for n in range(12, U_MIX):
                    eng.wait_ge(taken[n % 2], ab + n // 2 + 1)
                    product(n % 2, n % 2, KT, h_hi, h_lo, u + n)
                    if n == 12:
                        turn_logits()
                    if n == 15:
                        kq_sums()
                        g_sums()
                    if n >= 16 and n % 2 == 0:
                        ri((n - 16) // 2)
                decays(l, 0)
                for c in range(NCH + 1):
                    new, old = c < NCH, c > 0
                    if new:
                        start(l, c)
                    if old:
                        old_state(l, c - 1)
                    if new:
                        first_z(l, c)
                    if old:
                        z_r(l, c - 1)
                    level(l, c, 0)
                    if old:
                        update(l, c - 1)
                    level(l, c, 1)
                    if c == 1:
                        segments(l, 1)
                    level(l, c, 2)
                    if c == 1:
                        segments(l, 2)
                    level(l, c, 3)
                    if old:
                        o_turned(l, c - 1)
                    if c < NCH - 1:
                        decays(l, c + 1)
                    level(l, c, 4)
                    level(l, c, 5)
                    if new:
                        turn_z(l, c, len(LEVELS[c]) - 1)

            count = eng.alloc_register("awaited_count")

            def wait(c, sem, value):
                if CH[c] < P:
                    eng.reg_mov(count, value)
                    eng.wait_ge(init_done, 2)
                    value = count
                eng.wait_ge(sem, value)

            def mm(out, a, b):
                return eng.matmul(out, a, b, start=True, stop=True)

            def start(l, c):
                n, lc, t0 = CH[c], l * NCH + c, T0[c]
                tt = slice(t0, t0 + n)
                if c == 0:
                    wait(c, lru_a, l * (4 * LRU_A) + (3 * LRU_A + 2))
                else:
                    wait(c, z_upd, l * (2 * LV) + 2 * lv(c, 0))
                for h in range(H):
                    mm(PC0[0:n, h * n:(h + 1) * n], kqv[:, 4 + h, tt], kqv[:, 4 + h, tt])
                for h in range(H):
                    ins = mm(PC1[0:n, h * n:(h + 1) * n], kqv[:, 4 + h, tt], kqv[:, 8 + h, tt])
                ins.then_inc(kq_done, 1)
                if c:
                    wait(c, y_upd, l * (2 * LV) + 2 * lv(c, 0))
                for h in range(H):
                    ins = eng.transpose(PD1[0:n, h * P:(h + 1) * P], kqv[:, 4 + h, tt], mask[:, M_ID, :])
                ins.then_inc(kt_done, 1)

            def decays(l, c):
                n, lc = CH[c], l * NCH + c
                if c == 0:
                    wait(c, taken[1], l * AB_LAYER + AB_MIX + (U_MIX // 2 + 1))
                elif c == 2:
                    wait(c, seg_s_done, l * H + H)
                elif c > 2:
                    wait(c, s_done, l * NCH + c - 1)
                wait(c, grhs_done, lc + 1)
                for part in (gr_hi, gr_lo):
                    ins = eng.matmul(bank(PB1, n, n), after_r[0:n, c == 0, 0:n], head(part, n, n), start=part is gr_hi, stop=part is gr_lo)
                ins.then_inc(dt_done, 1)

            def first_z(l, c):
                n, lc, t0 = CH[c], l * NCH + c, T0[c]
                for h in range(H):
                    ins = eng.transpose(PD0[0:n, h * P:(h + 1) * P], kqv[:, h, t0:t0 + n], mask[:, M_ID, :])
                ins.then_inc(vt_done, 1)
                wait(c, y0_done, lc + 1)
                for h in range(H):
                    ins = eng.transpose(PC0[0:n, h * n:(h + 1) * n], y_c[c % 2][0:n, h, 0:n], mask[0:n, M_ID, 0:n])
                ins.then_inc(z0_done, 1)

            def level(l, c, k):
                if c == NCH or k >= len(LEVELS[c]):
                    return
                n, s = CH[c], LEVELS[c][k]
                if k:
                    turn_z(l, c, k - 1)
                    z = lower(head(z_m, n, n), s)
                else:
                    wait(c, z_init, l * NCH + c + 1)
                    wait(c, attn_done, l * NCH + c + 1)
                    z = packed(z_c, n, s)
                for g in range(2):
                    for h in (2 * g, 2 * g + 1):
                        ins = mm(packed((PC0, PC1)[g], n, s)[:, h], nt[0:n, h, 0:n], z[:, h])
                    ins.then_inc(nz_done, 1)
                for g in range(2):
                    wait(c, p_done, at(l, c, k, g))
                    if k:
                        wait(c, y_upd, at(l, c, k - 1, g))
                    for h in (2 * g, 2 * g + 1):
                        ins = mm(packed((PC0, PC1)[g], n, s)[:, h], y_c[c % 2][0:n, h, 0:n], packed(p_c, n, s)[:, h])
                    ins.then_inc(zp_done, 1)

            def turn_z(l, c, k):
                n = CH[c]
                for g in range(2):
                    wait(c, z_upd, at(l, c, k, g))
                    if k:
                        wait(c, y_upd, at(l, c, k - 1, g))
                    else:
                        wait(c, (vscaled_done, kdec_done)[g], l * NCH + c + 1)
                    for h in (2 * g, 2 * g + 1):
                        ins = eng.transpose((PD0, PD1)[g][0:n, h * n:(h + 1) * n], z_m[0:n, h, 0:n], mask[0:n, M_ID, 0:n])
                    ins.then_inc(zt_done, 1)

            def old_state(l, c):
                n, t0 = CH[c], T0[c]
                if c:
                    wait(c, s_done, l * NCH + c)
                    wait(c, og_done, l * NCH + c)
                    for h in range(H):
                        ins = mm(PA0[0:n, h * P:(h + 1) * P], kqv[:, 4 + h, t0:t0 + n], s_p[:, h, :])
                    ins.then_inc(ks_done, 1)
                    for h in range(H):
                        ins = mm(PA1[0:n, h * P:(h + 1) * P], kqv[:, 8 + h, t0:t0 + n], s_p[:, h, :])
                    ins.then_inc(qs_done, 1)
                    return
                wait(c, em_done, l * NCH + c + 2)
                wait(c, s0a_loaded, l * 16 + 16)
                wait(c, s0b_loaded, l * 16 + 16)

                def turn_head(h):
                    wait(c, kst_done, l * H + (h + 1))
                    eng.transpose(PA0[0:n, h * P:(h + 1) * P], ks_t[:, h % 2, 0, :], mask[:, M_ID, :])
                    eng.transpose(PA1[0:n, h * P:(h + 1) * P], ks_t[:, h % 2, 1, :], mask[:, M_ID, :]).then_inc(kstt_done, 1)
                for h in range(H):
                    out = (PB0, PB1)[h % 2][:, 0:2 * n].rearrange("p (k t) -> p k t", k=2)
                    for s in range(SEGS):
                        a, b = s * SLEN, (s + 1) * SLEN
                        ins = mm(out[:, :, a:b], seg_state(h, s), kqv[:, 4 + h:9 + h:4, t0 + a:t0 + b])
                    ins.then_inc(seg_done, 1)
                    if h:
                        turn_head(h - 1)
                turn_head(3)

            def z_r(l, c):
                n = CH[c]
                wait(c, r_done, l * NCH + c + 1)
                wait(c, y_upd, l * (2 * LV) + 2 * lv(c + 1, 0))
                for h in range(H):
                    ins = mm(PB0[0:n, h * P:(h + 1) * P], y_c[c % 2][0:n, h, 0:n], r_s[0:n, h, :])
                ins.then_inc(zr_done, 1)

            def update(l, c):
                n = CH[c]
                wait(c, vnew_done, l * NCH + c + 1)
                if c:
                    for h in range(H):
                        ins = mm(PB1[:, h * P:(h + 1) * P], kdec[c % 2][0:n, h, :], v_new[0:n, h, :])
                    ins.then_inc(kv_done, 1)
                for h in range(H):
                    ins = mm(PA0[0:n, h * P:(h + 1) * P], attn[c % 2][0:n, h, 0:n], v_new[0:n, h, :])
                ins.then_inc(av_done, 1)
                if c == 0:
                    segments(l, 0)

            def segments(l, h):
                i, n = l * H + (h + 1), CH[0]
                wait(0, vseg_done, i)
                if h:
                    wait(0, seg_s_done, i - 1)
                mm(PB0[:, :], kdec[0][0:n, h, :], vseg[0:n, 0:4, :])
                mm(PB1[:, :], kdec[0][0:n, h, :], vseg[0:n, 4:8, :]).then_inc(segkv_done, 1)

            def o_turned(l, c):
                n = CH[c]
                wait(c, on_done, l * NCH + c + 1)
                for h in range(H):
                    ins = eng.transpose(turned(c)[:, h * n:(h + 1) * n], o_s[0:n, h, :], mask[0:n, M_ID, 0:n])
                ins.then_inc(ot_done, 1)
                if c == 0:
                    segments(l, 3)

            eng.wait_ge(init_done, 2)
            with eng.Fori(0, DEPTH) as l:
                ffn(l, 0, l * NORMS, lambda: sum_squares(l * NORMS))
                mix(l)
                to_x(l * U_LAYER + B_OUT, l * AB_LAYER + AB_OUT, KT,
                     lambda k: eng.wait_ge(oy_done, l * KT + (k + 1)), (8, 9, 10, 11, 0, 1, 2, 3))
                ffn(l, 1, l * NORMS + 2, lambda: sum_squares(l * NORMS + 2))
            sum_squares(DEPTH * NORMS)


_OUTS = {"y": (KT, P, T), "conv": (DEPTH, P, 16, 27), "lru": (DEPTH, P, 4, 9), "dp": (DEPTH, P, H, P), "ds": (DEPTH * 2, P, 2, SEQS, P)}


def _units(w, m_tiles):
    rows = w.shape[0]
    return w.reshape(rows // P, P, m_tiles, P).transpose(2, 1, 0, 3).reshape(m_tiles, P, rows)


def _per_tile(v):
    return np.moveaxis(v.reshape(v.shape[:-1] + (-1, P)), -1, 0).reshape(P, -1)


def _rows(v):
    return np.broadcast_to(v, (P, v.shape[0]))


def _layout(a):
    d_a = H * DK
    x = np.concatenate([a["meta_tokens"], a["x_prompt"][0], a["x_sample"].reshape(TS, D)], axis=0)
    n1, nm, n2 = a["norm_ffn1"], a["norm_mix"], a["norm_ffn2"]
    vec, wba, wri, chist, lru0, s0, wgu, wda, wdb, win, wout = ([] for _ in range(11))
    for l in range(DEPTH):
        cw = a["conv_qkv"][l].T
        vkq = np.concatenate([cw[2 * d_a:], cw[d_a:2 * d_a], cw[:d_a], a["conv_lru_w"][l].T], axis=0)
        taps = vkq.reshape(16, P, TAPS).transpose(1, 0, 2).reshape(P, 16 * TAPS)
        after = n1[l + 1] if l + 1 < DEPTH else a["norm_final"]
        vec.append(np.concatenate([_per_tile(nm[l]), _per_tile(n2[l]), _per_tile(after), taps]
                                  + [_per_tile(a[n][l]) for n in ("conv_lru_b", "b_rgate", "b_igate", "lru_lambda")]
                                  + [_rows(a["a_log"][l]), _rows(a["dt_bias"][l]), _per_tile(a["norm_delta_out"][l])], axis=1))
        w = a["w_in"][l]
        q, k, v, z, ba, xr, gate = np.split(w, [d_a, 2 * d_a, 3 * d_a, 4 * d_a, 4 * d_a + 2 * H, 4 * d_a + 2 * H + DR], axis=1)
        wba.append(ba.reshape(KT, P, 8).transpose(1, 0, 2).reshape(P, KT * 8))
        u = lambda m: _units(m, 4)
        win.append(np.concatenate([u(v), u(k), u(q), np.stack([u(xr), u(gate)], axis=1).reshape(8, P, D), u(z)], axis=0))
        ri = np.zeros((P, 4, 2, P), np.float32)
        for g, name in enumerate(("w_rgate", "w_igate")):
            for b in range(8):
                r = slice((b % 2) * 64, (b % 2 + 1) * 64)
                ri[r, b // 2, g, r] = a[name][l, b]
        wri.append(ri)
        hq, hk, hv = np.split(a["state_delta_conv"][l], 3, axis=2)
        h = np.concatenate([hv, hk, hq, a["state_lru_conv"][l]], axis=2)
        chist.append(h.reshape(SEQS, TAPS - 1, 16, P).transpose(3, 2, 0, 1))
        lru0.append(a["state_lru"][l].reshape(SEQS, 4, P).transpose(2, 1, 0))
        s0.append(a["state_delta"][l].reshape(SEQS, 2, 2, DK, P).transpose(1, 3, 2, 0, 4))
        for f in ("1", "2"):
            gu = np.stack([_units(a[f"w_ffn{f}_gate"][l], FT), _units(a[f"w_ffn{f}_up"][l], FT)], axis=1)
            wgu.append(gu.reshape(2 * FT, P, D))
            down = _units(a[f"w_ffn{f}_down"][l], KT)
            wda.append(down[:, :, :FA * P])
            wdb.append(down[:, :, FA * P:])
        w = a["w_out"][l]
        wout.append(_units(np.concatenate([w[d_a:], w[:d_a]], axis=0), KT))
    cat = lambda t: np.concatenate(t, axis=0)
    return {"xT": x.T.reshape(KT, P, T), "gain0": _per_tile(n1[0]), "mask": chunk_masks(), "vec": np.stack(vec),
            "wba": np.stack(wba), "wri": np.stack(wri), "chist": np.stack(chist), "lru0": np.stack(lru0), "s0": cat(s0),
            "wgu": cat(wgu), "wda": cat(wda), "wdb": cat(wdb), "win": cat(win), "wout": cat(wout)}


def _results(r):
    y = r["y"].reshape(D, T).T
    conv = r["conv"].transpose(0, 3, 2, 1).reshape(DEPTH, 27, 16 * P)
    v, k, q, xr = np.split(conv, 4, axis=2)
    qkv = np.concatenate([q, k, v], axis=2)
    lru = r["lru"].transpose(0, 3, 2, 1).reshape(DEPTH, 9, DR)
    dp = r["dp"].transpose(0, 2, 1, 3)[:, None]
    ds = r["ds"].reshape(DEPTH, 2, P, 2, SEQS, P).transpose(0, 4, 1, 3, 2, 5).reshape(DEPTH, SEQS, H, DK, P)
    rows = lambda t: (t[:, 0:3][:, None], t[:, 3:].reshape(DEPTH, SEQS, 3, t.shape[2]))
    (qkv_p, qkv_s), (xr_p, xr_s) = rows(qkv), rows(xr)
    out = (y[N_META:TP][None], y[TP:].reshape(SEQS, SLEN, D), dp, qkv_p, lru[:, 0:1], xr_p, ds, qkv_s, lru[:, 1:], xr_s)
    return tuple(np.ascontiguousarray(o) for o in out)


def kernel(**inputs):
    import concourse.bacc as _bacc
    from concourse.bass_utils import run_bass_kernel_spmd as _run

    arrays = {f"in_{n}": np.ascontiguousarray(v) for n, v in _layout({n: np.asarray(v) for n, v in inputs.items()}).items()}
    nc = _bacc.Bacc("TRN2", target_bir_lowering=False, num_devices=1)
    I = {n[3:]: nc.dram_tensor(n, v.shape, mybir.dt.from_np(v.dtype), kind="ExternalInput").ap() for n, v in arrays.items()}
    O = {n: nc.dram_tensor(f"out_{n}", s, F32, kind="ExternalOutput").ap() for n, s in _OUTS.items()}
    build(nc, I, O)
    r = _run(nc, [arrays], core_ids=[0])
    return _results({n: r.results[0][f"out_{n}"] for n in _OUTS})
```
